# Optimizing a Trainium2 kernel written in Bass

```python
import math
import jax
import jax.numpy as jnp
from jax import lax
import numpy as np
import jax, jax.numpy as jnp

D_MODEL = 2048
BATCH = 1
SEQ = 256
DEPTH = 1

MEM_LEN = 256
MIX_W = D_MODEL
LRU_W = MIX_W // 4
LRU_BLOCKS = 4
LRU_CONV = 4
LRU_C = 8.0
ML_W = 3 * MIX_W // 8
ML_HEADS = 4
ML_DH = ML_W // ML_HEADS
ML_QKV_BLOCK = 4
ML_CONV = 4
ML_CHUNK = 128
MO_W = MIX_W - LRU_W - ML_W
MO_HEADS = 6
MO_DH = MO_W // MO_HEADS
MOBA_BLOCK = 256
MOBA_TOPK = 3
MOBA_Q_CHUNK = 16
XA_HEADS = 4
XA_DH = 128
XA_W = XA_HEADS * XA_DH

RMS_EPS = 1e-6
LN_EPS = 1e-5
NEG_INF = -1e30

SPLIT_SIZES = (LRU_W, LRU_W, ML_W, ML_W, ML_W, ML_HEADS, ML_HEADS, MO_W, MO_W, MO_W, MO_W)
IN_COLS = sum(SPLIT_SIZES)
SPLIT_POINTS = tuple(int(v) for v in np.cumsum(SPLIT_SIZES)[:-1])


def rms_norm(x, g):
    x32 = x.astype(jnp.float32)
    y = x32 * lax.rsqrt(jnp.mean(x32 * x32, axis=-1, keepdims=True) + RMS_EPS)
    return (y * g.astype(jnp.float32)).astype(x.dtype)

def causal_conv(x, w, b):
    K = w.shape[0]
    T = x.shape[1]
    xp = jnp.pad(x, ((0, 0), (K - 1, 0), (0, 0)))
    return sum(xp[:, j:j + T] * w[j] for j in range(K)) + b

def block_diag(x, w):
    G, bi, bo = w.shape
    xs = x.reshape(x.shape[:-1] + (G, bi))
    return jnp.einsum('...gi,gio->...go', xs, w).reshape(x.shape[:-1] + (G * bo,))

def alibi_slopes(n):
    def pow2(m):
        start = 2.0 ** (-8.0 / m)
        return [start ** (i + 1) for i in range(m)]
    if math.log2(n).is_integer():
        s = pow2(n)
    else:
        c = 2 ** int(math.floor(math.log2(n)))
        s = pow2(c) + pow2(2 * c)[0::2][:n - c]
    return jnp.array(s, dtype=jnp.float32)

def rg_lru_branch(xb, zb, conv_w, conv_b, wa, ba, wx, bx, lam):
    xc = causal_conv(xb, conv_w, conv_b).astype(jnp.float32)
    r = jax.nn.sigmoid(block_diag(xc, wa) + ba)
    i = jax.nn.sigmoid(block_diag(xc, wx) + bx)
    log_a = -LRU_C * r * jax.nn.softplus(-lam.astype(jnp.float32))
    a = jnp.exp(log_a)
    u = jnp.sqrt(-jnp.expm1(2.0 * log_a)) * (i * xc)

    def combine(left, right):
        a1, b1 = left
        a2, b2 = right
        return a1 * a2, a2 * b1 + b2

    _, h = lax.associative_scan(combine, (a, u), axis=1)
    return (h * jax.nn.silu(zb.astype(jnp.float32))).astype(xb.dtype)

def mlstm_chunkwise(q, k, v, ig, lf):
    B, H, T, dh = q.shape
    L = ML_CHUNK
    nc = T // L
    q, k, v = (t.reshape(B, H, nc, L, dh) for t in (q, k, v))
    ig = ig.reshape(B, H, nc, L)
    lf = lf.reshape(B, H, nc, L)
    b = jnp.cumsum(lf, axis=-1)
    g = b[..., -1]
    a = g[..., None] - b + ig
    m_loc = jnp.max(a, axis=-1)
    w = jnp.exp(a - m_loc[..., None])
    c_loc = jnp.einsum('bhcl,bhcld,bhcle->bhcde', w, k, v)
    n_loc = jnp.einsum('bhcl,bhcld->bhcd', w, k)

    def step(carry, inp):
        c_st, n_st, m_st = carry
        c_l, n_l, m_l, g_c = inp
        m_new = jnp.maximum(g_c + m_st, m_l)
        s_old = jnp.exp(g_c + m_st - m_new)
        s_new = jnp.exp(m_l - m_new)
        c_new = s_old[..., None, None] * c_st + s_new[..., None, None] * c_l
        n_new = s_old[..., None] * n_st + s_new[..., None] * n_l
        return (c_new, n_new, m_new), (c_st, n_st, m_st)

    init = (jnp.zeros((B, H, dh, dh), jnp.float32), jnp.zeros((B, H, dh), jnp.float32),
            jnp.zeros((B, H), jnp.float32))
    xs = tuple(jnp.moveaxis(t, 2, 0) for t in (c_loc, n_loc, m_loc, g))
    _, (c_prev, n_prev, m_prev) = lax.scan(step, init, xs)
    c_prev = jnp.moveaxis(c_prev, 0, 2)
    n_prev = jnp.moveaxis(n_prev, 0, 2)
    m_prev = jnp.moveaxis(m_prev, 0, 2)
    causal = jnp.tril(jnp.ones((L, L), dtype=bool))
    d = jnp.where(causal, b[..., :, None] - b[..., None, :] + ig[..., None, :], -jnp.inf)
    inter = b + m_prev[..., None]
    m = jnp.maximum(inter, jnp.max(d, axis=-1))
    s = jnp.einsum('bhcjd,bhcsd->bhcjs', q, k) * jnp.exp(d - m[..., None])
    s_int = jnp.exp(inter - m)
    num = (jnp.einsum('bhcjs,bhcsd->bhcjd', s, v)
           + s_int[..., None] * jnp.einsum('bhcjd,bhcde->bhcje', q, c_prev))
    den = jnp.sum(s, axis=-1) + s_int * jnp.einsum('bhcjd,bhcd->bhcj', q, n_prev)
    h = num / jnp.maximum(jnp.abs(den), jnp.exp(-m))[..., None]
    return h.reshape(B, H, T, dh)

def mlstm_branch(u, o, z, ig_pre, fg_pre, conv_w, conv_b, wq, wk, wv, bi, bf, norm_g):
    B, T, _ = u.shape
    uc = jax.nn.silu(causal_conv(u, conv_w, conv_b))
    q = block_diag(uc, wq)
    k = block_diag(uc, wk) * (ML_DH ** -0.5)
    v = block_diag(u, wv)

    def heads(t):
        return t.astype(jnp.float32).reshape(B, T, ML_HEADS, ML_DH).transpose(0, 2, 1, 3)

    ig = (ig_pre.astype(jnp.float32) + bi).transpose(0, 2, 1)
    lf = jax.nn.log_sigmoid(fg_pre.astype(jnp.float32) + bf).transpose(0, 2, 1)
    h = mlstm_chunkwise(heads(q), heads(k), heads(v), ig, lf).transpose(0, 2, 1, 3)
    h = jax.nn.sigmoid(o.astype(jnp.float32)).reshape(B, T, ML_HEADS, ML_DH) * h
    mu = jnp.mean(h, axis=-1, keepdims=True)
    var = jnp.mean(jnp.square(h - mu), axis=-1, keepdims=True)
    hn = (h - mu) * lax.rsqrt(var + LN_EPS) * norm_g.astype(jnp.float32).reshape(ML_HEADS, ML_DH)
    return (hn.reshape(B, T, ML_W) * jax.nn.silu(z.astype(jnp.float32))).astype(u.dtype)

def moba_attention(q, k, v):
    B, H, T, dh = q.shape
    nb = -(-T // MOBA_BLOCK)
    tp = nb * MOBA_BLOCK
    pad = ((0, 0), (0, 0), (0, tp - T), (0, 0))
    q, k, v = (jnp.pad(t, pad) for t in (q, k, v))
    kb = k.reshape(B, H, nb, MOBA_BLOCK, dh)
    vb = v.reshape(B, H, nb, MOBA_BLOCK, dh)
    kmean = jnp.mean(kb.astype(jnp.float32), axis=3)
    n_sel = min(MOBA_TOPK, nb - 1)
    slopes = alibi_slopes(H)
    scale = dh ** -0.5
    nq = tp // MOBA_Q_CHUNK
    qc = jnp.moveaxis(q.reshape(B, H, nq, MOBA_Q_CHUNK, dh), 2, 0)
    bidx = jnp.arange(B)[:, None, None, None]
    hidx = jnp.arange(H)[None, :, None, None]
    s_local = jnp.arange(MOBA_BLOCK)

    def one_chunk(args):
        qch, ci = args
        qch = qch.astype(jnp.float32)
        t = ci * MOBA_Q_CHUNK + jnp.arange(MOBA_Q_CHUNK)
        bq = (ci * MOBA_Q_CHUNK) // MOBA_BLOCK
        k_own = lax.dynamic_index_in_dim(kb, bq, axis=2, keepdims=False).astype(jnp.float32)
        v_own = lax.dynamic_index_in_dim(vb, bq, axis=2, keepdims=False).astype(jnp.float32)
        dist_own = (t[:, None] - (bq * MOBA_BLOCK + s_local)[None, :]).astype(jnp.float32)
        l_own = jnp.einsum('bhqd,bhsd->bhqs', qch, k_own) * scale - slopes[:, None, None] * dist_own
        l_own = jnp.where(dist_own >= 0, l_own, NEG_INF)
        if n_sel == 0:
            p_own = jax.nn.softmax(l_own, axis=-1)
            return jnp.einsum('bhqs,bhsd->bhqd', p_own, v_own)
        gate = jnp.einsum('bhqd,bhnd->bhqn', qch, kmean)
        gate = jnp.where(jnp.arange(nb) < bq, gate, -jnp.inf)
        _, idx = lax.top_k(gate, n_sel)
        k_sel = kb[bidx, hidx, idx].astype(jnp.float32)
        v_sel = vb[bidx, hidx, idx].astype(jnp.float32)
        dist_sel = (t[:, None, None] - (idx[..., None] * MOBA_BLOCK + s_local)).astype(jnp.float32)
        l_sel = (jnp.einsum('bhqd,bhqnsd->bhqns', qch, k_sel) * scale
                 - slopes[:, None, None, None] * dist_sel)
        l_sel = jnp.where((jnp.arange(n_sel) < bq)[:, None], l_sel, NEG_INF)
        n_past = n_sel * MOBA_BLOCK
        logits = jnp.concatenate(
            [l_sel.reshape(B, H, MOBA_Q_CHUNK, n_past), l_own], axis=-1)
        p = jax.nn.softmax(logits, axis=-1)
        p_sel = p[..., :n_past].reshape(B, H, MOBA_Q_CHUNK, n_sel, MOBA_BLOCK)
        p_own = p[..., n_past:]
        return (jnp.einsum('bhqns,bhqnsd->bhqd', p_sel, v_sel)
                + jnp.einsum('bhqs,bhsd->bhqd', p_own, v_own))

    out = lax.map(one_chunk, (qc, jnp.arange(nq)))
    out = jnp.moveaxis(out, 0, 2).reshape(B, H, tp, dh)
    return out[:, :, :T]

def moba_branch(qb, kb, vb, zb):
    B, T, _ = qb.shape

    def heads(t):
        return t.reshape(B, T, MO_HEADS, MO_DH).transpose(0, 2, 1, 3)

    o = moba_attention(heads(qb), heads(kb), heads(vb)).transpose(0, 2, 1, 3).reshape(B, T, MO_W)
    return (o * jax.nn.silu(zb.astype(jnp.float32))).astype(qb.dtype)

def memory_cross_attention(h, mem_n, wq, wkv, wo):
    B, T, _ = h.shape
    M = mem_n.shape[1]
    q = (h @ wq).reshape(B, T, XA_HEADS, XA_DH)
    k, v = jnp.split(mem_n @ wkv, 2, axis=-1)
    k = k.reshape(B, M, XA_HEADS, XA_DH)
    v = v.reshape(B, M, XA_HEADS, XA_DH)
    s = jnp.einsum('bthd,bmhd->bhtm', q, k).astype(jnp.float32) * (XA_DH ** -0.5)
    p = jax.nn.softmax(s, axis=-1).astype(v.dtype)
    o = jnp.einsum('bhtm,bmhd->bthd', p, v).reshape(B, T, XA_W)
    return o @ wo

def first_inputs(seed: int = 0) -> dict:
    key = jax.random.key(seed)
    ks = jax.random.split(key, 26)

    def nrm(k, shape, scale):
        return scale * jax.random.normal(k, shape, jnp.float32)

    def gain(k, shape):
        return 1.0 + 0.02 * jax.random.normal(k, shape, jnp.float32)

    u = jax.random.uniform(ks[10], (DEPTH, LRU_W), jnp.float32, 0.9, 0.999)
    a = u ** (1.0 / LRU_C)
    lam = jnp.log(a) - jnp.log1p(-a)
    bl = LRU_W // LRU_BLOCKS
    nqkv = ML_W // ML_QKV_BLOCK
    return {
        "x": nrm(ks[0], (BATCH, SEQ, D_MODEL), 1.0),
        "mem": nrm(ks[1], (BATCH, MEM_LEN, D_MODEL), 1.0),
        "mix_norm_g": gain(ks[2], (DEPTH, D_MODEL)),
        "w_in": nrm(ks[3], (DEPTH, D_MODEL, IN_COLS), D_MODEL ** -0.5),
        "lru_conv_w": nrm(ks[4], (DEPTH, LRU_CONV, LRU_W), LRU_CONV ** -0.5),
        "lru_conv_b": nrm(ks[5], (DEPTH, LRU_W), 0.02),
        "lru_wa": nrm(ks[6], (DEPTH, LRU_BLOCKS, bl, bl), bl ** -0.5),
        "lru_ba": nrm(ks[7], (DEPTH, LRU_W), 0.02),
        "lru_wx": nrm(ks[8], (DEPTH, LRU_BLOCKS, bl, bl), bl ** -0.5),
        "lru_bx": nrm(ks[9], (DEPTH, LRU_W), 0.02),
        "lru_lambda": lam,
        "ml_conv_w": nrm(ks[11], (DEPTH, ML_CONV, ML_W), ML_CONV ** -0.5),
        "ml_conv_b": nrm(ks[12], (DEPTH, ML_W), 0.02),
        "ml_wq": nrm(ks[13], (DEPTH, nqkv, ML_QKV_BLOCK, ML_QKV_BLOCK), ML_QKV_BLOCK ** -0.5),
        "ml_wk": nrm(ks[14], (DEPTH, nqkv, ML_QKV_BLOCK, ML_QKV_BLOCK), ML_QKV_BLOCK ** -0.5),
        "ml_wv": nrm(ks[15], (DEPTH, nqkv, ML_QKV_BLOCK, ML_QKV_BLOCK), ML_QKV_BLOCK ** -0.5),
        "ml_bi": nrm(ks[16], (DEPTH, ML_HEADS), 0.1),
        "ml_bf": jnp.linspace(3.0, 6.0, ML_HEADS, dtype=jnp.float32)[None, :] + nrm(ks[17], (DEPTH, ML_HEADS), 0.02),
        "ml_norm_g": gain(ks[18], (DEPTH, ML_W)),
        "w_out": nrm(ks[19], (DEPTH, MIX_W, D_MODEL), MIX_W ** -0.5),
        "xa_norm_g": gain(ks[20], (DEPTH, D_MODEL)),
        "mem_norm_g": gain(ks[21], (DEPTH, D_MODEL)),
        "xa_wq": nrm(ks[22], (DEPTH, D_MODEL, XA_W), D_MODEL ** -0.5),
        "xa_wkv": nrm(ks[23], (DEPTH, D_MODEL, 2 * XA_W), D_MODEL ** -0.5),
        "xa_wo": nrm(ks[24], (DEPTH, XA_W, D_MODEL), XA_W ** -0.5),
        "final_norm_g": gain(ks[25], (D_MODEL,)),
    }

def first_block(x, mem, mix_norm_g, w_in, lru_conv_w, lru_conv_b, lru_wa, lru_ba, lru_wx, lru_bx,
              lru_lambda, ml_conv_w, ml_conv_b, ml_wq, ml_wk, ml_wv, ml_bi, ml_bf, ml_norm_g,
              w_out, xa_norm_g, mem_norm_g, xa_wq, xa_wkv, xa_wo, final_norm_g):
    for l in range(DEPTH):
        h = rms_norm(x, mix_norm_g[l])
        p = h @ w_in[l]
        (lru_x, lru_z, ml_u, ml_o, ml_z, ml_i, ml_f,
         mo_q, mo_k, mo_v, mo_z) = jnp.split(p, SPLIT_POINTS, axis=-1)
        y_lru = rg_lru_branch(lru_x, lru_z, lru_conv_w[l], lru_conv_b[l], lru_wa[l], lru_ba[l],
                              lru_wx[l], lru_bx[l], lru_lambda[l])
        y_ml = mlstm_branch(ml_u, ml_o, ml_z, ml_i, ml_f, ml_conv_w[l], ml_conv_b[l], ml_wq[l],
                            ml_wk[l], ml_wv[l], ml_bi[l], ml_bf[l], ml_norm_g[l])
        y_mo = moba_branch(mo_q, mo_k, mo_v, mo_z)
        y = jnp.concatenate([y_lru, y_ml, y_mo], axis=-1)
        x = x + y @ w_out[l]
        hx = rms_norm(x, xa_norm_g[l])
        hm = rms_norm(mem, mem_norm_g[l])
        x = x + memory_cross_attention(hx, hm, xa_wq[l], xa_wkv[l], xa_wo[l])
    return rms_norm(x, final_norm_g)


DEPTH_2 = 2

GRID_W = 64
CTX_LEN = 256
N_MIXERS = 2
N_POOL_LAYERS = (DEPTH_2 + N_MIXERS - 1) // N_MIXERS
N_MLA_LAYERS = DEPTH_2 // N_MIXERS
POOL_WIDTH = D_MODEL
POOL_GROUPS = 4
POOL_GROUP_DIM = POOL_WIDTH // POOL_GROUPS
POOL_WINDOWS = (2, 4, 8, 16)
MLA_HEADS = 16
Q_LORA_RANK = 512
KV_LORA_RANK = 512
QK_NOPE_DIM = 128
QK_ROPE_DIM = 64
V_HEAD_DIM = 128
MLA_WIDTH = MLA_HEADS * V_HEAD_DIM
MLA_IN_WIDTH = Q_LORA_RANK + KV_LORA_RANK + QK_ROPE_DIM + MLA_WIDTH
MLA_SCALE = (QK_NOPE_DIM + QK_ROPE_DIM) ** -0.5
ROPE_BASE = 10000.0
Q_BLOCK = 128
NORM_EPS = 1e-6


def rms_norm_2(x, g):
    xf = x.astype(jnp.float32)
    y = xf * lax.rsqrt(jnp.mean(xf * xf, axis=-1, keepdims=True) + NORM_EPS)
    return (y * g.astype(jnp.float32)).astype(x.dtype)

def centred_multiscale_pool(u):
    L = u.shape[1]
    uf = u.astype(jnp.float32)
    cs = jnp.concatenate([jnp.zeros_like(uf[:, :1]), jnp.cumsum(uf, axis=1)], axis=1)
    win = jnp.array(POOL_WINDOWS, dtype=jnp.int32)
    left = win // 2
    right = win - 1 - left
    t = jnp.arange(L, dtype=jnp.int32)[:, None]
    hi = jnp.minimum(t + right + 1, L)
    lo = jnp.maximum(t - left, 0)
    g = jnp.arange(POOL_GROUPS, dtype=jnp.int32)[None, :]
    s = cs[:, hi, g] - cs[:, lo, g]
    mean = s / (hi - lo).astype(jnp.float32)[None, :, :, None]
    return (mean - uf).astype(u.dtype)

def pool_branch(h, w_in, w_grp, b_grp, scale, w_out):
    B, L, _ = h.shape
    u, gate = jnp.split(h @ w_in, 2, axis=-1)
    p = centred_multiscale_pool(u.reshape(B, L, POOL_GROUPS, POOL_GROUP_DIM))
    p = jnp.einsum('blgc,gcd->blgd', p, w_grp) + b_grp
    y = p.reshape(B, L, POOL_WIDTH) * scale
    return (y * jax.nn.silu(gate)) @ w_out

def axial_rope_tables(L):
    rows = L // GRID_W
    row = jnp.repeat(jnp.arange(rows, dtype=jnp.float32), GRID_W)
    col = jnp.tile(jnp.arange(GRID_W, dtype=jnp.float32), rows)
    n = QK_ROPE_DIM // 4
    freqs = ROPE_BASE ** (-jnp.arange(n, dtype=jnp.float32) / n)
    ang = jnp.stack([row[:, None] * freqs, col[:, None] * freqs], axis=1)
    return jnp.cos(ang), jnp.sin(ang)

def apply_axial_rope(x, cos, sin):
    xs = x.reshape(x.shape[:-1] + (2, 2, QK_ROPE_DIM // 4))
    x1, x2 = xs[..., 0, :], xs[..., 1, :]
    cos = cos.astype(x.dtype)
    sin = sin.astype(x.dtype)
    out = jnp.stack([x1 * cos - x2 * sin, x1 * sin + x2 * cos], axis=-2)
    return out.reshape(x.shape)

def mla_project(h, w_in, q_norm, kv_norm, w_uq, w_ukv, rope):
    B, L, _ = h.shape
    proj = h @ w_in
    c_q, c_kv, k_r, gate = jnp.split(
        proj, [Q_LORA_RANK, Q_LORA_RANK + KV_LORA_RANK, Q_LORA_RANK + KV_LORA_RANK + QK_ROPE_DIM], axis=-1)
    q = (rms_norm_2(c_q, q_norm) @ w_uq).reshape(B, L, MLA_HEADS, QK_NOPE_DIM + QK_ROPE_DIM)
    q_nope, q_rope = q[..., :QK_NOPE_DIM], q[..., QK_NOPE_DIM:]
    kv = (rms_norm_2(c_kv, kv_norm) @ w_ukv).reshape(B, L, MLA_HEADS, QK_NOPE_DIM + V_HEAD_DIM)
    k_nope, v = kv[..., :QK_NOPE_DIM], kv[..., QK_NOPE_DIM:]
    if rope is not None:
        cos, sin = rope
        q_rope = apply_axial_rope(q_rope, cos[:, None], sin[:, None])
        k_r = apply_axial_rope(k_r, cos, sin)
    return q_nope, q_rope, k_nope, k_r, v, gate

def mla_attend(q_nope, q_rope, k_nope, k_rope, v):
    s = (jnp.einsum('bqhd,bkhd->bhqk', q_nope, k_nope)
         + jnp.einsum('bqhr,bkr->bhqk', q_rope, k_rope)).astype(jnp.float32) * MLA_SCALE
    p = jax.nn.softmax(s, axis=-1).astype(v.dtype)
    return jnp.einsum('bhqk,bkhd->bqhd', p, v)

def blocked_mla_attend(q_nope, q_rope, k_nope, k_rope, v):
    B, L, H, _ = q_nope.shape
    nb = L // Q_BLOCK
    qn = q_nope.reshape(B, nb, Q_BLOCK, H, QK_NOPE_DIM).transpose(1, 0, 2, 3, 4)
    qr = q_rope.reshape(B, nb, Q_BLOCK, H, QK_ROPE_DIM).transpose(1, 0, 2, 3, 4)
    out = lax.map(lambda qb: mla_attend(qb[0], qb[1], k_nope, k_rope, v), (qn, qr))
    return out.transpose(1, 0, 2, 3, 4).reshape(B, L, H * V_HEAD_DIM)

def mla_branch(h_lat, h_ctx, w_in, q_norm, kv_norm, w_uq, w_ukv, w_out, need_ctx_out):
    L = h_lat.shape[1]
    rope = axial_rope_tables(L)
    qn_l, qr_l, kn_l, kr_l, v_l, g_l = mla_project(h_lat, w_in, q_norm, kv_norm, w_uq, w_ukv, rope)
    qn_c, qr_c, kn_c, kr_c, v_c, g_c = mla_project(h_ctx, w_in, q_norm, kv_norm, w_uq, w_ukv, None)
    kn = jnp.concatenate([kn_c, kn_l], axis=1)
    kr = jnp.concatenate([kr_c, kr_l], axis=1)
    v = jnp.concatenate([v_c, v_l], axis=1)
    o_lat = blocked_mla_attend(qn_l, qr_l, kn, kr, v)
    y_lat = (o_lat * jax.nn.silu(g_l)) @ w_out
    if not need_ctx_out:
        return y_lat, None
    B, Lc = h_ctx.shape[:2]
    o_ctx = mla_attend(qn_c, qr_c, kn_c, kr_c, v_c).reshape(B, Lc, MLA_WIDTH)
    y_ctx = (o_ctx * jax.nn.silu(g_c)) @ w_out
    return y_lat, y_ctx

def second_inputs(seed: int = 0) -> dict:
    key = jax.random.key(seed)
    ks = jax.random.split(key, 20)
    nrm = jax.random.normal
    f32 = jnp.float32
    return {
        "x": nrm(ks[0], (BATCH, SEQ, D_MODEL), f32),
        "c": nrm(ks[1], (BATCH, D_MODEL), f32),
        "ctx": nrm(ks[2], (BATCH, CTX_LEN, D_MODEL), f32),
        "c_ctx": nrm(ks[3], (D_MODEL,), f32),
        "ada_w": nrm(ks[4], (DEPTH_2, D_MODEL, 3 * D_MODEL), f32) * D_MODEL ** -0.5,
        "ada_b": nrm(ks[5], (DEPTH_2, 3 * D_MODEL), f32) * 0.01,
        "pre_norm": 1.0 + 0.1 * nrm(ks[6], (DEPTH_2, D_MODEL), f32),
        "post_norm": 1.0 + 0.1 * nrm(ks[7], (DEPTH_2, D_MODEL), f32),
        "pool_w_in": nrm(ks[8], (N_POOL_LAYERS, D_MODEL, 2 * POOL_WIDTH), f32) * D_MODEL ** -0.5,
        "pool_w_grp": nrm(ks[9], (N_POOL_LAYERS, POOL_GROUPS, POOL_GROUP_DIM, POOL_GROUP_DIM), f32) * POOL_GROUP_DIM ** -0.5,
        "pool_b_grp": nrm(ks[10], (N_POOL_LAYERS, POOL_GROUPS, POOL_GROUP_DIM), f32) * 0.01,
        "pool_scale": 1.0 + 0.1 * nrm(ks[11], (N_POOL_LAYERS, POOL_WIDTH), f32),
        "pool_w_out": nrm(ks[12], (N_POOL_LAYERS, POOL_WIDTH, D_MODEL), f32) * POOL_WIDTH ** -0.5,
        "mla_w_in": nrm(ks[13], (N_MLA_LAYERS, D_MODEL, MLA_IN_WIDTH), f32) * D_MODEL ** -0.5,
        "mla_q_norm": 1.0 + 0.1 * nrm(ks[14], (N_MLA_LAYERS, Q_LORA_RANK), f32),
        "mla_kv_norm": 1.0 + 0.1 * nrm(ks[15], (N_MLA_LAYERS, KV_LORA_RANK), f32),
        "mla_w_uq": nrm(ks[16], (N_MLA_LAYERS, Q_LORA_RANK, MLA_HEADS * (QK_NOPE_DIM + QK_ROPE_DIM)), f32) * Q_LORA_RANK ** -0.5,
        "mla_w_ukv": nrm(ks[17], (N_MLA_LAYERS, KV_LORA_RANK, MLA_HEADS * (QK_NOPE_DIM + V_HEAD_DIM)), f32) * KV_LORA_RANK ** -0.5,
        "mla_w_out": nrm(ks[18], (N_MLA_LAYERS, MLA_WIDTH, D_MODEL), f32) * MLA_WIDTH ** -0.5,
    }

def second_block(x, c, ctx, c_ctx, ada_w, ada_b, pre_norm, post_norm,
              pool_w_in, pool_w_grp, pool_b_grp, pool_scale, pool_w_out,
              mla_w_in, mla_q_norm, mla_kv_norm, mla_w_uq, mla_w_ukv, mla_w_out):
    for i in range(DEPTH_2):
        last = i == DEPTH_2 - 1
        j = i // N_MIXERS
        is_pool = (i % N_MIXERS) == 0
        need_ctx_out = not last
        need_ctx_in = need_ctx_out or not is_pool
        shift, scale, gate = jnp.split(jax.nn.silu(c) @ ada_w[i] + ada_b[i], 3, axis=-1)
        h_lat = rms_norm_2(x, pre_norm[i]) * (1 + scale[:, None]) + shift[:, None]
        h_ctx = None
        gate_c = None
        if need_ctx_in:
            shift_c, scale_c, gate_c = jnp.split(jax.nn.silu(c_ctx) @ ada_w[i] + ada_b[i], 3, axis=-1)
            h_ctx = rms_norm_2(ctx, pre_norm[i]) * (1 + scale_c) + shift_c
        if is_pool:
            y_lat = pool_branch(h_lat, pool_w_in[j], pool_w_grp[j], pool_b_grp[j], pool_scale[j], pool_w_out[j])
            y_ctx = (pool_branch(h_ctx, pool_w_in[j], pool_w_grp[j], pool_b_grp[j], pool_scale[j], pool_w_out[j])
                     if need_ctx_out else None)
        else:
            y_lat, y_ctx = mla_branch(h_lat, h_ctx, mla_w_in[j], mla_q_norm[j], mla_kv_norm[j],
                                      mla_w_uq[j], mla_w_ukv[j], mla_w_out[j], need_ctx_out)
        x = x + gate[:, None] * rms_norm_2(y_lat, post_norm[i])
        if need_ctx_out:
            ctx = ctx + gate_c * rms_norm_2(y_ctx, post_norm[i])
    return x


def setup_inputs(seed=0):
    out = dict(first_inputs(seed))
    for name, value in second_inputs(seed + 1).items():
        if name != "x":
            out[name + "_2"] = value
    return out


def reference(
    x, mem, mix_norm_g, w_in, lru_conv_w, lru_conv_b, lru_wa, lru_ba, lru_wx, lru_bx,
    lru_lambda, ml_conv_w, ml_conv_b, ml_wq, ml_wk, ml_wv, ml_bi, ml_bf, ml_norm_g, w_out,
    xa_norm_g, mem_norm_g, xa_wq, xa_wkv, xa_wo, final_norm_g, c_2, ctx_2, c_ctx_2, ada_w_2,
    ada_b_2, pre_norm_2, post_norm_2, pool_w_in_2, pool_w_grp_2, pool_b_grp_2, pool_scale_2,
    pool_w_out_2, mla_w_in_2, mla_q_norm_2, mla_kv_norm_2, mla_w_uq_2, mla_w_ukv_2, mla_w_out_2,
):
    x = first_block(
        x, mem, mix_norm_g, w_in, lru_conv_w, lru_conv_b, lru_wa, lru_ba, lru_wx, lru_bx,
        lru_lambda, ml_conv_w, ml_conv_b, ml_wq, ml_wk, ml_wv, ml_bi, ml_bf, ml_norm_g, w_out,
        xa_norm_g, mem_norm_g, xa_wq, xa_wkv, xa_wo, final_norm_g,
    )
    return second_block(
        x, c_2, ctx_2, c_ctx_2, ada_w_2, ada_b_2, pre_norm_2, post_norm_2, pool_w_in_2,
        pool_w_grp_2, pool_b_grp_2, pool_scale_2, pool_w_out_2, mla_w_in_2, mla_q_norm_2,
        mla_kv_norm_2, mla_w_uq_2, mla_w_ukv_2, mla_w_out_2,
    )


_drawn_inputs = setup_inputs


def setup_inputs(seed=0):
    import zlib

    import numpy as np

    out = dict(_drawn_inputs(seed))
    spreads = {}
    factors = {'mix_norm_g': 2.87,
     'lru_ba': 8.0,
     'lru_bx': 8.0,
     'ml_conv_b': 5.031,
     'ml_bi': 64.0,
     'ml_norm_g': 7.864,
     'xa_norm_g': 8.0,
     'mem_norm_g': 8.0,
     'ada_b_2': 3.274,
     'pool_b_grp_2': 8.0,
     'mla_q_norm_2': 3.429}
    for name, (base, spread) in spreads.items():
        noise = np.random.default_rng([zlib.crc32(name.encode()), seed]).standard_normal(out[name].shape)
        drawn = base * np.exp(spread * noise) if base else spread * noise
        out[name] = jnp.asarray(drawn.astype(out[name].dtype))
    for name, factor in factors.items():
        out[name] = (out[name] * factor).astype(out[name].dtype)
    return out
```

```python
from contextlib import ExitStack

import numpy as np
import concourse.bass as bass
from concourse import mybir

F32 = mybir.dt.float32
F32R = mybir.dt.float32r
ACT = mybir.ActivationFunctionType
ALU = mybir.AluOpType
AX = mybir.AxisListType

P = 128
T = 256
D = 2048
KD = D // P
GW = 512
KC = 4
RMS_EPS = 1e-6
LN_EPS = 1e-5
NEG = -1e30
DEBUG_STOP = None


class Product:

    def __init__(self, name, w, chunks, groups, tiles, seqs, kind, k_groups=1, stride=GW, width=None, pack=None,
                 half=0, src="xs", dest=None, col0=0):
        self.name, self.w = name, w
        self.chunks = chunks
        self.groups = groups
        self.tiles = tiles
        self.seqs = seqs
        self.kind = kind
        self.stride = stride
        self.width = width or tiles * P
        self.pack = pack
        self.half = half
        self.src = src
        self.dest = dest
        self.col0 = col0


def plan(steps):
    chunk = tile = 0
    dve_free = act_free = 0
    bank_last = [None] * 4
    for p in steps:
        p.chunk0, p.tile0 = chunk, tile
        p.first_bank_wait = list(bank_last)
        p.free0 = act_free if p.kind == "both" else dve_free
        chunk += p.chunks * p.groups
        tile += (p.tiles - 1) * p.groups
        if p.kind == "both":
            act_free += p.tiles * p.groups
            end, which = act_free, "act"
        else:
            dve_free += p.tiles * p.groups
            end, which = dve_free, "dve"
        for n in range(p.tiles):
            bank_last[n] = (which, end - p.tiles + n + 1)
    return chunk


def vectors(a):
    v = lambda ap: ap.rearrange("(k p) -> k p", p=P)
    m = lambda ap: ap.rearrange("j (k p) -> (j k) p", p=P)
    return [
        ("mem_g", v(a["mem_norm_g"][0]), 16), ("mix_g", v(a["mix_norm_g"][0]), 16),
        ("c", v(a["c_2"][0]), 16), ("c_ctx", v(a["c_ctx_2"]), 16),
        ("lru_conv_w", m(a["lru_conv_w"][0]), 16), ("lru_conv_b", v(a["lru_conv_b"][0]), 4),
        ("lru_ba", v(a["lru_ba"][0]), 4), ("lru_bx", v(a["lru_bx"][0]), 4), ("lru_lambda", v(a["lru_lambda"][0]), 4),
        ("ml_conv_w", m(a["ml_conv_w"][0]), 24), ("ml_conv_b", v(a["ml_conv_b"][0]), 6),
        ("ml_g", v(a["ml_norm_g"][0]), 6), ("xa_g", v(a["xa_norm_g"][0]), 16), ("final_g", v(a["final_norm_g"]), 16),
        ("ada_b0", v(a["ada_b_2"][0]), 48), ("ada_b1", v(a["ada_b_2"][1]), 48),
        ("pre0", v(a["pre_norm_2"][0]), 16), ("pre1", v(a["pre_norm_2"][1]), 16),
        ("post0", v(a["post_norm_2"][0]), 16), ("post1", v(a["post_norm_2"][1]), 16),
        ("pool_b", v(a["pool_b_grp_2"].rearrange("l g c -> l (g c)")[0]), 16),
        ("pool_s", v(a["pool_scale_2"][0]), 16),
        ("q_g", v(a["mla_q_norm_2"][0]), 4), ("kv_g", v(a["mla_kv_norm_2"][0]), 4),
    ]


LX, LZ, U, O, Z, G = 40, 44, 48, 54, 60, 66
XAK, XAV = 32, 36
MQ, MK, MV, MZ = 40, 46, 52, 58
CT0 = 16
YT0 = 32
UC, QT, KT = 16, 22, 67
VT, KTOK, EX, SOT = 40, 73, 28, 48
SQ0, HF0 = 64, 72
NB = 78


class Steps:

    def __init__(self, sem, order):
        self.sem, self.order, self.done = sem, {key: n + 1 for n, key in enumerate(order)}, 0
        self.chain = None

    def inc(self, ins, *key):
        self.done += 1
        assert self.order[key] == self.done, (key, self.order[key], self.done)
        ins.then_inc(self.sem, 1)
        if self.chain:
            self.chain.wait_ge(self.sem, self.done)

    def wait(self, eng, *key):
        eng.wait_ge(self.sem, self.order[key])


def build(nc, a, out):
    w_in, w_out = a["w_in"][0], a["w_out"][0]
    wq, wkv, wo = a["xa_wq"][0], a["xa_wkv"][0], a["xa_wo"][0]
    pw_in, pw_out = a["pool_w_in_2"][0], a["pool_w_out_2"][0]
    mw_in, mw_out, mw_uq, mw_ukv = a["mla_w_in_2"][0], a["mla_w_out_2"][0], a["mla_w_uq_2"][0], a["mla_w_ukv_2"][0]

    kv = Product("kv", wkv, 4, 2, 4, 1, "copy1", half=1, dest=XAK)
    win_a = Product("win_a", w_in, 4, 6, 4, 1, "copy1", dest=LX)
    win_b = Product("win_b", w_in, 4, 1, 3, 1, "copy1", dest=LX + 24, col0=6 * GW)
    win_c = Product("win_c", w_in, 4, 6, 4, 1, "copy1", dest=MQ, col0=3336)
    mixo = Product("mixo", w_out, 4, 4, 4, 1, "add1", half=1, dest=0)
    xq = Product("xq", wq, 4, 1, 4, 1, "copy1", dest=40)
    xo = Product("xo", wo, 1, 4, 4, 1, "add1", half=1, dest=0)
    pu = [Product(f"pu{g}", pw_in, 4, 1, 4, 2, "copy2", dest=("pool_u", g), col0=g * GW) for g in range(4)]
    pg = [Product(f"pg{g}", a["pool_w_grp_2"][0][g], 1, 1, 4, 2, "grp", src="ps", dest=("y", 4 * g)) for g in range(4)]
    pgate = Product("pgate", pw_in, 4, 4, 4, 2, "gate2", dest=("y", 0), col0=D)
    po = Product("po", pw_out, 4, 4, 4, 2, "copy2", dest=("y", 0))
    ckv = Product("ckv", mw_in, 4, 1, 4, 2, "copy2", dest=("y", 0), col0=GW)
    kr = Product("kr", mw_in, 4, 1, 1, 2, "copy2", dest=("kr", 0), col0=2 * GW, width=64, pack="twice")
    cq = Product("cq", mw_in, 4, 1, 4, 1, "copy1", dest=40)
    mg = Product("mg", mw_in, 4, 4, 4, 1, "copy1", dest=16, col0=1088)
    uq = [Product(f"uq{j}", mw_uq, 1, 1, 3, 1, "copy1", half=1, width=384, pack="heads", col0=384 * j, dest=44)
          for j in range(8)]
    ukv = [Product(f"ukv{j}", mw_ukv, 1, 1, 4, 2, "copy2", src="ps", col0=GW * j, dest=("y", 0)) for j in range(8)]
    mo = Product("mo", mw_out, 4, 4, 4, 1, "copy1", dest=32)
    products = [kv, win_a, win_b, win_c, mixo, xq, xo, pu[0], pu[1], pg[0], pu[2], pg[1], pu[3], pg[2], pgate, pg[3],
                po, ckv, kr, cq, mg]
    products = [kv, win_a, win_b, win_c, mixo, xq, xo, pu[0], pg[0], pu[1], pg[1], pu[2], pg[2], pu[3], pg[3], pgate,
                po, ckv, kr, cq, mg]
    for j in range(8):
        products += [uq[j], ukv[j]]
    products += [mo]
    plan(products)

    ada = {win_a: 1, win_b: 1, win_c: 1, mixo: 1, xq: 1, xo: 1, pgate: 2, po: 2, ckv: 1, mg: 1}
    ada.update({p: 2 for p in pu})
    unit = 0
    for p in products:
        p.ada = ada.get(p, 0)
        p.unit0 = unit
        unit += p.ada * p.chunks * p.groups
    assert unit == 4 * 48

    ctx = ExitStack()
    with ctx:
        def sb(name, shape, dt=F32):
            return ctx.enter_context(nc.sbuf_tensor(name, shape, dt))

        def sem(name):
            return ctx.enter_context(nc.semaphore(name))

        all_steps = []

        def steps(name, order):
            st = Steps(sem(name), order)
            all_steps.append((name, st))
            return st

        BIG = sb("big", [P, NB, T])
        XS = sb("operand", [P, KD, 2, 2 * T], F32R)
        PS = sb("operand_small", [P, KC, 2, 2 * T], F32R)
        RAW = sb("raw", [P, 2, KC, GW])
        HI = sb("w_high", [P, 2, KC, GW], F32R)
        LO = sb("w_low", [P, 2, KC, GW], F32R)
        ARAW = sb("ada_raw", [P, 2, KC, 256])
        ACC = sb("ada_acc", [P, 2, 256])
        AD = sb("ada_out", [P, 48 * 4])
        VEC = vectors(a)
        PV = sb("vectors", [P, 4 * P])
        V, place, at = {}, {}, 0
        for name, _, n in VEC:
            if at % P + n > P:
                at += P - at % P
            V[name], place[name] = PV[:, at:at + n], at
            at += n
        assert at <= 4 * P
        VROW = BIG[:, 32:34, :].rearrange("p a t -> p (a t)")
        MODS = sb("modulations", [P, 10, KD])
        SC = sb("silu_c", [P, 2, KD])
        ident = sb("ident", [P, P])
        blockmask = sb("blockmask", [P, P])
        mlmask = sb("mlmask", [P, P])
        ones = sb("ones", [P, P])
        RST = sb("rstd", [P, T])
        small = sb("small", [P, 64])
        EPS = small[:, 60:61]
        EPSLN = small[:, 61:62]
        PB = [ctx.enter_context(nc.psum_tensor(f"bank{i}", [P, 512], F32)) for i in range(8)]

        raw_ready = [sem("raw_ready0"), sem("raw_ready1")]
        hi_ready, lo_ready, chunk_done, tile_done = sem("hi_ready"), sem("lo_ready"), sem("chunk_done"), sem("tile_done")
        half_moved, dve_freed, act_freed = sem("half_moved"), sem("bank_freed_dve"), sem("bank_freed_act")
        gate_ready, resid = sem("gate_ready"), sem("residual_step")
        ada_loaded = [sem("ada_loaded0"), sem("ada_loaded1")]
        ada_summed, ada_moved = sem("ada_summed"), sem("ada_moved")
        ada_link = sem("ada_link")
        freed = {"dve": dve_freed, "act": act_freed}
        consts_in, vec_in, tok_in, tok_free = sem("consts_in"), sem("vec_in"), sem("tok_in"), sem("tok_free")
        setup_done, silu_c = sem("setup_done"), sem("silu_c")
        tr_done, tr_free = sem("transposed"), sem("transpose_moved")
        sq_ready, sq_used, std_ready = sem("squares_ready"), sem("squares_summed"), sem("std_ready")
        hf_ready, xh_ready, xs_ready, norm_link = sem("normed"), sem("operand_high"), sem("operand_ready"), sem("norm_link")
        norm_done, out_done = sem("norm_done"), sem("out_done")
        dch, ach = sem("dve_chain"), sem("act_chain")
        S = {}

        def named(*names):
            for n in names:
                S[n] = sem(n)
        tiles = lambda t0, n=1: BIG[:, t0:t0 + n, :]
        tile = lambda t: BIG[:, t, :]

        block = ctx.enter_context(nc.Block())

        def sp_group(sp, p, i):
            for j in range(p.chunks):
                c = p.chunk0 + j
                w = p.chunks * i
                if isinstance(i, int):
                    c, w = c + w, 0
                slot = c % 2
                if c >= 2 or not isinstance(i, int):
                    sp.wait_ge(lo_ready, c + w - 1)
                rows = p.w[j * KC * P:(j + 1) * KC * P, :]
                src = rows.rearrange("(k p) n -> p k n", p=P)[:, :, bass.ds(p.col0 + p.stride * i, p.width)]
                sp.dma_start(RAW[:, slot, :, 0:p.width], src).then_inc(raw_ready[slot], 16)
                for q in range(p.ada):
                    u0 = p.unit0 + p.ada * j + q
                    uw = p.ada * p.chunks * i
                    if isinstance(i, int):
                        u0, uw = u0 + uw, 0
                    part, us = u0 % 4, u0 % 2
                    if u0 >= 2 or not isinstance(i, int):
                        sp.wait_ge(ada_link, 8 * (u0 + uw - 1))
                    if isinstance(i, int):
                        b = (u0 + uw) // 4
                        layer, col = b // 24, (b % 24) * 256
                    else:
                        b = u0 // 4
                        layer, col = b // 24, (b % 24) * 256 + 64 * uw
                    src = a["ada_w_2"][layer, part * KC * P:(part + 1) * KC * P, :]
                    src = src.rearrange("(k p) n -> p k n", p=P)[:, :, bass.ds(col, 256)]
                    sp.dma_start(ARAW[:, us], src).then_inc(ada_loaded[us], 16)

        def packed(p):
            if p.pack == "heads":
                def nope(buf, slot, raw):
                    if raw:
                        return buf[:, slot, :, 0:384].rearrange("p k (a n) -> p k a n", a=2)[:, :, :, 0:P]
                    return buf[:, slot, :, 0:2 * P].rearrange("p k (a n) -> p k a n", a=2)

                def rope(buf, slot, raw):
                    if raw:
                        return buf[:, slot, :, 0:384].rearrange("p k (a n) -> p k a n", a=2)[:, :, :, P:P + 64]
                    return buf[:, slot, :, 2 * P:3 * P].rearrange("p k (a n) -> p k a n", a=2)
                return [nope, rope]
            if p.pack == "twice":
                return [lambda buf, slot, raw, r=r: buf[:, slot, :, 0:64] if raw else buf[:, slot, :, 64 * r:64 * r + 64]
                        for r in range(2)]
            return [lambda buf, slot, raw: buf[:, slot, :, 0:p.width]]

        def act_high(act, p, i, j):
            c, w = p.chunk0 + j, p.chunks * i
            if isinstance(i, int):
                c, w = c + w, 0
            slot = c % 2
            act.wait_ge(raw_ready[slot], 16 * (c // 2 + 1) + 8 * w)
            if c >= 2 or not isinstance(i, int):
                act.wait_ge(chunk_done, c + w - 1)
            for view in packed(p):
                ins = nc.scalar.activation(view(HI, slot, False), view(RAW, slot, True), ACT.Copy)
            ins.then_inc(hi_ready, 1)

        def dve_low(dve, p, i, j):
            c, w = p.chunk0 + j, p.chunks * i
            if isinstance(i, int):
                c, w = c + w, 0
            slot = c % 2
            dve.wait_ge(hi_ready, c + w + 1)
            for view in packed(p):
                ins = nc.vector.tensor_sub(view(LO, slot, False), view(RAW, slot, True), view(HI, slot, False).bitcast(F32))
            ins.then_inc(lo_ready, 1)

        def wait_tile(eng, p, i, n):
            if n < p.tiles - 1:
                eng.wait_ge(tile_done, p.tile0 + n + 1 + (p.tiles - 1) * i)
            else:
                eng.wait_ge(chunk_done, p.chunk0 + p.chunks + p.chunks * i)

        def dest_ap(p, i, n):
            if isinstance(p.dest, tuple):
                where, t0 = p.dest
                if where == "pool_u":
                    return UPAD[:, n]
                if where == "kr":
                    return KRT[:, :]
                base = YT0 + 2 * (t0 + n)
                if isinstance(i, int):
                    base += 2 * p.tiles * i
                    return BIG[:, base:base + 2, :].rearrange("p a t -> p (a t)")
                return BIG[:, bass.ds(base + 2 * p.tiles * i, 2), :].rearrange("p a t -> p (a t)")
            base = p.dest + n
            if isinstance(i, int):
                return BIG[:, base + p.tiles * i, :]
            return BIG[:, bass.ds(base + p.tiles * i, 1), :].rearrange("p a t -> p (a t)")

        def act_evac(act, p, i):
            for n in range(p.tiles):
                if p.kind == "copy1":
                    wait_tile(act, p, i, n)
                    nc.scalar.activation(dest_ap(p, i, n), PB[n][:, T:2 * T], ACT.Copy).then_inc(half_moved, 1)
                elif p.kind == "copy2":
                    wait_tile(act, p, i, n)
                    src = PB[n][:, :]
                    d = dest_ap(p, i, n)
                    if p.dest[0] == "pool_u":
                        src = src.rearrange("p (s t) -> p s t", s=2)
                        d = d[:, :, 8:8 + T]
                    nc.scalar.activation(d, src, ACT.Copy).then_inc(dve_freed, 1)
                elif p.kind == "gate2":
                    wait_tile(act, p, i, n)
                    nc.scalar.activation(GT[:, n], PB[n][:, :], ACT.Sigmoid).then_inc(gate_ready, 1)

        def dve_evac(dve, p, i):
            for n in range(p.tiles):
                d = dest_ap(p, i, n)
                if p.kind == "copy1":
                    dve.wait_ge(half_moved, p.half0 + n + 1 + p.tiles * i)
                    nc.vector.tensor_tensor(d, PB[n][:, 0:T], d, ALU.add).then_inc(dve_freed, 1)
                elif p.kind == "add1":
                    wait_tile(dve, p, i, n)
                    nc.vector.tensor_tensor(d, PB[n][:, T:2 * T], d, ALU.add).then_inc(resid, 1)
                    dve.wait_ge(resid, p.half0 + n + 1 + p.tiles * i)
                    nc.vector.tensor_tensor(d, PB[n][:, 0:T], d, ALU.add).then_inc(dve_freed, 1)
                elif p.kind == "grp":
                    wait_tile(dve, p, i, n)
                    k = p.dest[1] + n
                    nc.vector.tensor_scalar(d, PB[n][:, :], V["pool_b"][:, k:k + 1], V["pool_s"][:, k:k + 1],
                                            ALU.add, ALU.mult).then_inc(dve_freed, 1)
                elif p.kind == "gate2":
                    dve.wait_ge(gate_ready, n + 1 + p.tiles * i)
                    nc.vector.tensor_tensor(GT[:, n], GT[:, n], PB[n][:, :], ALU.mult).then_inc(dve_freed, 1)
                    dve.wait_ge(dve_freed, p.free0 + n + 1 + p.tiles * i)
                    nc.vector.tensor_tensor(d, GT[:, n], d, ALU.mult).then_inc(resid, 1)

        def dve_ada(dve, p, i, j):
            for q in range(p.ada):
                u0, uw = p.unit0 + p.ada * j + q, p.ada * p.chunks * i
                if isinstance(i, int):
                    u0, uw = u0 + uw, 0
                part, us = u0 % 4, u0 % 2
                dve.wait_ge(ada_loaded[us], 16 * (u0 // 2 + 1) + 8 * uw)
                if part == 0 and (u0 >= 4 or not isinstance(i, int)):
                    dve.wait_ge(ada_summed, u0 // 4 + (0 if isinstance(i, int) else (p.ada * p.chunks // 4) * i))
                for k in range(KC):
                    for v in range(2):
                        if part == 0 and k == 0:
                            ins = nc.vector.tensor_scalar(ACC[:, v], ARAW[:, us, k], SC[:, v, 0:1], None, ALU.mult)
                        else:
                            dve.wait_ge(ada_link, 8 * u0 + 2 * k + v - 1 + 8 * uw)
                            ins = nc.vector.scalar_tensor_tensor(ACC[:, v], ARAW[:, us, k],
                                                                 SC[:, v, part * KC + k:part * KC + k + 1], ACC[:, v],
                                                                 ALU.mult, ALU.add)
                        ins.then_inc(ada_link, 1)

        def pe_ada(pe, b, w=0):
            pe.wait_ge(ada_link, 32 * (b + 1) + 32 * w)
            if b >= 1 or not isinstance(w, int):
                pe.wait_ge(ada_moved, b + w)
            for n in range(2):
                for v in range(2):
                    ins = pe.matmul(PB[4][:, 2 * n + v:2 * n + v + 1], ACC[:, v, n * P:(n + 1) * P], ones[:, 0:1],
                                    start=True, stop=True, skip_group_check=True)
            ins.then_inc(ada_summed, 1)

        def act_ada(act, b, w=0):
            act.wait_ge(ada_summed, b + 1 + w)
            nc.scalar.activation(AD[:, bass.ds(4 * b + 4 * w, 4)], PB[4][:, 0:4], ACT.Copy).then_inc(ada_moved, 1)

        def ada_ready(p, i, j):
            done = p.ada * (j + (p.chunks * i if isinstance(i, int) else 0))
            if not p.ada or done % 4 or (done == 0 and isinstance(i, int)):
                return None
            return (p.unit0 + done) // 4 - 1

        def pe_chunk(pe, p, i, j):
            c, w = p.chunk0 + j, p.chunks * i
            if isinstance(i, int):
                c, w = c + w, 0
            slot = c % 2
            pe.wait_ge(lo_ready, c + w + 1)
            for n in range(p.tiles):
                if j == 0:
                    if isinstance(i, int) and i == 0:
                        if p.first_bank_wait[n]:
                            pe.wait_ge(freed[p.first_bank_wait[n][0]], p.first_bank_wait[n][1])
                    else:
                        pe.wait_ge(dve_freed, p.free0 + p.tiles * i - p.tiles + n + 1)
                for k in range(KC):
                    kk = j * KC + k
                    pick = lambda buf: buf[:, slot, k, n * P:(n + 1) * P]
                    first, last = kk == 0, kk == p.chunks * KC - 1
                    if p.seqs == 1:
                        x = XS[:, kk, :, p.half * T:(p.half + 1) * T]
                        pe.matmul(PB[n][:, :], pick(HI), x, start=first, stop=False, skip_group_check=True)
                        ins = pe.matmul(PB[n][:, T:2 * T], pick(LO), x[:, 0, :], start=False, stop=last,
                                        skip_group_check=True)
                    else:
                        x = (XS if p.src == "xs" else PS)[:, kk]
                        pe.matmul(PB[n][:, :], pick(HI), x[:, 0, :], start=first, stop=False, skip_group_check=True)
                        pe.matmul(PB[n][:, :], pick(HI), x[:, 1, :], start=False, stop=False, skip_group_check=True)
                        ins = pe.matmul(PB[n][:, :], pick(LO), x[:, 0, :], start=False, stop=last,
                                        skip_group_check=True)
                if n < p.tiles - 1:
                    if j == p.chunks - 1:
                        ins.then_inc(tile_done, 1)
                else:
                    ins.then_inc(chunk_done, 1)

        half = 0
        rs = 0
        for p in products:
            if p.kind == "copy1":
                p.half0 = half
                half += p.tiles * p.groups
            elif p.kind == "add1":
                p.half0 = rs
                rs += p.tiles * p.groups

        def sp_product(sp, p):
            sp_group(sp, p, 0)
            if p.groups > 1:
                step = 2 if p.chunks % 2 else 1
                if step == 2:
                    for g in range(1, p.groups):
                        sp_group(sp, p, g)
                    return
                with sp.Fori(1, p.groups) as i:
                    sp_group(sp, p, i)

        def act_product(act, p):
            def group(i, prev, aw):
                for j in range(p.chunks):
                    act_high(act, p, i, j)
                    if j == 0 and prev is not None:
                        act_evac(act, p, prev)
                    b = ada_ready(p, i, j)
                    if b is not None:
                        act_ada(act, b, aw)
            group(0, None, 0)
            if p.groups > 1:
                if p.chunks % 2:
                    for g in range(1, p.groups):
                        group(g, g - 1, 0)
                    act_evac(act, p, p.groups - 1)
                else:
                    with act.Fori(1, p.groups) as i:
                        group(i, i - 1, (p.ada * p.chunks // 4) * i)
                    act_evac(act, p, p.groups - 1)
            else:
                act_evac(act, p, 0)
            if p.ada:
                act_ada(act, (p.unit0 + p.ada * p.chunks * p.groups) // 4 - 1)

        def dve_product(dve, p):
            def group(i, prev):
                for j in range(p.chunks):
                    dve_low(dve, p, i, j)
                    if j == 0 and prev is not None:
                        dve_evac(dve, p, prev)
                    dve_ada(dve, p, i, j)
            group(0, None)
            if p.groups > 1:
                if p.chunks % 2:
                    for g in range(1, p.groups):
                        group(g, g - 1)
                else:
                    with dve.Fori(1, p.groups) as i:
                        group(i, i - 1)
            dve_evac(dve, p, p.groups - 1)

        def pe_product(pe, p, ready=None):
            def group(i, first, aw):
                for j in range(p.chunks):
                    if first and ready:
                        ready(pe, j)
                    pe_chunk(pe, p, i, j)
                    b = ada_ready(p, i, j)
                    if b is not None:
                        pe_ada(pe, b, aw)
            group(0, True, 0)
            if p.groups > 1:
                if p.chunks % 2:
                    for g in range(1, p.groups):
                        group(g, False, 0)
                else:
                    with pe.Fori(1, p.groups) as i:
                        group(i, False, (p.ada * p.chunks // 4) * i)
            if p.ada:
                pe_ada(pe, (p.unit0 + p.ada * p.chunks * p.groups) // 4 - 1)

        TOKT = {0: 40, 1: 40, 2: 40}
        XDEST = {0: CT0, 1: 0, 2: CT0}

        def tok(q):
            return BIG[:, TOKT[q]:TOKT[q] + 16, :].rearrange("p (a k) t -> p a (k t)", a=2)

        def sp_turn(sp, q, src):
            sp.dma_start(tok(q), src.rearrange("(a p) f -> p a f", p=P)).then_inc(tok_in, 16)

        def pe_turn(pe, q):
            if q == 0:
                pe.wait_ge(consts_in, 16 * 3)
            pe.wait_ge(tok_in, 16 * (q + 1))
            for kk in range(8):
                n = 8 * q + kk
                if n >= 2:
                    pe.wait_ge(tr_free, n - 1)
                for s in range(4):
                    k, h = 2 * kk + s // 2, s % 2
                    ins = pe.transpose(PB[5 + kk % 2][:, s * P:(s + 1) * P], tok(q)[:, h, k * P:(k + 1) * P], ident[:, :])
                ins.then_inc(tr_done, 1)

        def act_turn(act, q):
            for kk in range(8):
                act.wait_ge(tr_done, 8 * q + kk + 1)
                d = BIG[:, XDEST[q] + 2 * kk:XDEST[q] + 2 * kk + 2, :].rearrange("p k t -> p (k t)")
                nc.scalar.activation(d, PB[5 + kk % 2][:, :], ACT.Copy).then_inc(tr_free, 1)

        def src_tiles(n, k, count=1):
            t0, st = n["src"]
            if count == 1:
                return BIG[:, t0 + st * k, :]
            return BIG[:, t0 + st * k:t0 + st * (k + count - 1) + 1:st, :]

        def act_norm(act, n):
            groups = n["nk"] // 4
            for s in range(groups):
                if s >= 2:
                    act.wait_ge(sq_used, n["sq0"] + s - 1)
                nc.scalar.activation(BIG[:, SQ0 + 4 * (s % 2):SQ0 + 4 * (s % 2) + 4, :], src_tiles(n, 4 * s, 4),
                                     ACT.Square).then_inc(sq_ready, 1)
            act.wait_ge(sq_used, n["sq0"] + groups)
            if n["rst_wait"]:
                act.wait_ge(*n["rst_wait"])
            nc.scalar.activation(RST[:, :], PB[5][:, 0:T], ACT.Sqrt, bias=EPS, scale=1.0 / (P * n["nk"])).then_inc(std_ready, 1)
            if n["mode"] == "operand":
                for k in range(n["nk"]):
                    act.wait_ge(hf_ready, n["hf0"] + k + 1)
                    hf = BIG[:, HF0 + k % 4, :]
                    if n["shift"] is None:
                        nc.scalar.activation(n["dst"](k, 0), hf, ACT.Copy).then_inc(xh_ready, 1)
                    else:
                        nc.scalar.activation(n["dst"](k, 0), hf, ACT.Identity, bias=n["shift"](k)).then_inc(xh_ready, 1)

        def pe_norm(pe, n):
            for s in range(n["nk"] // 4):
                pe.wait_ge(sq_ready, n["sq0"] + s + 1)
                for k in range(4):
                    ins = pe.matmul(PB[5][:, 0:T], ones[:, :], BIG[:, SQ0 + 4 * (s % 2) + k, :],
                                    start=(s == 0 and k == 0), stop=(s == n["nk"] // 4 - 1 and k == 3))
                ins.then_inc(sq_used, 1)

        def dve_norm(dve, n):
            dve.wait_ge(std_ready, n["index"] + 1)
            nc.vector.reciprocal(RST[:, :], RST[:, :]).then_inc(norm_link, 1)
            dve.wait_ge(norm_link, n["link0"] + 1)

            def low(k):
                dve.wait_ge(xh_ready, n["xh0"] + k + 1)
                hf, hi, lo = BIG[:, HF0 + k % 4, :], n["dst"](k, 0).bitcast(F32), n["dst"](k, 1)
                if n["shift"] is None:
                    nc.vector.tensor_sub(lo, hf, hi).then_inc(xs_ready, 1)
                else:
                    nc.vector.scalar_tensor_tensor(lo, hf, n["shift"](k), hi, ALU.add, ALU.subtract).then_inc(xs_ready, 1)

            for k in range(n["nk"]):
                if n["mode"] == "operand":
                    if k >= 4:
                        dve.wait_ge(xs_ready, n["xs0"] + k - 3)
                    nc.vector.scalar_tensor_tensor(BIG[:, HF0 + k % 4, :], src_tiles(n, k), n["gain"](k), RST[:, :],
                                                   ALU.mult, ALU.mult).then_inc(hf_ready, 1)
                    if k >= 1:
                        low(k - 1)
                elif n["mode"] == "inplace":
                    nc.vector.scalar_tensor_tensor(src_tiles(n, k), src_tiles(n, k), n["gain"](k), RST[:, :],
                                                   ALU.mult, ALU.mult).then_inc(norm_done, 1)
                else:
                    if k >= 4:
                        dve.wait_ge(norm_done, n["nd0"] + k - 3)
                    nc.vector.scalar_tensor_tensor(BIG[:, HF0 + k % 4, :], src_tiles(n, k), n["gain"](k), RST[:, :],
                                                   ALU.mult, ALU.mult).then_inc(norm_link, 1)
                    dve.wait_ge(norm_link, n["link0"] + 2 + k)
                    d = BIG[:, n["dst"] + k, :]
                    nc.vector.tensor_tensor(d, d, BIG[:, HF0 + k % 4, :], ALU.add).then_inc(norm_done, 1)
            if n["mode"] == "operand":
                low(n["nk"] - 1)

        xs_dst = lambda half: (lambda k, part: XS[:, k, part, half * T:(half + 1) * T])
        ps_dst = lambda half: (lambda k, part: PS[:, k, part, half * T:(half + 1) * T])
        vcol = lambda name: (lambda k: V[name][:, k:k + 1])
        mod = lambda r: (lambda k: MODS[:, r, k:k + 1])
        norms = {
            "mem": dict(src=(CT0, 1), nk=16, gain=vcol("mem_g"), shift=None, dst=xs_dst(1), mode="operand"),
            "mix": dict(src=(0, 1), nk=16, gain=vcol("mix_g"), shift=None, dst=xs_dst(0), mode="operand"),
            "xa": dict(src=(0, 1), nk=16, gain=vcol("xa_g"), shift=None, dst=xs_dst(0), mode="operand"),
            "final": dict(src=(0, 1), nk=16, gain=vcol("final_g"), shift=None, dst=None, mode="inplace"),
            "pre0": dict(src=(0, 1), nk=16, gain=mod(0), shift=mod(2), dst=xs_dst(0), mode="operand"),
            "pre0c": dict(src=(CT0, 1), nk=16, gain=mod(1), shift=mod(3), dst=xs_dst(1), mode="operand"),
            "post0": dict(src=(YT0, 2), nk=16, gain=mod(4), shift=None, dst=0, mode="update"),
            "post0c": dict(src=(YT0 + 1, 2), nk=16, gain=mod(5), shift=None, dst=CT0, mode="update"),
            "pre1": dict(src=(0, 1), nk=16, gain=mod(0), shift=mod(2), dst=xs_dst(0), mode="operand"),
            "pre1c": dict(src=(CT0, 1), nk=16, gain=mod(1), shift=mod(3), dst=xs_dst(1), mode="operand"),
            "ckv": dict(src=(32, 2), nk=4, gain=vcol("kv_g"), shift=None, dst=ps_dst(0), mode="operand"),
            "ckvc": dict(src=(33, 2), nk=4, gain=vcol("kv_g"), shift=None, dst=ps_dst(1), mode="operand"),
            "cq": dict(src=(40, 1), nk=4, gain=vcol("q_g"), shift=None, dst=xs_dst(1), mode="operand"),
            "post1": dict(src=(32, 1), nk=16, gain=mod(4), shift=None, dst=0, mode="update"),
        }
        sq = hf = link = nd = 0
        rst_wait = None
        for index, n in enumerate(norms.values()):
            n.update(rst_wait=rst_wait, index=index, sq0=sq, hf0=hf, xh0=hf, xs0=hf, link0=link, nd0=nd)
            sq += n["nk"] // 4
            link += 1
            if n["mode"] == "operand":
                hf += n["nk"]
            elif n["mode"] == "update":
                link += n["nk"]
                nd += n["nk"]
            else:
                nd += n["nk"]
            rst_wait = (xs_ready, hf) if n["mode"] == "operand" else (norm_done, nd)

        setup = steps("setup_dve", [("rows",), ("ones",), ("eps",), ("epsln",), ("silu",)])
        sc_act, vec_turned, pv_ready = sem("silu_c_sigmoid"), sem("vectors_turned"), sem("vectors_ready")

        def pe_setup(pe):
            pe.wait_ge(vec_in, VEC_IN)
            pe.wait_ge(consts_in, 48)
            for b in range(4):
                ins = pe.transpose(PB[5][:, b * P:(b + 1) * P], VROW[:, b * P:(b + 1) * P], ident[:, :])
            ins.then_inc(vec_turned, 1)

        def act_setup(act):
            for i, (dst, name) in enumerate(((ident, "ident"), (blockmask, "blockmask"), (mlmask, "mlmask"))):
                act.dma_start(dst[:, :], a[name]).then_inc(consts_in, 16)
            act.wait_ge(setup.sem, 1)
            for name, src, n in VEC:
                b, r = place[name] // P, place[name] % P
                act.dma_start(VROW[r:r + n, b * P:(b + 1) * P], src).then_inc(vec_in, 16)
            act.dma_start(gb[0:4, 0:1], a["ml_bi"].rearrange("l h -> h l")).then_inc(vec_in, 16)
            act.dma_start(gb[0:4, 1:2], a["ml_bf"].rearrange("l h -> h l")).then_inc(vec_in, 16)
            act.wait_ge(vec_turned, 1)
            nc.scalar.activation(PV[:, :], PB[5][:, :], ACT.Copy).then_inc(pv_ready, 1)
            act.wait_ge(pv_ready, 1)
            for v, name in enumerate(("c", "c_ctx")):
                nc.scalar.activation(SC[:, v, :], V[name], ACT.Sigmoid).then_inc(sc_act, 1)

        def dve_setup(dve):
            setup.inc(nc.vector.memset(VROW, 0.0), "rows")
            setup.inc(nc.vector.memset(ones[:, :], 1.0), "ones")
            setup.inc(nc.vector.memset(EPS, RMS_EPS), "eps")
            setup.inc(nc.vector.memset(EPSLN, LN_EPS), "epsln")
            dve.wait_ge(sc_act, 2)
            setup.inc(nc.vector.tensor_tensor(SC[:, :, :], SC[:, :, :],
                                              PV[:, CCOL:CCOL + 32].rearrange("p (v k) -> p v k", v=2), ALU.mult), "silu")
            assert place["c"] == CCOL and place["c_ctx"] == CCOL + 16

        ends = {"pe": sem("stage_end_pe"), "act": sem("stage_end_act"), "dve": sem("stage_end_dve")}
        stages = {"pe": 0, "act": 0, "dve": 0}

        def stage_end(eng, me):
            stages[me] += 1
            eng.drain().then_inc(ends[me], 1)
            for other in ends:
                if other != me:
                    eng.wait_ge(ends[other], stages[me])

        def l1p_names():
            return ["den", "rec", "z", "z2", "h17"] + [f"h{c}" for c in (15, 13, 11, 9, 7, 5, 3)] + ["l1p"]

        def dve_log1p(dve, st, y, t, z, z2, out_):
            v = nc.vector
            st.inc(v.tensor_scalar(t, y, 2.0, None, ALU.add), "den")
            st.wait(dve, "den")
            st.inc(v.reciprocal(t, t), "rec")
            st.wait(dve, "rec")
            st.inc(v.tensor_tensor(z, y, t, ALU.mult), "z")
            st.wait(dve, "z")
            st.inc(v.tensor_tensor(z2, z, z, ALU.mult), "z2")
            st.wait(dve, "z2")
            st.inc(v.tensor_scalar(t, z2, 1.0 / 17, None, ALU.mult), "h17")
            last = "h17"
            for c in (15, 13, 11, 9, 7, 5, 3):
                st.wait(dve, last)
                last = f"h{c}"
                st.inc(v.scalar_tensor_tensor(t, t, 1.0 / c, z2, ALU.add, ALU.mult), last)
            st.wait(dve, last)
            st.inc(v.scalar_tensor_tensor(out_, t, 1.0, z, ALU.add, ALU.mult), "l1p")
            st.wait(dve, "l1p")

        LW = BIG[:, 20:24, :].rearrange("p a (b t) -> p (a b) t", b=2)
        MW = BIG[:, 46, 0:72].rearrange("p (n t o) -> p n t o", n=3, t=6)
        mw_in = sem("ml_w_in")
        SEL = BIG[0:4, 16:18, :].rearrange("p a t -> p (a t)")
        gb = small[:, 56:58]
        VEC_IN = 16 * (len(VEC) + 2)
        CCOL = 32
        sp4, spt, spz, spz2 = small[:, 0:4], small[:, 4:8], small[:, 8:12], small[:, 12:16]
        xc = lambda b: tile(24 + b)
        ra = lambda b: tile(28 + b)
        ix = lambda b: tile(67 + b)
        lq = lambda b: tile(71 + b)
        lru_act = steps("lru_act", [("abs",), ("exp",)] + [(n, b) for b in range(4) for n in ("r", "i", "zs")]
                        + [("q", b) for b in range(4)] + [("a", b) for b in range(4)] + [("sq", b) for b in range(4)])
        lru_pe = steps("lru_pe", [(n, b) for b in range(4) for n in ("r", "i")])
        lru_dve = steps("lru_dve", [(n, b) for b in range(4) for n in ("c3", "c2", "c1", "c0")]
                        + [(n,) for n in l1p_names()] + [("spm",), ("sp",)]
                        + [(n, b) for b in range(4) for n in ("la", "ixc", "zsz")]
                        + [(n, b) for b in range(4) for n in ("q1", "q1r", "q2")]
                        + [(n, b) for b in range(4) for n in ("u", "scan", "y")])

        def dve_conv(dve, st, src, dst, w, b, taps, key):
            st.inc(nc.vector.tensor_scalar(dst, src, w(3), b, ALU.mult, ALU.add), "c3", key)
            for j in (2, 1, 0):
                s = 3 - j
                st.wait(dve, f"c{j + 1}", key)
                st.inc(nc.vector.scalar_tensor_tensor(dst[:, s:T], src[:, 0:T - s], w(j), dst[:, s:T], ALU.mult, ALU.add),
                       f"c{j}", key)

        def dve_lru(dve):
            v = nc.vector
            for b in range(4):
                dve_conv(dve, lru_dve, tile(LX + b), xc(b), lambda j: V["lru_conv_w"][:, 4 * j + b:4 * j + b + 1],
                         V["lru_conv_b"][:, b:b + 1], 4, b)
            lru_act.wait(dve, "exp")
            dve_log1p(dve, lru_dve, sp4, spt, spz, spz2, spz)
            lru_dve.inc(v.tensor_scalar(spt, V["lru_lambda"], -1.0, 0.0, ALU.mult, ALU.max), "spm")
            lru_dve.wait(dve, "spm")
            lru_dve.inc(v.scalar_tensor_tensor(sp4, spz, 2.0, spt, ALU.mult, ALU.add), "sp")
            lru_dve.wait(dve, "sp")
            for b in range(4):
                lru_act.wait(dve, "r", b)
                lru_dve.inc(v.tensor_scalar(ra(b), ra(b), sp4[:, b:b + 1], 8.0, ALU.mult, ALU.mult), "la", b)
                lru_act.wait(dve, "i", b)
                lru_dve.inc(v.tensor_tensor(ix(b), ix(b), xc(b), ALU.mult), "ixc", b)
                lru_act.wait(dve, "zs", b)
                lru_dve.inc(v.tensor_tensor(tile(LZ + b), tile(LZ + b), xc2(b), ALU.mult), "zsz", b)
            for b in range(4):
                lru_act.wait(dve, "q", b)
                lru_dve.inc(v.tensor_scalar(xc(b), lq(b), 1.0, None, ALU.add), "q1", b)
                lru_dve.wait(dve, "q1", b)
                lru_dve.inc(v.reciprocal(xc(b), xc(b)), "q1r", b)
                lru_dve.wait(dve, "q1r", b)
                lru_dve.inc(v.scalar_tensor_tensor(lq(b), lq(b), 2.0, xc(b), ALU.mult, ALU.mult), "q2", b)
            for b in range(4):
                lru_act.wait(dve, "sq", b)
                lru_dve.inc(v.tensor_tensor(ix(b), ix(b), lq(b), ALU.mult), "u", b)
                lru_dve.wait(dve, "u", b)
                lru_act.wait(dve, "a", b)
                lru_dve.inc(v.tensor_tensor_scan(xc(b), ra(b), ix(b), 0.0, ALU.mult, ALU.add), "scan", b)
                lru_dve.wait(dve, "scan", b)
                lru_dve.inc(v.tensor_tensor(tile(LX + b), xc(b), tile(LZ + b), ALU.mult), "y", b)

        xc2 = lambda b: tile(16 + b)

        def pe_lru(pe):
            for b in range(4):
                lru_dve.wait(pe, "c0", b)
                if b >= 1:
                    lru_act.wait(pe, "i", b - 1)
                lru_pe.inc(pe.matmul(PB[5][:, 0:T], LW[:, b], xc(b), start=True, stop=True), "r", b)
                lru_pe.inc(pe.matmul(PB[6][:, 0:T], LW[:, 4 + b], xc(b), start=True, stop=True), "i", b)

        def act_lru(act):
            s = nc.scalar.activation
            lru_act.inc(s(sp4, V["lru_lambda"], ACT.Abs), "abs")
            lru_act.wait(act, "abs")
            lru_act.inc(s(sp4, sp4, ACT.Exp, scale=-1.0), "exp")
            for b in range(4):
                lru_pe.wait(act, "r", b)
                lru_act.inc(s(ra(b), PB[5][:, 0:T], ACT.Sigmoid, bias=V["lru_ba"][:, b:b + 1]), "r", b)
                lru_pe.wait(act, "i", b)
                lru_act.inc(s(ix(b), PB[6][:, 0:T], ACT.Sigmoid, bias=V["lru_bx"][:, b:b + 1]), "i", b)
                lru_act.inc(s(xc2(b), tile(LZ + b), ACT.Sigmoid), "zs", b)
            for b in range(4):
                lru_dve.wait(act, "la", b)
                lru_act.inc(s(lq(b), ra(b), ACT.Tanh), "q", b)
            for b in range(4):
                lru_act.wait(act, "q", b)
                lru_act.inc(s(ra(b), ra(b), ACT.Exp, scale=-1.0), "a", b)
            for b in range(4):
                lru_dve.wait(act, "q2", b)
                lru_act.inc(s(lq(b), lq(b), ACT.Sqrt), "sq", b)

        split_hi, split_lo = sem("split_high"), sem("split_low")
        splits = {}
        order = [("lru", 4), ("ml", 6), ("mo", 6), ("xo", 4), ("py", 16), ("pp0", 4), ("pp1", 4), ("pp2", 4), ("pp3", 4),
                 ("mla", 16)]
        order = [("lru", 4), ("ml", 6), ("mo", 6), ("xo", 4), ("pp0", 4), ("pp1", 4), ("pp2", 4), ("pp3", 4), ("py", 16)]
        n0 = 0
        for name, n in order:
            splits[name] = n0
            n0 += n

        def act_split(act, name, k, src, dst):
            nc.scalar.activation(dst, src, ACT.Copy).then_inc(split_hi, 1)

        def dve_split(dve, name, k, src, dst, hi):
            dve.wait_ge(split_hi, splits[name] + k + 1)
            nc.vector.tensor_sub(dst, src, hi.bitcast(F32)).then_inc(split_lo, 1)

        def rows(t):
            return BIG[0:4, t, :]
        rF, rY, rT, rZ, rZ2, rB, rE, rM, rI = (rows(t) for t in (76, 77, 28, 29, 30, 31, 46, 47, G))
        QR = BIG[0:4, 73:76, :].rearrange("p a (b l) -> p (a b) l", l=P)
        QC = small[:, 20:44].rearrange("p (q h) -> p q h", h=4)
        m1, nm0 = small[0:4, 44:45], small[0:4, 45:46]
        fg_in, sel_in, lw_in = sem("forget_rows_in"), sem("sel_in"), sem("lru_w_in")
        mg_dve = steps("mg_dve", [("f",), ("i",)] + [(n,) for n in l1p_names()] + [("fm",), ("lf",), ("b0",), ("b1",),
                       ("e",), ("M0",), ("nm0",), ("m1",), ("M1",), ("bm",), ("qe",), ("qc",)] + [("t", h) for h in range(4)])
        mg_act = steps("mg_act", [("abs",), ("exp",), ("em",), ("w0",), ("s1",)]
                       + [("E", h, c) for h in range(4) for c in range(2)])
        mg_pe = steps("mg_pe", [("cols",), ("M", 0), ("M", 1), ("M", 2), ("M", 3)])

        def act_mgates(act):
            s = nc.scalar.activation
            act.dma_start(rF, BIG[4:8, G, :]).then_inc(fg_in, 16)
            act.dma_start(SEL, a["sel"]).then_inc(sel_in, 16)
            mg_dve.wait(act, "f")
            mg_act.inc(s(rY, rF, ACT.Abs), "abs")
            mg_act.wait(act, "abs")
            mg_act.inc(s(rY, rY, ACT.Exp, scale=-1.0), "exp")
            mg_dve.wait(act, "bm")
            mg_act.inc(s(QR[:, 2:4, :], rB.rearrange("p (c l) -> p c l", c=2), ACT.Exp, scale=-1.0), "em")
            mg_act.inc(s(QR[:, 4, :], rE[:, 0:P], ACT.Exp, bias=nm0), "w0")
            mg_act.inc(s(QR[:, 5, :], rM[:, P:T], ACT.Exp, bias=m1, scale=-1.0), "s1")
            for h in range(4):
                mg_dve.wait(act, "t", h)
                for c in range(2):
                    e = BIG[:, EX + h, c * P:(c + 1) * P]
                    mg_act.inc(s(e, e, ACT.Exp, bias=QC[:, c, h:h + 1]), "E", h, c)

        def dve_mgates(dve):
            v, st = nc.vector, mg_dve
            dve.wait_ge(fg_in, 16)
            st.inc(v.tensor_scalar(rF, rF, gb[0:4, 1:2], None, ALU.add), "f")
            st.inc(v.tensor_scalar(rI, rI, gb[0:4, 0:1], None, ALU.add), "i")
            mg_act.wait(dve, "exp")
            dve_log1p(dve, st, rY, rT, rZ, rZ2, rZ)
            st.inc(v.tensor_scalar(rF, rF, 0.0, None, ALU.min), "fm")
            st.wait(dve, "fm")
            st.inc(v.scalar_tensor_tensor(rF, rZ, -2.0, rF, ALU.mult, ALU.add), "lf")
            st.wait(dve, "lf")
            for c in range(2):
                st.inc(v.tensor_tensor_scan(rB[:, c * P:(c + 1) * P], ones[0:4, :], rF[:, c * P:(c + 1) * P], 0.0,
                                            ALU.mult, ALU.add), f"b{c}")
            st.wait(dve, "b1")
            st.inc(v.tensor_tensor(rE, rI, rB, ALU.subtract), "e")
            st.wait(dve, "e")
            st.inc(v.tensor_tensor_scan(rM[:, 0:P], ones[0:4, :], rE[:, 0:P], 0.0, ALU.mult, ALU.max), "M0")
            st.wait(dve, "M0")
            st.inc(v.tensor_scalar(nm0, rM[:, P - 1:P], -1.0, None, ALU.mult), "nm0")
            st.inc(v.tensor_tensor(m1, rM[:, P - 1:P], rB[:, P - 1:P], ALU.add), "m1")
            st.wait(dve, "m1")
            st.inc(v.tensor_tensor_scan(rM[:, P:T], ones[0:4, :], rE[:, P:T], m1, ALU.mult, ALU.max), "M1")
            st.wait(dve, "M1")
            st.inc(v.tensor_tensor(rB, rB, rM, ALU.add), "bm")
            st.inc(v.tensor_copy(QR[:, 0:2, :], rE.rearrange("p (c l) -> p c l", c=2)), "qe")
            mg_pe.wait(dve, "cols")
            st.inc(v.tensor_copy(small[:, 20:44], PB[5][:, 0:24]), "qc")
            for h in range(4):
                mg_pe.wait(dve, "M", 1 if h < 2 else 3)
                st.inc(v.scalar_tensor_tensor(BIG[:, EX + h, :].rearrange("p (c l) -> p c l", c=2),
                                              PB[6 + h // 2][:, (h % 2) * T:(h % 2 + 1) * T].rearrange("p (c l) -> p c l", c=2),
                                              -1.0, mlmask[:, :].unsqueeze(1).to_broadcast([P, 2, P]),
                                              ALU.mult, ALU.add), "t", h)

        def pe_mgates(pe):
            mg_act.wait(pe, "s1")
            mg_dve.wait(pe, "qe")
            for q in range(6):
                ins = pe.transpose(PB[5][:, 4 * q:4 * q + 4], QR[:, q, :], ident[0:4, 0:4])
            mg_pe.inc(ins, "cols")
            mg_dve.wait(pe, "bm")
            pe.wait_ge(sel_in, 16)
            for h in range(4):
                mg_pe.inc(pe.matmul(PB[6 + h // 2][:, (h % 2) * T:(h % 2 + 1) * T], SEL[:, h * P:(h + 1) * P], rM,
                                    start=True, stop=True, skip_group_check=True), "M", h)

        DH = 192
        BD = lambda n: BIG[:, 76 + (n % 4) // 2, (n % 2) * P:(n % 2 + 1) * P]
        VTV = BIG[:, VT:VT + 6, :].rearrange("p a t -> p (a t)").rearrange("p (c f) -> p c f", c=2)
        KTV = BIG[:, KTOK:KTOK + 3, :].rearrange("p a t -> p (a t)")
        SOV = BIG[:, SOT:SOT + 6, :].rearrange("p a t -> p (a t)").rearrange("p (c f) -> p c f", c=2)
        HNV = BIG[:, O:O + 6, :].rearrange("p a t -> p (a t)").rearrange("p (c f) -> p c f", c=2)
        mp_dve = steps("mp_dve", [(n, i) for i in range(6) for n in ("c3", "c2", "c1", "c0")] + [("uc", i) for i in range(6)]
                       + [("bd", n) for n in range(18)] + [("so", i) for i in range(6)])
        mp_act = steps("mp_act", [("sg", i) for i in range(6)]
                       + [(n, i) for i in range(6) for n in ("q", "k", "kt", "v")] + [("o", i) for i in range(6)])
        mp_pe = steps("mp_pe", [(n, i) for i in range(6) for n in ("q", "k", "v")] + [("o", i) for i in range(6)])

        def act_mproj(act):
            s = nc.scalar.activation
            for n, w in enumerate(("ml_wq", "ml_wk", "ml_wv")):
                act.dma_start(MW[:, n], a[w][0].rearrange("(t g) i o -> (g i) t o", g=32)).then_inc(mw_in, 16)
            for i in range(6):
                mp_dve.wait(act, "c0", i)
                mp_act.inc(s(tile(KT + i), tile(UC + i), ACT.Sigmoid), "sg", i)
            for i in range(6):
                mp_pe.wait(act, "q", i)
                mp_act.inc(s(tile(QT + i), PB[5][:, 0:T], ACT.Copy), "q", i)
                mp_pe.wait(act, "k", i)
                mp_act.inc(s(tile(KT + i), PB[6][:, 0:T], ACT.Copy, scale=DH ** -0.5), "k", i)
                mp_act.inc(s(KTV[:, i * P:(i + 1) * P], PB[6][:, T:T + P], ACT.Copy, scale=DH ** -0.5), "kt", i)
                mp_pe.wait(act, "v", i)
                mp_act.inc(s(VTV[:, :, i * P:(i + 1) * P], PB[7][:, 0:T].rearrange("p (c f) -> p c f", c=2), ACT.Copy), "v", i)
            for i in range(6):
                mp_act.inc(s(tile(O + i), tile(O + i), ACT.Sigmoid), "o", i)

        def dve_mproj(dve):
            v, st = nc.vector, mp_dve
            for i in range(6):
                dve_conv(dve, st, tile(U + i), tile(UC + i), lambda j: V["ml_conv_w"][:, 6 * j + i:6 * j + i + 1],
                         V["ml_conv_b"][:, i:i + 1], 4, i)
            for i in range(6):
                mp_act.wait(dve, "sg", i)
                st.inc(v.tensor_tensor(tile(UC + i), tile(UC + i), tile(KT + i), ALU.mult), "uc", i)
            dve.wait_ge(mw_in, 48)
            for n in range(18):
                i, m = n // 3, n % 3
                if n >= 4:
                    mp_pe.wait(dve, "qkv"[(n - 4) % 3], (n - 4) // 3)
                st.inc(v.tensor_tensor(BD(n).rearrange("p (g o) -> p g o", o=4),
                                       blockmask[:, :].rearrange("p (g o) -> p g o", o=4),
                                       MW[:, m, i, :].unsqueeze(1).to_broadcast([P, 32, 4]), ALU.mult), "bd", n)
            for i in range(6):
                mp_pe.wait(dve, "o", i)
                st.inc(v.tensor_copy(SOV[:, :, i * P:(i + 1) * P],
                                     PB[5 + i % 2][:, 0:T].rearrange("p (c f) -> p c f", c=2)), "so", i)

        def pe_mproj(pe):
            st = mp_pe
            for i in range(6):
                mp_dve.wait(pe, "bd", 3 * i)
                if i:
                    mp_act.wait(pe, "q", i - 1)
                st.inc(pe.matmul(PB[5][:, 0:T], BD(3 * i), tile(UC + i), start=True, stop=True), "q", i)
                mp_dve.wait(pe, "bd", 3 * i + 1)
                if i:
                    mp_act.wait(pe, "kt", i - 1)
                pe.matmul(PB[6][:, 0:T], BD(3 * i + 1), tile(UC + i), start=True, stop=True, skip_group_check=True)
                st.inc(pe.matmul(PB[6][:, T:T + P], tile(UC + i)[:, 0:P], BD(3 * i + 1), start=True, stop=True,
                                 skip_group_check=True), "k", i)
                mp_dve.wait(pe, "bd", 3 * i + 2)
                if i:
                    mp_act.wait(pe, "v", i - 1)
                for c in range(2):
                    ins = pe.matmul(PB[7][:, c * P:(c + 1) * P], tile(U + i)[:, c * P:(c + 1) * P], BD(3 * i + 2),
                                    start=True, stop=True, skip_group_check=True)
                st.inc(ins, "v", i)
            for i in range(6):
                mp_act.wait(pe, "o", i)
                if i >= 2:
                    mp_dve.wait(pe, "so", i - 2)
                for c in range(2):
                    ins = pe.transpose(PB[5 + i % 2][:, c * P:(c + 1) * P], tile(O + i)[:, c * P:(c + 1) * P], ident[:, :])
                st.inc(ins, "o", i)

        def segs(h):
            t = 3 * (h // 2)
            return [(t, 0, P, 0), (t + 1, 0, 64, P)] if h % 2 == 0 else [(t + 1, 64, P, 0), (t + 2, 0, P, 64)]

        CS = BIG[:, 16:21, :].rearrange("p a t -> p (a t)")[:, 0:6 * 193].rearrange("p (i e) -> p i e", e=193)
        WK = lambda h: BIG[:, 46 + h % 2, 0:DH]
        PT_ = lambda u: BIG[:, 76, (u % 2) * P:(u % 2 + 1) * P]
        NUM = BIG[:, 77, 0:193]
        INT = BIG[:, 75, 0:193]
        ST = small[:, 46:52]
        MV_ = small[:, 52:54]
        DEN = small[:, 54:55]
        units = [(h, c) for h in range(4) for c in range(2)]
        mh_dve = steps("mh_dve", [("wk", h) for h in range(4)] +
                       [k for u, (h, c) in enumerate(units) for k in
                        ([("p", u)] + ([("int", u)] if c else []) + [("num", u), ("abs", u), ("den", u), ("rden", u), ("h", u),
                         ("st", u), ("ag", u), ("rs", u), ("hn", u)])])
        mh_act = steps("mh_act", [("cs", h) for h in range(4)] + [("std", u) for u in range(8)])
        mh_pe = steps("mh_pe", [("cs", h) for h in range(4)] +
                      [k for u, (h, c) in enumerate(units) for k in ([("s", u)] + ([("int", u)] if c else []) + [("num", u)])])

        def pe_mheads(pe):
            for h in range(4):
                mh_dve.wait(pe, "wk", h)
                if h:
                    mh_act.wait(pe, "cs", h - 1)
                for n, (t, r0, r1, off) in enumerate(segs(h)):
                    w = WK(h)[:, off:off + r1 - r0]
                    pe.matmul(PB[7][r0:r1, 256 * n:256 * n + DH], w, VTV[:, 0, DH * h:DH * (h + 1)], start=True, stop=True,
                              skip_group_check=True)
                    ins = pe.matmul(PB[7][r0:r1, 256 * n + DH:256 * n + 193], w, ones[:, 0:1], start=True, stop=True,
                                    skip_group_check=True)
                mh_pe.inc(ins, "cs", h)
            mh_act.wait(pe, "cs", 3)
            for u, (h, c) in enumerate(units):
                if u:
                    mh_dve.wait(pe, "p", u - 1)
                sg = segs(h)
                for n, (t, r0, r1, off) in enumerate(sg):
                    ins = pe.matmul(PB[5][:, 0:P], BIG[r0:r1, KT + t, c * P:(c + 1) * P], BIG[r0:r1, QT + t, c * P:(c + 1) * P],
                                    start=n == 0, stop=n == 1)
                mh_pe.inc(ins, "s", u)
                if c:
                    if u >= 2:
                        mh_dve.wait(pe, "int", u - 2)
                    for n, (t, r0, r1, off) in enumerate(sg):
                        ins = pe.matmul(PB[7][:, 0:193], BIG[r0:r1, QT + t, P:T], CS[r0:r1, t, :], start=n == 0, stop=n == 1)
                    mh_pe.inc(ins, "int", u)
                mh_dve.wait(pe, "p", u)
                if u:
                    mh_dve.wait(pe, "num", u - 1)
                pe.matmul(PB[6][:, 0:DH], PT_(u), VTV[:, c, DH * h:DH * (h + 1)], start=True, stop=True, skip_group_check=True)
                mh_pe.inc(pe.matmul(PB[6][:, DH:193], PT_(u), ones[:, 0:1], start=True, stop=True, skip_group_check=True),
                          "num", u)

        def act_mheads(act):
            for h in range(4):
                mh_pe.wait(act, "cs", h)
                for n, (t, r0, r1, off) in enumerate(segs(h)):
                    ins = nc.scalar.activation(CS[r0:r1, t, :], PB[7][r0:r1, 256 * n:256 * n + 193], ACT.Copy)
                mh_act.inc(ins, "cs", h)
            for u in range(8):
                mh_dve.wait(act, "ag", u)
                mh_act.inc(nc.scalar.activation(MV_[:, 1:2], MV_[:, 1:2], ACT.Sqrt, bias=EPSLN), "std", u)

        def dve_mheads(dve):
            v, st = nc.vector, mh_dve
            for h in range(4):
                if h >= 2:
                    mh_pe.wait(dve, "cs", h - 2)
                st.inc(v.tensor_scalar(WK(h), KTV[:, DH * h:DH * (h + 1)], QC[:, 4, h:h + 1], None, ALU.mult), "wk", h)
            for u, (h, c) in enumerate(units):
                mh_pe.wait(dve, "s", u)
                if u >= 2:
                    mh_pe.wait(dve, "num", u - 2)
                st.inc(v.tensor_tensor(PT_(u), BIG[:, EX + h, c * P:(c + 1) * P], PB[5][:, 0:P], ALU.mult), "p", u)
                if c:
                    mh_pe.wait(dve, "int", u)
                    st.inc(v.tensor_scalar(INT, PB[7][:, 0:193], QC[:, 5, h:h + 1], None, ALU.mult), "int", u)
                    st.wait(dve, "int", u)
                    mh_pe.wait(dve, "num", u)
                    st.inc(v.tensor_tensor(NUM, PB[6][:, 0:193], INT, ALU.add), "num", u)
                else:
                    mh_pe.wait(dve, "num", u)
                    st.inc(v.tensor_copy(NUM, PB[6][:, 0:193]), "num", u)
                st.wait(dve, "num", u)
                st.inc(v.scalar_tensor_tensor(DEN, NUM[:, 192:193], -1.0, NUM[:, 192:193], ALU.mult, ALU.max), "abs", u)
                st.wait(dve, "abs", u)
                st.inc(v.tensor_scalar(DEN, DEN, QC[:, 2 + c, h:h + 1], None, ALU.max), "den", u)
                st.wait(dve, "den", u)
                st.inc(v.reciprocal(DEN, DEN), "rden", u)
                st.wait(dve, "rden", u)
                hn = HNV[:, c, DH * h:DH * (h + 1)]
                st.inc(v.scalar_tensor_tensor(hn, NUM[:, 0:DH], DEN, SOV[:, c, DH * h:DH * (h + 1)], ALU.mult, ALU.mult), "h", u)
                st.wait(dve, "h", u)
                st.inc(v.bn_stats(ST, hn), "st", u)
                st.wait(dve, "st", u)
                st.inc(v.bn_aggr(MV_, ST), "ag", u)
                mh_act.wait(dve, "std", u)
                st.inc(v.reciprocal(MV_[:, 1:2], MV_[:, 1:2]), "rs", u)
                st.wait(dve, "rs", u)
                st.inc(v.tensor_scalar(hn, hn, MV_[:, 0:1], MV_[:, 1:2], ALU.subtract, ALU.mult), "hn", u)

        mf_act = steps("mf_act", [("z", i) for i in range(6)])
        mf_dve = steps("mf_dve", [("z", i) for i in range(6)] + [("y", i) for i in range(6)])
        mf_pe = steps("mf_pe", [("t", i) for i in range(6)])

        def act_mfinish(act):
            for i in range(6):
                mf_act.inc(nc.scalar.activation(tile(QT + i), tile(Z + i), ACT.Sigmoid), "z", i)
            for i in range(6):
                mf_dve.wait(act, "y", i)
                act_split(act, "ml", i, tile(Z + i), XS[:, 4 + i, 0, T:2 * T])

        def dve_mfinish(dve):
            for i in range(6):
                mf_act.wait(dve, "z", i)
                mf_dve.inc(nc.vector.tensor_tensor(tile(Z + i), tile(Z + i), tile(QT + i), ALU.mult), "z", i)
            for i in range(6):
                mf_pe.wait(dve, "t", i)
                mf_dve.wait(dve, "z", i)
                mf_dve.inc(nc.vector.scalar_tensor_tensor(tile(Z + i), PB[5 + i % 2][:, 0:T], V["ml_g"][:, i:i + 1],
                                                          tile(Z + i), ALU.mult, ALU.mult), "y", i)
            for i in range(6):
                dve_split(dve, "ml", i, tile(Z + i), XS[:, 4 + i, 1, T:2 * T], XS[:, 4 + i, 0, T:2 * T])

        def pe_mfinish(pe):
            for i in range(6):
                if i >= 2:
                    mf_dve.wait(pe, "y", i - 2)
                for c in range(2):
                    ins = pe.transpose(PB[5 + i % 2][:, c * P:(c + 1) * P], HNV[:, c, i * P:(i + 1) * P], ident[:, :])
                mf_pe.inc(ins, "t", i)

        def slopes(n):
            pow2 = lambda m: [2.0 ** (-8.0 / m * (i + 1)) for i in range(m)]
            c = 2 ** int(np.floor(np.log2(n)))
            return pow2(c) + pow2(2 * c)[0::2][:n - c]

        DIST = BIG[:, 64:66, :]
        dist_in = sem("distances_in")

        class Attn:
            def __init__(self, name, heads, q, k, v, biased, outs, gates):
                self.heads, self.q, self.k, self.v, self.biased, self.outs, self.gates = heads, q, k, v, biased, outs, gates
                self.name = name
                self.pe = steps(name + "_pe", [("v", h) for h in range(heads)] + [("s", 0)] +
                                [x for h in range(heads) for x in ([("s", h + 1)] if h + 1 < heads else []) + [("t", h), ("o", h)]])
                self.act = steps(name + "_act", ([("z", h) for h in range(heads)] if gates else []) +
                                 [("v", h) for h in range(heads)] +
                                 [x for h in range(heads) for x in [("e", h, 0), ("e", h, 1), ("pt", h)]])
                self.dve = steps(name + "_dve", ([("z", h) for h in range(heads)] if gates else []) +
                                 [x for h in range(heads) for x in ([("l", h)] if biased else []) +
                                  [("mx", h), ("nm", h), ("rs", h), ("nr", h, 0), ("nr", h, 1), ("o", h)]])

            def L(self, h):
                return BIG[:, 66 + 2 * (h % 2):68 + 2 * (h % 2), :]

            def PT(self, h):
                return BIG[:, 70 + 2 * (h % 2):72 + 2 * (h % 2), :]

        scale_o = float(P) ** -0.5
        mo_att = Attn("moba", 6, MQ, MK, MV, True, MZ, True)
        xa_att = Attn("cross", 4, 40, XAK, XAV, False, 44, False)
        AST = small[:, 46:56]

        def pe_attn(pe, A):
            for h in range(A.heads):
                if h >= 2:
                    A.act.wait(pe, "v", h - 2)
                for kt in range(2):
                    ins = pe.transpose(PB[6 + h % 2][:, kt * P:(kt + 1) * P], tile(A.v + h)[:, kt * P:(kt + 1) * P], ident[:, :])
                A.pe.inc(ins, "v", h)

            def scores(h):
                if h:
                    A.act.wait(pe, "e", h - 1, 1)
                for qt in range(2):
                    ins = pe.matmul(PB[5][:, qt * T:(qt + 1) * T], tile(A.q + h)[:, qt * P:(qt + 1) * P], tile(A.k + h),
                                    start=True, stop=True, skip_group_check=True)
                A.pe.inc(ins, "s", h)
            scores(0)
            A.act.wait(pe, "v", A.heads - 1)
            for h in range(A.heads):
                if h + 1 < A.heads:
                    scores(h + 1)
                A.dve.wait(pe, "nr", h, 1)
                if h:
                    A.act.wait(pe, "pt", h - 1)
                for kt in range(2):
                    for qt in range(2):
                        ins = pe.transpose(PB[6][:, kt * T + qt * P:kt * T + (qt + 1) * P],
                                           A.L(h)[:, qt, kt * P:(kt + 1) * P], ident[:, :])
                A.pe.inc(ins, "t", h)
                A.act.wait(pe, "pt", h)
                if h:
                    A.dve.wait(pe, "o", h - 1)
                for kt in range(2):
                    ins = pe.matmul(PB[7][:, 0:T], tile(A.v + h)[:, kt * P:(kt + 1) * P], A.PT(h)[:, kt, :],
                                    start=kt == 0, stop=kt == 1)
                A.pe.inc(ins, "o", h)

        def act_attn(act, A):
            s = nc.scalar.activation
            if A.gates:
                for h in range(A.heads):
                    A.act.inc(s(tile(16 + h), tile(A.outs + h), ACT.Sigmoid), "z", h)
            for h in range(A.heads):
                A.pe.wait(act, "v", h)
                A.act.inc(s(tile(A.v + h), PB[6 + h % 2][:, 0:T], ACT.Copy), "v", h)
            for h in range(A.heads):
                m = AST[:, 4 * (h % 2):4 * (h % 2) + 4]
                A.dve.wait(act, "nm", h)
                for qt in range(2):
                    src = A.L(h)[:, qt, :] if A.biased else PB[5][:, qt * T:(qt + 1) * T]
                    A.act.inc(s(A.L(h)[:, qt, :], src, ACT.Exp, bias=m[:, qt:qt + 1], scale=scale_o,
                                accum_out=m[:, 2 + qt:3 + qt]), "e", h, qt)
                A.pe.wait(act, "t", h)
                if h >= 2:
                    A.pe.wait(act, "o", h - 2)
                A.act.inc(s(A.PT(h).rearrange("p a t -> p (a t)"), PB[6][:, :], ACT.Copy), "pt", h)
            off = 10 if A.gates else 0
            for h in range(A.heads):
                A.dve.wait(act, "o", h)
                act_split(act, None, h, tile(A.outs + h), XS[:, off + h, 0, T:2 * T])

        def dve_attn(dve, A):
            v, st = nc.vector, A.dve
            sl = slopes(A.heads)
            if A.gates:
                for h in range(A.heads):
                    A.act.wait(dve, "z", h)
                    st.inc(v.tensor_tensor(tile(A.outs + h), tile(A.outs + h), tile(16 + h), ALU.mult), "z", h)
            if A.biased:
                dve.wait_ge(dist_in, 16)
            for h in range(A.heads):
                m = AST[:, 4 * (h % 2):4 * (h % 2) + 4]
                A.pe.wait(dve, "s", h)
                src = PB[5][:, :].rearrange("p (q t) -> p q t", q=2)
                if A.biased:
                    if h >= 2:
                        A.pe.wait(dve, "t", h - 2)
                    st.inc(v.scalar_tensor_tensor(A.L(h), DIST, sl[h] / scale_o, src, ALU.mult, ALU.add), "l", h)
                    st.wait(dve, "l", h)
                    src = A.L(h)
                st.inc(v.tensor_reduce(m[:, 0:2], src, AX.X, ALU.max), "mx", h)
                st.wait(dve, "mx", h)
                if not A.biased and h >= 2:
                    A.pe.wait(dve, "t", h - 2)
                st.inc(v.tensor_scalar(m[:, 0:2], m[:, 0:2], -scale_o, None, ALU.mult), "nm", h)
                A.act.wait(dve, "e", h, 1)
                st.inc(v.reciprocal(m[:, 2:4], m[:, 2:4]), "rs", h)
                st.wait(dve, "rs", h)
                for qt in range(2):
                    st.inc(v.tensor_scalar(A.L(h)[:, qt, :], A.L(h)[:, qt, :], m[:, 2 + qt:3 + qt], None, ALU.mult), "nr", h, qt)
                A.pe.wait(dve, "o", h)
                if A.gates:
                    st.inc(v.tensor_tensor(tile(A.outs + h), PB[7][:, 0:T], tile(A.outs + h), ALU.mult), "o", h)
                else:
                    st.inc(v.tensor_copy(tile(A.outs + h), PB[7][:, 0:T]), "o", h)
            off = 10 if A.gates else 0
            for h in range(A.heads):
                dve_split(dve, "mo" if A.gates else "xo", h, tile(A.outs + h), XS[:, off + h, 1, T:2 * T],
                          XS[:, off + h, 0, T:2 * T])

        ADV = AD[:, :].rearrange("p (f v) -> p f v", v=2)
        md = sem("modulation_step")
        mdc = [0]

        def dve_mods(dve, l):
            v = nc.vector
            for w in range(2):
                v.tensor_tensor(MODS[:, 2 + w, :], ADV[:, 48 * l:48 * l + 16, w], V[f"ada_b{l}"][:, 0:16], ALU.add).then_inc(md, 1)
                v.tensor_tensor(MODS[:, w, :], ADV[:, 48 * l + 16:48 * l + 32, w], V[f"ada_b{l}"][:, 16:32], ALU.add).then_inc(md, 1)
                mdc[0] += 2
                dve.wait_ge(md, mdc[0])
                v.scalar_tensor_tensor(MODS[:, w, :], MODS[:, w, :], 1.0, V[f"pre{l}"], ALU.add, ALU.mult).then_inc(md, 1)
                mdc[0] += 1

        def dve_gates(dve, l):
            v = nc.vector
            for w in range(2):
                v.tensor_tensor(MODS[:, 4 + w, :], ADV[:, 48 * l + 32:48 * l + 48, w], V[f"ada_b{l}"][:, 32:48], ALU.add).then_inc(md, 1)
                mdc[0] += 1
                dve.wait_ge(md, mdc[0])
                v.tensor_tensor(MODS[:, 4 + w, :], MODS[:, 4 + w, :], V[f"post{l}"], ALU.mult).then_inc(md, 1)
                mdc[0] += 1

        flat = BIG[:, :, :].rearrange("p a t -> p (a t)")
        PADW = T + 16
        UPAD = flat[:, 64 * T:64 * T + 4 * 2 * PADW].rearrange("p (n s t) -> p n s t", n=4, s=2)
        p0 = 64 * T + 8 * PADW
        INV = flat[:, p0:p0 + T]
        TA = [flat[:, p0 + T + m * 2 * PADW:p0 + T + (m + 1) * 2 * PADW].rearrange("p (s t) -> p s t", s=2) for m in range(2)]
        GT = BIG[:, 64:72, :].rearrange("p (n a) t -> p n (a t)", a=2)
        inv_in, pooled, pool_link, pads = sem("inverse_counts_in"), sem("pooled"), sem("pool_link"), sem("pads_clear")
        plc = [0]

        def gp_pool(gp, g):
            w = 2 ** (g + 1)
            left = w // 2
            if g == 0:
                gp.wait_ge(ends["dve"], POOL_STAGE)
                gp.wait_ge(ends["act"], POOL_STAGE)
                gp.wait_ge(ends["pe"], POOL_STAGE)
                nc.gpsimd.memset(UPAD[:, :, :, 0:8], 0.0).then_inc(pads, 1)
                nc.gpsimd.memset(UPAD[:, :, :, 8 + T:PADW], 0.0).then_inc(pads, 1)
                gp.wait_ge(pads, 2)
            if g:
                gp.wait_ge(pooled, 4 * g)
            gp.dma_start(INV, a["inv_counts"][g:g + 1, :].to_broadcast([P, T])).then_inc(inv_in, 16)
            gp.wait_ge(inv_in, 16 * (g + 1))
            gp.wait_ge(dve_freed, pu[g].free0 + 4)

            def link(ins):
                plc[0] += 1
                ins.then_inc(pool_link, 1)
                gp.wait_ge(pool_link, plc[0])
            for n in range(4):
                src, width, span = UPAD[:, n], PADW, 1
                m = 0
                while span < w:
                    width -= span
                    link(nc.gpsimd.tensor_tensor(TA[m][:, :, 0:width], src[:, :, 0:width], src[:, :, span:span + width], ALU.add))
                    src, m, span = TA[m], 1 - m, 2 * span
                link(nc.gpsimd.tensor_tensor(TA[m][:, :, 0:T], src[:, :, 8 - left:8 - left + T],
                                             INV.unsqueeze(1).to_broadcast([P, 2, T]), ALU.mult))
                u = UPAD[:, n, :, 8:8 + T]
                nc.gpsimd.tensor_tensor(u, TA[m][:, :, 0:T], u, ALU.subtract).then_inc(pooled, 1)
                gp.wait_ge(pooled, 4 * g + n + 1)

        def act_pool(act, g):
            for n in range(4):
                act.wait_ge(pooled, 4 * g + n + 1)
                act_split(act, None, n, UPAD[:, n, :, 8:8 + T], PS[:, n, 0, :].rearrange("p (s t) -> p s t", s=2))

        def dve_pool(dve, g):
            for n in range(4):
                s2 = lambda part: PS[:, n, part, :].rearrange("p (s t) -> p s t", s=2)
                dve_split(dve, f"pp{g}", n, UPAD[:, n, :, 8:8 + T], s2(1), s2(0))

        def act_ysplit(act):
            for k in range(16):
                act_split(act, "py", k, BIG[:, YT0 + 2 * k:YT0 + 2 * k + 2, :].rearrange("p a t -> p (a t)"), XS[:, k, 0, :])

        def dve_ysplit(dve):
            for k in range(16):
                dve_split(dve, "py", k, BIG[:, YT0 + 2 * k:YT0 + 2 * k + 2, :].rearrange("p a t -> p (a t)"),
                          XS[:, k, 1, :], XS[:, k, 0, :])

        COS, SIN = tile(60), tile(61)
        ROT = BIG[:, 64, 0:P]
        RTMP = tile(62)
        KRT = BIG[:, 76:78, :].rearrange("p a t -> p (a t)")
        rope_in = sem("rope_in")
        VA = [BIG[:, 48 + 2 * h:50 + 2 * h, :].rearrange("p a (b d) -> p (a b) d", b=2) for h in range(2)]
        PP = [BIG[:, 52 + 2 * h:54 + 2 * h, :].rearrange("p a t -> p (a t)") for h in range(2)]
        PPT = [BIG[:, 56 + 2 * h:58 + 2 * h, :].rearrange("p a t -> p (a t)") for h in range(2)]
        mla_scale = float(192) ** -0.5
        ml_units = [(j, u) for j in range(8) for u in range(4)]
        la_pe = steps("latent_pe", [("kr",)] + [x for j in range(8) for x in
                      [("rot", j), ("v", j, 0), ("v", j, 1)] + [y for u in range(4) for y in [("s", j, u), ("t", j, u), ("o", j, u)]]])
        la_act = steps("latent_act", [("g", k) for k in range(4)] + [x for j in range(8) for x in
                       [("v", j, 0), ("v", j, 1)] + [y for u in range(4) for y in [("e", j, u), ("pt", j, u), ("hi", j, u)]]])
        la_dve = steps("latent_dve", [("kr1",), ("kr2",), ("kr3",)] + [("g", k) for k in range(4)] + [x for j in range(8) for x in
                       [("r1", j), ("r2", j), ("r3", j)] + [y for u in range(4) for y in
                       [("mx", j, u), ("nm", j, u), ("rs", j, u), ("nr", j, u), ("o", j, u), ("lo", j, u)]]])

        def dve_rope(dve, x, names, key):
            v, st = nc.vector, la_dve
            st.inc(v.tensor_tensor(RTMP, PB[5][:, 0:T], SIN, ALU.mult), names[0], *key)
            st.inc(v.tensor_tensor(x, x, COS, ALU.mult), names[1], *key)
            st.wait(dve, names[1], *key)
            st.inc(v.tensor_tensor(x, x, RTMP, ALU.add), names[2], *key)

        def act_latent0(act):
            for k in range(4):
                la_act.inc(nc.scalar.activation(BIG[:, 32 + 4 * k:36 + 4 * k, :], BIG[:, 16 + 4 * k:20 + 4 * k, :], ACT.Sigmoid), "g", k)

        def pe_latent0(pe):
            pe.wait_ge(rope_in, 48)
            la_pe.inc(pe.matmul(PB[5][:, 0:T], ROT, KRT[:, 0:T], start=True, stop=True), "kr")

        def dve_latent0(dve):
            dve.wait_ge(rope_in, 48)
            la_pe.wait(dve, "kr")
            dve_rope(dve, KRT[:, 0:T], ("kr1", "kr2", "kr3"), ())
            for k in range(4):
                la_act.wait(dve, "g", k)
                la_dve.inc(nc.vector.tensor_tensor(BIG[:, 16 + 4 * k:20 + 4 * k, :], BIG[:, 16 + 4 * k:20 + 4 * k, :],
                                                   BIG[:, 32 + 4 * k:36 + 4 * k, :], ALU.mult), "g", k)

        def pe_latent(pe, j):
            la_pe.inc(pe.matmul(PB[5][:, 0:T], ROT, tile(46), start=True, stop=True), "rot", j)
            for h in range(2):
                vt = BIG[:, 34 + 4 * h:36 + 4 * h, :].rearrange("p a t -> p (a t)")
                for kt in range(4):
                    ins = pe.transpose(PB[6 + h][:, kt * P:(kt + 1) * P], vt[:, kt * P:(kt + 1) * P], ident[:, :])
                la_pe.inc(ins, "v", j, h)
            la_dve.wait(pe, "r3", j)
            la_act.wait(pe, "v", j, 1)
            for u in range(4):
                h, qt = u // 2, u % 2
                bank = PB[5 + u % 2]
                kn = BIG[:, 32 + 4 * h:34 + 4 * h, :].rearrange("p a t -> p (a t)")
                if u >= 2:
                    la_act.wait(pe, "e", j, u - 2)
                r = slice(64 * h, 64 * h + 64)
                pe.matmul(bank[:, :], tile(44 + h)[:, qt * P:(qt + 1) * P], kn, start=True, stop=False)
                la_pe.inc(pe.matmul(bank[:, :], BIG[r, 46, qt * P:(qt + 1) * P], KRT[r, :], start=False, stop=True), "s", j, u)
                la_dve.wait(pe, "nr", j, u)
                if u:
                    la_act.wait(pe, "pt", j, u - 1)
                for kt in range(4):
                    ins = pe.transpose(PB[7][:, kt * P:(kt + 1) * P], PP[u % 2][:, kt * P:(kt + 1) * P], ident[:, :])
                la_pe.inc(ins, "t", j, u)
                la_act.wait(pe, "pt", j, u)
                if u:
                    la_dve.wait(pe, "o", j, u - 1)
                for kt in range(4):
                    ins = pe.matmul(PB[4][:, 0:P], VA[h][:, kt, :], PPT[u % 2][:, kt * P:(kt + 1) * P], start=kt == 0, stop=kt == 3)
                la_pe.inc(ins, "o", j, u)

        def act_latent(act, j):
            s = nc.scalar.activation
            for h in range(2):
                la_pe.wait(act, "v", j, h)
                la_act.inc(s(VA[h].rearrange("p k d -> p (k d)"), PB[6 + h][:, :], ACT.Copy), "v", j, h)
            for u in range(4):
                h, qt = u // 2, u % 2
                m = AST[:, 2 * (u % 2):2 * (u % 2) + 2]
                la_dve.wait(act, "nm", j, u)
                la_act.inc(s(PP[u % 2], PB[5 + u % 2][:, :], ACT.Exp, bias=m[:, 0:1], scale=mla_scale, accum_out=m[:, 1:2]), "e", j, u)
                la_pe.wait(act, "t", j, u)
                la_act.inc(s(PPT[u % 2], PB[7][:, :], ACT.Copy), "pt", j, u)
                la_dve.wait(act, "o", j, u)
                la_act.inc(s(XS[:, 2 * j + h, 0, qt * P:(qt + 1) * P], BIG[:, 65 + h, qt * P:(qt + 1) * P], ACT.Copy), "hi", j, u)

        def dve_latent(dve, j):
            v, st = nc.vector, la_dve
            la_pe.wait(dve, "rot", j)
            dve_rope(dve, tile(46), ("r1", "r2", "r3"), (j,))
            for u in range(4):
                h, qt = u // 2, u % 2
                m = AST[:, 2 * (u % 2):2 * (u % 2) + 2]
                la_pe.wait(dve, "s", j, u)
                st.inc(v.tensor_reduce(m[:, 0:1], PB[5 + u % 2][:, :], AX.X, ALU.max), "mx", j, u)
                st.wait(dve, "mx", j, u)
                st.inc(v.tensor_scalar(m[:, 0:1], m[:, 0:1], -mla_scale, None, ALU.mult), "nm", j, u)
                la_act.wait(dve, "e", j, u)
                st.inc(v.reciprocal(m[:, 1:2], m[:, 1:2]), "rs", j, u)
                st.wait(dve, "rs", j, u)
                st.inc(v.tensor_scalar(PP[u % 2], PP[u % 2], m[:, 1:2], None, ALU.mult), "nr", j, u)
                la_pe.wait(dve, "o", j, u)
                o = BIG[:, 65 + h, qt * P:(qt + 1) * P]
                st.inc(v.tensor_tensor(o, PB[4][:, 0:P], BIG[:, 16 + 2 * j + h, qt * P:(qt + 1) * P], ALU.mult), "o", j, u)
                la_act.wait(dve, "hi", j, u)
                st.inc(v.tensor_sub(XS[:, 2 * j + h, 1, qt * P:(qt + 1) * P], o,
                                    XS[:, 2 * j + h, 0, qt * P:(qt + 1) * P].bitcast(F32)), "lo", j, u)

        out_t, out_c = sem("out_turned"), sem("out_copied")
        OUTT = BIG[:, 40:56, :].rearrange("p (a k) t -> p a (k t)", a=2)

        def pe_out(pe):
            for n in range(8):
                h, k4 = n // 4, n % 4
                if n >= 2:
                    pe.wait_ge(out_c, n - 1)
                for m in range(4):
                    ins = pe.transpose(PB[5 + n % 2][:, m * P:(m + 1) * P], BIG[:, 4 * k4 + m, h * P:(h + 1) * P], ident[:, :])
                ins.then_inc(out_t, 1)

        def act_out(act):
            for n in range(8):
                h, k4 = n // 4, n % 4
                act.wait_ge(out_t, n + 1)
                nc.scalar.activation(OUTT[:, h, 512 * k4:512 * (k4 + 1)], PB[5 + n % 2][:, :], ACT.Copy).then_inc(out_c, 1)
            act.wait_ge(out_c, 8)
            act.dma_start(out.rearrange("b (a p) f -> p (b a) f", p=P), OUTT).then_inc(out_done, 16)
            act.wait_ge(out_done, 16)

        STAGES = ["in_mem", "kv", "in_x", "win_a", "win_b", "lru", "mgates", "mproj", "mheads", "mfinish", "win_c", "moba", "mixo",
                  "norm_xa", "xq", "cross", "xo", "final", "pre0", "pu0", "pool0", "pg0", "pu1", "pool1", "pg1", "pu2", "pool2",
                  "pg2", "pu3", "pool3", "pg3", "pgate", "ysplit", "po", "post0", "pre1", "ckv", "kr", "cq", "mg", "latnorm",
                  "latent0"] + [x for j in range(8) for x in (f"uq{j}", f"ukv{j}", f"latent{j + 1}")] + ["mo", "post1", "out"]
        POOL_STAGE = STAGES.index("pre0") + 1
        by_name = {p.name: p for p in products}

        def run(eng, me, stage_fn, product_fn):
            for name in STAGES:
                if DEBUG_STOP == name:
                    name = "dump"
                if name in by_name:
                    product_fn(eng, by_name[name])
                elif name in stage_fn:
                    stage_fn[name](eng)
                if name == "dump":
                    return
                if name != "out":
                    stage_end(eng, me)

        @block.sync
        def _(sp):
            sp_turn(sp, 0, a["mem"][0])
            sp_product(sp, kv)
            sp.wait_ge(ends["pe"], 1)
            sp_turn(sp, 1, a["x"][0])
            for p in products[1:3]:
                sp_product(sp, p)
            sp.wait_ge(ends["act"], 2)
            sp.dma_start(LW[:, 0:4], a["lru_wa"][0].rearrange("g i o -> i g o")).then_inc(lw_in, 16)
            sp.dma_start(LW[:, 4:8], a["lru_wx"][0].rearrange("g i o -> i g o")).then_inc(lw_in, 16)
            if DEBUG_STOP:
                lim = STAGES.index(DEBUG_STOP)
            else:
                lim = len(STAGES)
            for p in products[3:]:
                if STAGES.index(p.name) >= lim:
                    break
                if p is mixo:
                    sp.wait_ge(ends["dve"], STAGES.index("mfinish") + 1)
                    sp.dma_start(DIST, a["dist"].rearrange("(q p) k -> p q k", p=P)).then_inc(dist_in, 16)
                if p is pu[0]:
                    sp.wait_ge(ends["dve"], STAGES.index("cross") + 1)
                    sp.wait_ge(ends["act"], STAGES.index("final"))
                    sp_turn(sp, 2, a["ctx_2"][0])
                if p is uq[0]:
                    sp.wait_ge(ends["act"], STAGES.index("latnorm") + 1)
                    sp.wait_ge(ends["dve"], STAGES.index("latnorm") + 1)
                    sp.dma_start(COS, a["cos"]).then_inc(rope_in, 16)
                    sp.dma_start(SIN, a["sin"]).then_inc(rope_in, 16)
                    sp.dma_start(ROT, a["rot"]).then_inc(rope_in, 16)
                sp_product(sp, p)

        @block.gpsimd
        def _(gp):
            if not DEBUG_STOP or STAGES.index(DEBUG_STOP) > STAGES.index("pool3"):
                for g in range(4):
                    gp_pool(gp, g)

        @block.scalar
        def _(act):
            for name, st in all_steps:
                if name.endswith("_act"):
                    st.chain = act
            def in_mem(act):
                act_setup(act)
                setup.wait(act, "epsln")
                act_turn(act, 0)
                act_norm(act, norms["mem"])

            def in_x(act):
                act_turn(act, 1)
                act_norm(act, norms["mix"])

            def pre0(act):
                act_turn(act, 2)
                act_norm(act, norms["pre0"])
                act_norm(act, norms["pre0c"])

            def lru(act):
                act_lru(act)
                for b in range(4):
                    lru_dve.wait(act, "y", b)
                    act_split(act, "lru", b, tile(LX + b), XS[:, b, 0, T:2 * T])
            both = lambda *names: (lambda act: [act_norm(act, norms[n]) for n in names])
            stages_ = dict(in_mem=in_mem, in_x=in_x, lru=lru, mgates=act_mgates, mproj=act_mproj, mheads=act_mheads,
                           mfinish=act_mfinish, moba=lambda e: act_attn(e, mo_att), norm_xa=both("xa"),
                           cross=lambda e: act_attn(e, xa_att), final=both("final"), pre0=pre0, ysplit=act_ysplit,
                           post0=both("post0", "post0c"), pre1=both("pre1", "pre1c"), latnorm=both("ckv", "ckvc", "cq"),
                           latent0=act_latent0, post1=both("post1"), out=act_out)
            for g in range(4):
                stages_[f"pool{g}"] = lambda e, g=g: act_pool(e, g)
            for j in range(8):
                stages_[f"latent{j + 1}"] = lambda e, j=j: act_latent(e, j)
            run(act, "act", stages_, act_product)

        @block.vector
        def _(dve):
            for name, st in all_steps:
                if name.endswith("_dve"):
                    st.chain = dve
            def in_mem(dve):
                dve_setup(dve)
                dve_norm(dve, norms["mem"])

            def pre0(dve):
                dve_mods(dve, 0)
                dve_norm(dve, norms["pre0"])
                dve_norm(dve, norms["pre0c"])

            def post0(dve):
                dve_gates(dve, 0)
                dve_norm(dve, norms["post0"])
                dve_norm(dve, norms["post0c"])

            def pre1(dve):
                dve_mods(dve, 1)
                dve_norm(dve, norms["pre1"])
                dve_norm(dve, norms["pre1c"])

            def post1(dve):
                dve_gates(dve, 1)
                dve_norm(dve, norms["post1"])

            def lru(dve):
                dve_lru(dve)
                for b in range(4):
                    dve_split(dve, "lru", b, tile(LX + b), XS[:, b, 1, T:2 * T], XS[:, b, 0, T:2 * T])
            both = lambda *names: (lambda dve: [dve_norm(dve, norms[n]) for n in names])
            stages_ = dict(in_mem=in_mem, in_x=both("mix"), lru=lru, mgates=dve_mgates, mproj=dve_mproj, mheads=dve_mheads,
                           mfinish=dve_mfinish, moba=lambda e: dve_attn(e, mo_att), norm_xa=both("xa"),
                           cross=lambda e: dve_attn(e, xa_att), final=both("final"), pre0=pre0, ysplit=dve_ysplit,
                           post0=post0, pre1=pre1, latnorm=both("ckv", "ckvc", "cq"), latent0=dve_latent0, post1=post1)
            for g in range(4):
                stages_[f"pool{g}"] = lambda e, g=g: dve_pool(e, g)
            for j in range(8):
                stages_[f"latent{j + 1}"] = lambda e, j=j: dve_latent(e, j)
            run(dve, "dve", stages_, dve_product)

        @block.tensor
        def _(pe):
            def turn_norm(q, *names):
                def go(pe):
                    if q is not None:
                        pe_turn(pe, q)
                    for n in names:
                        pe_norm(pe, norms[n])
                return go

            def in_mem(pe):
                setup.wait(pe, "ones")
                pe_setup(pe)
                pe.wait_ge(pv_ready, 1)
                turn_norm(0, "mem")(pe)

            def lru(pe):
                pe.wait_ge(lw_in, 32)
                pe_lru(pe)
            stages_ = dict(in_mem=in_mem, in_x=turn_norm(1, "mix"), lru=lru, mgates=pe_mgates, mproj=pe_mproj, mheads=pe_mheads,
                           mfinish=pe_mfinish, moba=lambda e: pe_attn(e, mo_att), norm_xa=turn_norm(None, "xa"),
                           cross=lambda e: pe_attn(e, xa_att), final=turn_norm(None, "final"), pre0=turn_norm(2, "pre0", "pre0c"),
                           post0=turn_norm(None, "post0", "post0c"), pre1=turn_norm(None, "pre1", "pre1c"),
                           latnorm=turn_norm(None, "ckv", "ckvc", "cq"), latent0=pe_latent0, post1=turn_norm(None, "post1"),
                           out=pe_out)
            for j in range(8):
                stages_[f"latent{j + 1}"] = lambda e, j=j: pe_latent(e, j)
            run(pe, "pe", stages_, pe_product)


def constants():
    p = np.arange(P)
    t = np.arange(T)
    dist = t[None, :] - t[:, None]
    freqs = 10000.0 ** (-np.arange(16, dtype=np.float32) / np.float32(16))
    pos = np.stack([t // 64, t % 64]).astype(np.float32)
    axis, part, f = (p % 64) // 32, (p % 32) // 16, p % 16
    ang = pos[axis, :] * freqs[f].astype(np.float32)[:, None]
    rot = np.zeros((P, P), np.float32)
    partner = np.where(part == 0, p + 16, p - 16)
    rot[partner, p] = np.where(part == 0, -1.0, 1.0)
    counts = []
    for w in (2, 4, 8, 16):
        left = w // 2
        counts.append(np.minimum(t + w - left, T) - np.maximum(t - left, 0))
    return {
        "ident": np.eye(P, dtype=np.float32),
        "blockmask": (p[:, None] // 4 == p[None, :] // 4).astype(np.float32),
        "mlmask": np.where(p[:, None] <= p[None, :], 0.0, NEG).astype(np.float32),
        "sel": np.kron(np.eye(4, dtype=np.float32), np.ones((1, P), np.float32)),
        "dist": np.where(dist <= 0, dist, -1e33).astype(np.float32),
        "cos": np.cos(ang).astype(np.float32), "sin": np.sin(ang).astype(np.float32), "rot": rot,
        "inv_counts": (1.0 / np.stack(counts)).astype(np.float32),
    }


def kernel(**inputs):
    import concourse.bacc as bacc
    from concourse.bass_utils import run_bass_kernel_spmd

    nc = bacc.Bacc("TRN2", target_bir_lowering=False, num_devices=1, dynamic_dma_scratch_size=1024)
    arrays, args = {}, {}
    for name, value in list(inputs.items()) + list(constants().items()):
        x = np.ascontiguousarray(value)
        arrays["in_" + name] = x
        args[name] = nc.dram_tensor("in_" + name, x.shape, F32, kind="ExternalInput").ap()
    out = nc.dram_tensor("out_0", (1, T, D), F32, kind="ExternalOutput").ap()
    build(nc, args, out)
    result = run_bass_kernel_spmd(nc, [arrays], core_ids=[0])
    return result.results[0]["out_0"]
```

```python
from contextlib import ExitStack

import numpy as np
import concourse.bass as bass
from concourse import mybir

F32 = mybir.dt.float32
F32R = mybir.dt.float32r
ACT = mybir.ActivationFunctionType
ALU = mybir.AluOpType
AX = mybir.AxisListType

P = 128
T = 256
D = 2048
KD = D // P
GW = 512
KC = 4
RMS_EPS = 1e-6
LN_EPS = 1e-5
NEG = -1e30
DEBUG_STOP = None


class Product:

    def __init__(self, name, w, chunks, groups, tiles, seqs, kind, k_groups=1, stride=GW, width=None, pack=None,
                 half=0, src="xs", dest=None, col0=0):
        self.name, self.w = name, w
        self.chunks = chunks
        self.groups = groups
        self.tiles = tiles
        self.seqs = seqs
        self.kind = kind
        self.stride = stride
        self.width = width or tiles * P
        self.pack = pack
        self.half = half
        self.src = src
        self.dest = dest
        self.col0 = col0
        self.primed = 0


def plan(steps):
    chunk = tile = 0
    dve_free = act_free = 0
    bank_last = [None] * 4
    for p in steps:
        p.chunk0, p.tile0 = chunk, tile
        p.first_bank_wait = list(bank_last)
        p.freed = "act" if p.kind == "copy2" else "dve"
        p.free0 = act_free if p.freed == "act" else dve_free
        chunk += p.chunks * p.groups
        tile += (p.tiles - 1) * p.groups
        if p.freed == "act":
            act_free += p.tiles * p.groups
            end, which = act_free, "act"
        else:
            dve_free += p.tiles * p.groups
            end, which = dve_free, "dve"
        for n in range(p.tiles):
            bank_last[n] = (which, end - p.tiles + n + 1)
    return chunk


def vectors(a):
    v = lambda ap: ap.rearrange("(k p) -> k p", p=P)
    m = lambda ap: ap.rearrange("j (k p) -> (j k) p", p=P)
    return [
        ("mem_g", v(a["mem_norm_g"][0]), 16), ("mix_g", v(a["mix_norm_g"][0]), 16),
        ("c", v(a["c_2"][0]), 16), ("c_ctx", v(a["c_ctx_2"]), 16),
        ("lru_conv_w", m(a["lru_conv_w"][0]), 16), ("lru_conv_b", v(a["lru_conv_b"][0]), 4),
        ("lru_ba", v(a["lru_ba"][0]), 4), ("lru_bx", v(a["lru_bx"][0]), 4), ("lru_lambda", v(a["lru_lambda"][0]), 4),
        ("ml_conv_w", m(a["ml_conv_w"][0]), 24), ("ml_conv_b", v(a["ml_conv_b"][0]), 6),
        ("ml_g", v(a["ml_norm_g"][0]), 6), ("xa_g", v(a["xa_norm_g"][0]), 16), ("final_g", v(a["final_norm_g"]), 16),
        ("ada_b0", v(a["ada_b_2"][0]), 48), ("ada_b1", v(a["ada_b_2"][1]), 48),
        ("pre0", v(a["pre_norm_2"][0]), 16), ("pre1", v(a["pre_norm_2"][1]), 16),
        ("post0", v(a["post_norm_2"][0]), 16), ("post1", v(a["post_norm_2"][1]), 16),
        ("pool_b", v(a["pool_b_grp_2"].rearrange("l g c -> l (g c)")[0]), 16),
        ("pool_s", v(a["pool_scale_2"][0]), 16),
        ("q_g", v(a["mla_q_norm_2"][0]), 4), ("kv_g", v(a["mla_kv_norm_2"][0]), 4),
    ]


LX, LZ, U, O, Z, G = 40, 44, 48, 54, 60, 66
XAK, XAV = 32, 36
MQ, MK, MV, MZ = 40, 46, 52, 58
CT0 = 16
YT0 = 32
UC, QT, KT = 16, 22, 67
VT, KTOK, EX, SOT = 40, 73, 28, 48
SQ0, HF0 = 64, 72
NB = 78


class Steps:

    def __init__(self, sem, order):
        self.sem, self.order, self.done = sem, {key: n + 1 for n, key in enumerate(order)}, 0
        self.chain = None

    def inc(self, ins, *key):
        self.done += 1
        assert self.order[key] == self.done, (key, self.order[key], self.done)
        ins.then_inc(self.sem, 1)
        if self.chain:
            self.chain.wait_ge(self.sem, self.done)

    def wait(self, eng, *key):
        eng.wait_ge(self.sem, self.order[key])


def build(nc, a, out):
    w_in, w_out = a["w_in"][0], a["w_out"][0]
    wq, wkv, wo = a["xa_wq"][0], a["xa_wkv"][0], a["xa_wo"][0]
    pw_in, pw_out = a["pool_w_in_2"][0], a["pool_w_out_2"][0]
    mw_in, mw_out, mw_uq, mw_ukv = a["mla_w_in_2"][0], a["mla_w_out_2"][0], a["mla_w_uq_2"][0], a["mla_w_ukv_2"][0]

    kv = Product("kv", wkv, 4, 2, 4, 1, "copy1", half=1, dest=XAK)
    win_a = Product("win_a", w_in, 4, 6, 4, 1, "copy1", dest=LX)
    win_b = Product("win_b", w_in, 4, 1, 3, 1, "copy1", dest=LX + 24, col0=6 * GW)
    win_c = Product("win_c", w_in, 4, 6, 4, 1, "copy1", dest=MQ, col0=3336)
    mixo = Product("mixo", w_out, 4, 4, 4, 1, "add1", half=1, dest=0)
    xq = Product("xq", wq, 4, 1, 4, 1, "copy1", dest=40)
    xo = Product("xo", wo, 1, 4, 4, 1, "add1", half=1, dest=0)
    pu = [Product(f"pu{g}", pw_in, 4, 1, 4, 2, "copy2", dest=("pool_u", g), col0=g * GW) for g in range(4)]
    pg = [Product(f"pg{g}", a["pool_w_grp_2"][0][g], 1, 1, 4, 2, "grp", src="ps", dest=("y", 4 * g)) for g in range(4)]
    pgate = Product("pgate", pw_in, 4, 4, 4, 2, "gate2", dest=("y", 0), col0=D)
    po = Product("po", pw_out, 4, 4, 4, 2, "copy2", dest=("y", 0))
    ckv = Product("ckv", mw_in, 4, 1, 4, 2, "copy2", dest=("y", 0), col0=GW)
    kr = Product("kr", mw_in, 4, 1, 1, 2, "copy2", dest=("kr", 0), col0=2 * GW, width=64, pack="twice")
    cq = Product("cq", mw_in, 4, 1, 4, 1, "copy1", dest=40)
    mg = Product("mg", mw_in, 4, 4, 4, 1, "copy1", dest=16, col0=1088)
    Q_SETS = [[44, 45, 46], [71, 72, 73]]
    KV_SETS = [[32, 34, 36, 38], [40, 67, 42, 69]]
    uq = [Product(f"uq{j}", mw_uq, 1, 1, 3, 1, "copy1", half=1, width=384, pack="heads", col0=384 * j, dest=Q_SETS[j % 2])
          for j in range(8)]
    ukv = [Product(f"ukv{j}", mw_ukv, 1, 1, 4, 2, "copy2", src="ps", col0=GW * j, dest=KV_SETS[j % 2]) for j in range(8)]
    mo = Product("mo", mw_out, 4, 4, 4, 1, "copy1", dest=32)
    POOLS = [3, 2, 1, 0]
    pool_chain = [pu[3], pu[2], pg[3], pu[1], pg[2], pu[0], pg[1], pg[0], pgate, po]
    products = [kv, win_a, win_b, win_c, mixo, xq, xo] + pool_chain + [ckv, kr, cq, mg]
    for j in range(8):
        products += [uq[j], ukv[j]]
    products += [mo]
    plan(products)

    ada = {win_a: 1, win_c: 1, mixo: 1, pgate: 2, po: 2}
    ada.update({p: 2 for p in pu + uq + ukv})
    unit = 0
    for p in products:
        p.ada = ada.get(p, 0)
        p.unit0 = unit
        unit += p.ada * p.chunks * p.groups
    assert unit == 4 * 48

    ctx = ExitStack()
    with ctx:
        def sb(name, shape, dt=F32):
            return ctx.enter_context(nc.sbuf_tensor(name, shape, dt))

        def sem(name):
            return ctx.enter_context(nc.semaphore(name))

        all_steps = []

        def steps(name, order):
            st = Steps(sem(name), order)
            all_steps.append((name, st))
            return st

        BIG = sb("big", [P, NB, T])
        XS = sb("operand", [P, KD, 2, 2 * T], F32R)
        PS = sb("operand_small", [P, KC, 2, 2 * T], F32R)
        RAW = sb("raw", [P, 2, KC, GW])
        HI = sb("w_high", [P, 2, KC, GW], F32R)
        LO = sb("w_low", [P, 2, KC, GW], F32R)
        ARAW = sb("ada_raw", [P, 2, KC, 256])
        ACC = sb("ada_acc", [P, 2, 256])
        AD = sb("ada_out", [P, 48 * 4])
        VEC = vectors(a)
        PV = sb("vectors", [P, 4 * P])
        V, place, at = {}, {}, 0
        for name, _, n in VEC:
            if at % P + n > P:
                at += P - at % P
            V[name], place[name] = PV[:, at:at + n], at
            at += n
        assert at <= 4 * P
        VROW = BIG[:, 32:34, :].rearrange("p a t -> p (a t)")
        MODS = sb("modulations", [P, 10, KD])
        SC = sb("silu_c", [P, 2, KD])
        ident = sb("ident", [P, P])
        blockmask = sb("blockmask", [P, P])
        mlmask = sb("mlmask", [P, P])
        ones = sb("ones", [P, P])
        RST = sb("rstd", [P, T])
        small = sb("small", [P, 64])
        EPS = small[:, 60:61]
        EPSLN = small[:, 61:62]
        PB = [ctx.enter_context(nc.psum_tensor(f"bank{i}", [P, 512], F32)) for i in range(8)]

        raw_ready = [sem("raw_ready0"), sem("raw_ready1")]
        hi_ready, lo_ready, chunk_done, tile_done = sem("hi_ready"), sem("lo_ready"), sem("chunk_done"), sem("tile_done")
        half_moved, dve_freed, act_freed = sem("half_moved"), sem("bank_freed_dve"), sem("bank_freed_act")
        gate_ready, resid = sem("gate_ready"), sem("residual_step")
        ada_loaded = [sem("ada_loaded0"), sem("ada_loaded1")]
        ada_summed, ada_moved = sem("ada_summed"), sem("ada_moved")
        ada_link = sem("ada_link")
        freed = {"dve": dve_freed, "act": act_freed}
        consts_in, vec_in, tok_in, tok_free = sem("consts_in"), sem("vec_in"), [sem(f"tok_in{n}") for n in range(4)], sem("tok_free")
        setup_done, silu_c = sem("setup_done"), sem("silu_c")
        tr_done, tr_free = sem("transposed"), sem("transpose_moved")
        sq_ready, sq_used, std_ready = sem("squares_ready"), sem("squares_summed"), sem("std_ready")
        hf_ready, xh_ready, xs_ready, norm_link = sem("normed"), sem("operand_high"), sem("operand_ready"), sem("norm_link")
        norm_done, out_done = sem("norm_done"), sem("out_done")
        dch, ach = sem("dve_chain"), sem("act_chain")
        S = {}

        def named(*names):
            for n in names:
                S[n] = sem(n)
        tiles = lambda t0, n=1: BIG[:, t0:t0 + n, :]
        tile = lambda t: BIG[:, t, :]

        block = ctx.enter_context(nc.Block())

        def sp_chunk(sp, p, i, j):
            c, w = p.chunk0 + j, p.chunks * i
            if isinstance(i, int):
                c, w = c + w, 0
            slot = c % 2
            if c >= 2 or not isinstance(i, int):
                sp.wait_ge(lo_ready, c + w - 1)
            rows = p.w[j * KC * P:(j + 1) * KC * P, :]
            src = rows.rearrange("(k p) n -> p k n", p=P)[:, :, bass.ds(p.col0 + p.stride * i, p.width)]
            sp.dma_start(RAW[:, slot, :, 0:p.width], src).then_inc(raw_ready[slot], 16)

        def sp_unit(sp, p, i, j, q):
            u0 = p.unit0 + p.ada * j + q
            uw = p.ada * p.chunks * i
            if isinstance(i, int):
                u0, uw = u0 + uw, 0
            part, us = u0 % 4, u0 % 2
            if u0 >= 2 or not isinstance(i, int):
                sp.wait_ge(ada_link, 8 * (u0 + uw - 1))
            b = u0 // 4
            layer, col = b // 24, (b % 24) * 256 + 64 * uw
            src = a["ada_w_2"][layer, part * KC * P:(part + 1) * KC * P, :]
            src = src.rearrange("(k p) n -> p k n", p=P)[:, :, bass.ds(col, 256)]
            sp.dma_start(ARAW[:, us], src).then_inc(ada_loaded[us], 16)

        def sp_group(sp, p, i):
            for j in range(p.chunks):
                sp_chunk(sp, p, i, j)
                for q in range(p.ada):
                    sp_unit(sp, p, i, j, q)

        def packed(p):
            if p.pack == "heads":
                def nope(buf, slot, raw):
                    if raw:
                        return buf[:, slot, :, 0:384].rearrange("p k (a n) -> p k a n", a=2)[:, :, :, 0:P]
                    return buf[:, slot, :, 0:2 * P].rearrange("p k (a n) -> p k a n", a=2)

                def rope(buf, slot, raw):
                    if raw:
                        return buf[:, slot, :, 0:384].rearrange("p k (a n) -> p k a n", a=2)[:, :, :, P:P + 64]
                    return buf[:, slot, :, 2 * P:3 * P].rearrange("p k (a n) -> p k a n", a=2)
                return [nope, rope]
            if p.pack == "twice":
                return [lambda buf, slot, raw, r=r: buf[:, slot, :, 0:64] if raw else buf[:, slot, :, 64 * r:64 * r + 64]
                        for r in range(2)]
            return [lambda buf, slot, raw: buf[:, slot, :, 0:p.width]]

        def act_high(act, p, i, j):
            c, w = p.chunk0 + j, p.chunks * i
            if isinstance(i, int):
                c, w = c + w, 0
            slot = c % 2
            act.wait_ge(raw_ready[slot], 16 * (c // 2 + 1) + 8 * w)
            if c >= 2 or not isinstance(i, int):
                act.wait_ge(chunk_done, c + w - 1)
            for view in packed(p):
                ins = nc.scalar.activation(view(HI, slot, False), view(RAW, slot, True), ACT.Copy)
            ins.then_inc(hi_ready, 1)

        def dve_low(dve, p, i, j):
            c, w = p.chunk0 + j, p.chunks * i
            if isinstance(i, int):
                c, w = c + w, 0
            slot = c % 2
            dve.wait_ge(hi_ready, c + w + 1)
            for view in packed(p):
                ins = nc.vector.tensor_sub(view(LO, slot, False), view(RAW, slot, True), view(HI, slot, False).bitcast(F32))
            ins.then_inc(lo_ready, 1)

        def wait_tile(eng, p, i, n):
            if n < p.tiles - 1:
                eng.wait_ge(tile_done, p.tile0 + n + 1 + (p.tiles - 1) * i)
            else:
                eng.wait_ge(chunk_done, p.chunk0 + p.chunks + p.chunks * i)

        def dest_ap(p, i, n):
            if isinstance(p.dest, list):
                if p.seqs == 1:
                    return tile(p.dest[n])
                return BIG[:, p.dest[n]:p.dest[n] + 2, :].rearrange("p a t -> p (a t)")
            if isinstance(p.dest, tuple):
                where, t0 = p.dest
                if where == "pool_u":
                    return UPAD[:, n]
                if where == "kr":
                    return KRT[:, :]
                base = YT0 + 2 * (t0 + n)
                if isinstance(i, int):
                    base += 2 * p.tiles * i
                    return BIG[:, base:base + 2, :].rearrange("p a t -> p (a t)")
                return BIG[:, bass.ds(base + 2 * p.tiles * i, 2), :].rearrange("p a t -> p (a t)")
            base = p.dest + n
            if isinstance(i, int):
                return BIG[:, base + p.tiles * i, :]
            return BIG[:, bass.ds(base + p.tiles * i, 1), :].rearrange("p a t -> p (a t)")

        def act_evac(act, p, i, only=None):
            for n in range(p.tiles) if only is None else [only]:
                if p.kind == "copy1":
                    wait_tile(act, p, i, n)
                    nc.scalar.activation(dest_ap(p, i, n), PB[n][:, T:2 * T], ACT.Copy).then_inc(half_moved, 1)
                elif p.kind == "copy2":
                    wait_tile(act, p, i, n)
                    src = PB[n][:, :]
                    d = dest_ap(p, i, n)
                    if p.dest[0] == "pool_u":
                        src = src.rearrange("p (s t) -> p s t", s=2)
                        d = d[:, :, 8:8 + T]
                    nc.scalar.activation(d, src, ACT.Copy).then_inc(act_freed, 1)
                elif p.kind == "gate2":
                    wait_tile(act, p, i, n)
                    nc.scalar.activation(GT[:, n], PB[n][:, :], ACT.Sigmoid).then_inc(gate_ready, 1)

        def dve_evac(dve, p, i, only=None):
            for n in range(p.tiles) if only is None else [only]:
                d = dest_ap(p, i, n)
                if p.kind == "copy1":
                    dve.wait_ge(half_moved, p.half0 + n + 1 + p.tiles * i)
                    nc.vector.tensor_tensor(d, PB[n][:, 0:T], d, ALU.add).then_inc(dve_freed, 1)
                elif p.kind == "add1":
                    wait_tile(dve, p, i, n)
                    nc.vector.tensor_tensor(d, PB[n][:, T:2 * T], d, ALU.add).then_inc(resid, 1)
                    dve.wait_ge(resid, p.half0 + n + 1 + p.tiles * i)
                    nc.vector.tensor_tensor(d, PB[n][:, 0:T], d, ALU.add).then_inc(dve_freed, 1)
                elif p.kind == "grp":
                    wait_tile(dve, p, i, n)
                    k = p.dest[1] + n
                    nc.vector.tensor_scalar(d, PB[n][:, :], V["pool_b"][:, k:k + 1], V["pool_s"][:, k:k + 1],
                                            ALU.add, ALU.mult).then_inc(dve_freed, 1)
                elif p.kind == "gate2":
                    dve.wait_ge(gate_ready, n + 1 + p.tiles * i)
                    nc.vector.tensor_tensor(GT[:, n], GT[:, n], PB[n][:, :], ALU.mult).then_inc(dve_freed, 1)
                    dve.wait_ge(dve_freed, p.free0 + n + 1 + p.tiles * i)
                    nc.vector.tensor_tensor(d, GT[:, n], d, ALU.mult).then_inc(resid, 1)

        def dve_ada(dve, p, i, j, only=None):
            for q in range(p.ada) if only is None else [only]:
                u0, uw = p.unit0 + p.ada * j + q, p.ada * p.chunks * i
                if isinstance(i, int):
                    u0, uw = u0 + uw, 0
                part, us = u0 % 4, u0 % 2
                dve.wait_ge(ada_loaded[us], 16 * (u0 // 2 + 1) + 8 * uw)
                if part == 0 and (u0 >= 4 or not isinstance(i, int)):
                    dve.wait_ge(ada_summed, u0 // 4 + (0 if isinstance(i, int) else (p.ada * p.chunks // 4) * i))
                for k in range(KC):
                    for v in range(2):
                        if part == 0 and k == 0:
                            ins = nc.vector.tensor_scalar(ACC[:, v], ARAW[:, us, k], SC[:, v, 0:1], None, ALU.mult)
                        else:
                            dve.wait_ge(ada_link, 8 * u0 + 2 * k + v - 1 + 8 * uw)
                            ins = nc.vector.scalar_tensor_tensor(ACC[:, v], ARAW[:, us, k],
                                                                 SC[:, v, part * KC + k:part * KC + k + 1], ACC[:, v],
                                                                 ALU.mult, ALU.add)
                        ins.then_inc(ada_link, 1)

        def pe_ada(pe, b, w=0, bank=4):
            pe.wait_ge(ada_link, 32 * (b + 1) + 32 * w)
            if b >= 1 or not isinstance(w, int):
                pe.wait_ge(ada_moved, b + w)
            for n in range(2):
                for v in range(2):
                    ins = pe.matmul(PB[bank][:, 2 * n + v:2 * n + v + 1], ACC[:, v, n * P:(n + 1) * P], ones[:, 0:1],
                                    start=True, stop=True, skip_group_check=True)
            ins.then_inc(ada_summed, 1)

        def act_ada(act, b, w=0, bank=4):
            act.wait_ge(ada_summed, b + 1 + w)
            nc.scalar.activation(AD[:, bass.ds(4 * b + 4 * w, 4)], PB[bank][:, 0:4], ACT.Copy).then_inc(ada_moved, 1)

        def ada_ready(p, i, j):
            done = p.ada * (j + (p.chunks * i if isinstance(i, int) else 0))
            if not p.ada or done % 4 or (done == 0 and isinstance(i, int)):
                return None
            return (p.unit0 + done) // 4 - 1

        def pe_chunk(pe, p, i, j, only=None):
            c, w = p.chunk0 + j, p.chunks * i
            if isinstance(i, int):
                c, w = c + w, 0
            slot = c % 2
            if only in (None, 0):
                pe.wait_ge(lo_ready, c + w + 1)
            for n in range(p.tiles) if only is None else [only]:
                if j == 0:
                    if isinstance(i, int) and i == 0:
                        if p.first_bank_wait[n]:
                            pe.wait_ge(freed[p.first_bank_wait[n][0]], p.first_bank_wait[n][1])
                    else:
                        pe.wait_ge(freed[p.freed], p.free0 + p.tiles * i - p.tiles + n + 1)
                for k in range(KC):
                    kk = j * KC + k
                    pick = lambda buf: buf[:, slot, k, n * P:(n + 1) * P]
                    first, last = kk == 0, kk == p.chunks * KC - 1
                    if p.seqs == 1:
                        x = XS[:, kk, :, p.half * T:(p.half + 1) * T]
                        pe.matmul(PB[n][:, :], pick(HI), x, start=first, stop=False, skip_group_check=True)
                        ins = pe.matmul(PB[n][:, T:2 * T], pick(LO), x[:, 0, :], start=False, stop=last,
                                        skip_group_check=True)
                    else:
                        x = (XS if p.src == "xs" else PS)[:, kk]
                        pe.matmul(PB[n][:, :], pick(HI), x[:, 0, :], start=first, stop=False, skip_group_check=True)
                        pe.matmul(PB[n][:, :], pick(HI), x[:, 1, :], start=False, stop=False, skip_group_check=True)
                        ins = pe.matmul(PB[n][:, :], pick(LO), x[:, 0, :], start=False, stop=last,
                                        skip_group_check=True)
                if n < p.tiles - 1:
                    if j == p.chunks - 1:
                        ins.then_inc(tile_done, 1)
                else:
                    ins.then_inc(chunk_done, 1)

        half = 0
        rs = 0
        for p in products:
            if p.kind == "copy1":
                p.half0 = half
                half += p.tiles * p.groups
            elif p.kind == "add1":
                p.half0 = rs
                rs += p.tiles * p.groups
            elif p.kind == "gate2":
                p.steps0 = rs
                rs += p.tiles * p.groups

        def sp_product(sp, p):
            sp_group(sp, p, 0)
            if p.groups > 1:
                step = 2 if p.chunks % 2 else 1
                if step == 2:
                    for g in range(1, p.groups):
                        sp_group(sp, p, g)
                    return
                with sp.Fori(1, p.groups) as i:
                    sp_group(sp, p, i)

        PRIMED = {"in_mem": [kv], "in_x": [win_a], "mfinish": [win_c], "moba": [mixo], "norm_xa": [xq], "cross": [xo],
                  "pre0": [pu[3]], "pre1": [ckv], "latent0": [uq[0]], "pairs": [mo]}
        for ps in PRIMED.values():
            for p in ps:
                p.primed = 1

        def prime(eng, name, split):
            for p in PRIMED.get(name, []):
                split(eng, p, 0, 0)

        def unprimed(p, i, j):
            return not isinstance(i, int) or p.chunks * i + j >= p.primed

        def act_product(act, p, former=None, last=True, extra=None):
            def group(i, prev, aw):
                for j in range(p.chunks):
                    if unprimed(p, i, j):
                        act_high(act, p, i, j)
                    more = extra and isinstance(i, int) and i == 0
                    if more and p.kind == "grp":
                        extra(act, j)
                    if j == 0 and prev is not None:
                        act_evac(act, *prev)
                    if more and p.kind != "grp":
                        extra(act, j)
                    b = ada_ready(p, i, j)
                    if b is not None:
                        act_ada(act, b, aw)
            group(0, (former, former.groups - 1) if former else None, 0)
            if p.groups > 1:
                if p.chunks % 2:
                    for g in range(1, p.groups):
                        group(g, (p, g - 1), 0)
                else:
                    with act.Fori(1, p.groups) as i:
                        group(i, (p, i - 1), (p.ada * p.chunks // 4) * i)
            if last:
                act_evac(act, p, p.groups - 1)
            if p.ada:
                act_ada(act, (p.unit0 + p.ada * p.chunks * p.groups) // 4 - 1)

        def dve_product(dve, p, former=None, last=True, extra=None):
            def group(i, prev):
                for j in range(p.chunks):
                    if unprimed(p, i, j):
                        dve_low(dve, p, i, j)
                    if j == 0 and prev is not None:
                        dve_evac(dve, *prev)
                    if extra and isinstance(i, int) and i == 0:
                        extra(dve, j)
                    dve_ada(dve, p, i, j)
            group(0, (former, former.groups - 1) if former else None)
            if p.groups > 1:
                if p.chunks % 2:
                    for g in range(1, p.groups):
                        group(g, (p, g - 1))
                else:
                    with dve.Fori(1, p.groups) as i:
                        group(i, (p, i - 1))
            if last:
                dve_evac(dve, p, p.groups - 1)

        def pe_product(pe, p, ready=None):
            def group(i, first, aw):
                for j in range(p.chunks):
                    if first and ready:
                        ready(pe, j)
                    for n in range(p.tiles):
                        pe_chunk(pe, p, i, j, only=n)
                        done = p.ada * (j + 1 + (p.chunks * i if isinstance(i, int) else 0))
                        if n == 2 and done and done % 4 == 0:
                            pe_ada(pe, (p.unit0 + done) // 4 - 1, aw)
            group(0, True, 0)
            if p.groups > 1:
                if p.chunks % 2:
                    for g in range(1, p.groups):
                        group(g, False, 0)
                else:
                    with pe.Fori(1, p.groups) as i:
                        group(i, False, (p.ada * p.chunks // 4) * i)

        TOKT = {0: 40, 1: 40, 2: 40}
        XDEST = {0: CT0, 1: 0, 2: CT0}

        def tok(q):
            return BIG[:, TOKT[q]:TOKT[q] + 16, :].rearrange("p (a k) t -> p a (k t)", a=2)

        def sp_turn(sp, q, src):
            for part in range(4):
                cols = slice(512 * part, 512 * (part + 1))
                sp.dma_start(tok(q)[:, :, cols], src[:, cols].rearrange("(a p) f -> p a f", p=P)).then_inc(tok_in[part], 16)

        def pe_turn(pe, q):
            if q == 0:
                pe.wait_ge(consts_in, 16 * 3)
            for kk in range(8):
                n = 8 * q + kk
                pe.wait_ge(tok_in[kk // 2], 16 * (q + 1))
                if n >= 2:
                    pe.wait_ge(tr_free, n - 1)
                for s in range(4):
                    k, h = 2 * kk + s // 2, s % 2
                    ins = pe.transpose(PB[5 + kk % 2][:, s * P:(s + 1) * P], tok(q)[:, h, k * P:(k + 1) * P], ident[:, :])
                ins.then_inc(tr_done, 1)

        def act_turn(act, q):
            for kk in range(8):
                act.wait_ge(tr_done, 8 * q + kk + 1)
                d = BIG[:, XDEST[q] + 2 * kk:XDEST[q] + 2 * kk + 2, :].rearrange("p k t -> p (k t)")
                nc.scalar.activation(d, PB[5 + kk % 2][:, :], ACT.Copy).then_inc(tr_free, 1)

        def src_tiles(n, k, count=1):
            t0, st = n["src"]
            if count == 1:
                return BIG[:, t0 + st * k, :]
            return BIG[:, t0 + st * k:t0 + st * (k + count - 1) + 1:st, :]

        def act_norm(act, *ns):
            for n in ns:
                act_norm_sums(act, n)
            for n in ns:
                act_norm_high(act, n)

        def act_norm_sums(act, n):
            groups = n["nk"] // 4
            for s in range(groups):
                if s >= 2:
                    act.wait_ge(sq_used, n["sq0"] + s - 1)
                nc.scalar.activation(BIG[:, SQ0 + 4 * (s % 2):SQ0 + 4 * (s % 2) + 4, :], src_tiles(n, 4 * s, 4),
                                     ACT.Square).then_inc(sq_ready, 1)
            act.wait_ge(sq_used, n["sq0"] + groups)
            if n["rst_wait"]:
                act.wait_ge(*n["rst_wait"])
            nc.scalar.activation(n["rst"], PB[5][:, 0:T], ACT.Sqrt, bias=EPS, scale=1.0 / (P * n["nk"])).then_inc(std_ready, 1)

        def act_norm_high(act, n):
            if n["mode"] == "operand":
                for k in range(n["nk"]):
                    act.wait_ge(hf_ready, n["hf0"] + k + 1)
                    hf = BIG[:, HF0 + k % 4, :]
                    if n["shift"] is None:
                        nc.scalar.activation(n["dst"](k, 0), hf, ACT.Copy).then_inc(xh_ready, 1)
                    else:
                        nc.scalar.activation(n["dst"](k, 0), hf, ACT.Identity, bias=n["shift"](k)).then_inc(xh_ready, 1)

        def pe_norm(pe, n):
            for s in range(n["nk"] // 4):
                pe.wait_ge(sq_ready, n["sq0"] + s + 1)
                for k in range(4):
                    ins = pe.matmul(PB[5][:, 0:T], ones[:, :], BIG[:, SQ0 + 4 * (s % 2) + k, :],
                                    start=(s == 0 and k == 0), stop=(s == n["nk"] // 4 - 1 and k == 3))
                ins.then_inc(sq_used, 1)

        def dve_norm(dve, n):
            dve.wait_ge(std_ready, n["index"] + 1)
            nc.vector.reciprocal(n["rst"], n["rst"]).then_inc(norm_link, 1)
            dve.wait_ge(norm_link, n["link0"] + 1)

            def low(k):
                dve.wait_ge(xh_ready, n["xh0"] + k + 1)
                hf, hi, lo = BIG[:, HF0 + k % 4, :], n["dst"](k, 0).bitcast(F32), n["dst"](k, 1)
                if n["shift"] is None:
                    nc.vector.tensor_sub(lo, hf, hi).then_inc(xs_ready, 1)
                else:
                    nc.vector.scalar_tensor_tensor(lo, hf, n["shift"](k), hi, ALU.add, ALU.subtract).then_inc(xs_ready, 1)

            for k in range(n["nk"]):
                if n["mode"] == "operand":
                    if k >= 4:
                        dve.wait_ge(xs_ready, n["xs0"] + k - 3)
                    nc.vector.scalar_tensor_tensor(BIG[:, HF0 + k % 4, :], src_tiles(n, k), n["gain"](k), n["rst"],
                                                   ALU.mult, ALU.mult).then_inc(hf_ready, 1)
                    if k >= 1:
                        low(k - 1)
                elif n["mode"] == "inplace":
                    nc.vector.scalar_tensor_tensor(src_tiles(n, k), src_tiles(n, k), n["gain"](k), n["rst"],
                                                   ALU.mult, ALU.mult).then_inc(norm_done, 1)
                else:
                    if k >= 4:
                        dve.wait_ge(norm_done, n["nd0"] + k - 3)
                    nc.vector.scalar_tensor_tensor(BIG[:, HF0 + k % 4, :], src_tiles(n, k), n["gain"](k), n["rst"],
                                                   ALU.mult, ALU.mult).then_inc(norm_link, 1)
                    dve.wait_ge(norm_link, n["link0"] + 2 + k)
                    d = BIG[:, n["dst"] + k, :]
                    nc.vector.tensor_tensor(d, d, BIG[:, HF0 + k % 4, :], ALU.add).then_inc(norm_done, 1)
            if n["mode"] == "operand":
                low(n["nk"] - 1)

        xs_dst = lambda half: (lambda k, part: XS[:, k, part, half * T:(half + 1) * T])
        ps_dst = lambda half: (lambda k, part: PS[:, k, part, half * T:(half + 1) * T])
        vcol = lambda name: (lambda k: V[name][:, k:k + 1])
        mod = lambda r: (lambda k: MODS[:, r, k:k + 1])
        norms = {
            "mem": dict(src=(CT0, 1), nk=16, gain=vcol("mem_g"), shift=None, dst=xs_dst(1), mode="operand"),
            "mix": dict(src=(0, 1), nk=16, gain=vcol("mix_g"), shift=None, dst=xs_dst(0), mode="operand"),
            "xa": dict(src=(0, 1), nk=16, gain=vcol("xa_g"), shift=None, dst=xs_dst(0), mode="operand"),
            "final": dict(src=(0, 1), nk=16, gain=vcol("final_g"), shift=None, dst=None, mode="inplace"),
            "pre0": dict(src=(0, 1), nk=16, gain=mod(0), shift=mod(2), dst=xs_dst(0), mode="operand"),
            "pre0c": dict(src=(CT0, 1), nk=16, gain=mod(1), shift=mod(3), dst=xs_dst(1), mode="operand"),
            "post0": dict(src=(YT0, 2), nk=16, gain=mod(4), shift=None, dst=0, mode="update"),
            "post0c": dict(src=(YT0 + 1, 2), nk=16, gain=mod(5), shift=None, dst=CT0, mode="update"),
            "pre1": dict(src=(0, 1), nk=16, gain=mod(0), shift=mod(2), dst=xs_dst(0), mode="operand"),
            "pre1c": dict(src=(CT0, 1), nk=16, gain=mod(1), shift=mod(3), dst=xs_dst(1), mode="operand"),
            "ckv": dict(src=(32, 2), nk=4, gain=vcol("kv_g"), shift=None, dst=ps_dst(0), mode="operand"),
            "ckvc": dict(src=(33, 2), nk=4, gain=vcol("kv_g"), shift=None, dst=ps_dst(1), mode="operand"),
            "cq": dict(src=(40, 1), nk=4, gain=vcol("q_g"), shift=None, dst=xs_dst(1), mode="operand"),
            "post1": dict(src=(32, 1), nk=16, gain=mod(4), shift=None, dst=0, mode="update"),
        }
        sq = hf = link = nd = 0
        rst_wait = None
        for index, n in enumerate(norms.values()):
            n.update(rst_wait=rst_wait, index=index, sq0=sq, hf0=hf, xh0=hf, xs0=hf, link0=link, nd0=nd)
            sq += n["nk"] // 4
            link += 1
            if n["mode"] == "operand":
                hf += n["nk"]
            elif n["mode"] == "update":
                link += n["nk"]
                nd += n["nk"]
            else:
                nd += n["nk"]
            rst_wait = (xs_ready, hf) if n["mode"] == "operand" else (norm_done, nd)
        own = {"pre0c": 76, "post0c": 76, "pre1c": 76, "ckvc": 62, "cq": 63}
        for name, n in norms.items():
            n["rst"] = tile(own[name]) if name in own else RST[:, :]
            if name in own:
                n["rst_wait"] = None

        setup = steps("setup_dve", [("rows",), ("ones",), ("eps",), ("epsln",), ("silu",)])
        sc_act, vec_turned, pv_ready = sem("silu_c_sigmoid"), sem("vectors_turned"), sem("vectors_ready")

        def pe_setup(pe):
            pe.wait_ge(vec_in, VEC_IN)
            pe.wait_ge(consts_in, 48)
            for b in range(4):
                ins = pe.transpose(PB[5][:, b * P:(b + 1) * P], VROW[:, b * P:(b + 1) * P], ident[:, :])
            ins.then_inc(vec_turned, 1)

        def act_setup(act):
            for i, (dst, name) in enumerate(((ident, "ident"), (blockmask, "blockmask"), (mlmask, "mlmask"))):
                act.dma_start(dst[:, :], a[name]).then_inc(consts_in, 16)
            act.wait_ge(setup.sem, 1)
            for name, src, n in VEC:
                b, r = place[name] // P, place[name] % P
                act.dma_start(VROW[r:r + n, b * P:(b + 1) * P], src).then_inc(vec_in, 16)
            act.dma_start(gb[0:4, 0:1], a["ml_bi"].rearrange("l h -> h l")).then_inc(vec_in, 16)
            act.dma_start(gb[0:4, 1:2], a["ml_bf"].rearrange("l h -> h l")).then_inc(vec_in, 16)
            act.wait_ge(vec_turned, 1)
            nc.scalar.activation(PV[:, :], PB[5][:, :], ACT.Copy).then_inc(pv_ready, 1)
            act.wait_ge(pv_ready, 1)
            for v, name in enumerate(("c", "c_ctx")):
                nc.scalar.activation(SC[:, v, :], V[name], ACT.Sigmoid).then_inc(sc_act, 1)

        def dve_setup(dve):
            setup.inc(nc.vector.memset(VROW, 0.0), "rows")
            setup.inc(nc.vector.memset(ones[:, :], 1.0), "ones")
            setup.inc(nc.vector.memset(EPS, RMS_EPS), "eps")
            setup.inc(nc.vector.memset(EPSLN, LN_EPS), "epsln")
            dve.wait_ge(sc_act, 2)
            setup.inc(nc.vector.tensor_tensor(SC[:, :, :], SC[:, :, :],
                                              PV[:, CCOL:CCOL + 32].rearrange("p (v k) -> p v k", v=2), ALU.mult), "silu")
            assert place["c"] == CCOL and place["c_ctx"] == CCOL + 16

        ends = {"pe": sem("stage_end_pe"), "act": sem("stage_end_act"), "dve": sem("stage_end_dve")}
        stages = {"pe": 0, "act": 0, "dve": 0}

        def stage_end(eng, me):
            stages[me] += 1
            eng.drain().then_inc(ends[me], 1)
            for other in ends:
                if other != me:
                    eng.wait_ge(ends[other], stages[me])

        def l1p_names():
            return ["den", "rec", "z", "z2", "h17"] + [f"h{c}" for c in (15, 13, 11, 9, 7, 5, 3)] + ["l1p"]

        def dve_log1p(dve, st, y, t, z, z2, out_):
            v = nc.vector
            st.inc(v.tensor_scalar(t, y, 2.0, None, ALU.add), "den")
            st.wait(dve, "den")
            st.inc(v.reciprocal(t, t), "rec")
            st.wait(dve, "rec")
            st.inc(v.tensor_tensor(z, y, t, ALU.mult), "z")
            st.wait(dve, "z")
            st.inc(v.tensor_tensor(z2, z, z, ALU.mult), "z2")
            st.wait(dve, "z2")
            st.inc(v.tensor_scalar(t, z2, 1.0 / 17, None, ALU.mult), "h17")
            last = "h17"
            for c in (15, 13, 11, 9, 7, 5, 3):
                st.wait(dve, last)
                last = f"h{c}"
                st.inc(v.scalar_tensor_tensor(t, t, 1.0 / c, z2, ALU.add, ALU.mult), last)
            st.wait(dve, last)
            st.inc(v.scalar_tensor_tensor(out_, t, 1.0, z, ALU.add, ALU.mult), "l1p")
            st.wait(dve, "l1p")

        LW = BIG[:, 20:24, :].rearrange("p a (b t) -> p (a b) t", b=2)
        MW = BIG[:, 46, 0:72].rearrange("p (n t o) -> p n t o", n=3, t=6)
        mw_in = sem("ml_w_in")
        SEL = BIG[0:4, 16:18, :].rearrange("p a t -> p (a t)")
        gb = small[:, 56:58]
        VEC_IN = 16 * (len(VEC) + 2)
        CCOL = 32
        sp4, spt, spz, spz2 = small[:, 0:4], small[:, 4:8], small[:, 8:12], small[:, 12:16]
        xc = lambda b: tile(24 + b)
        ra = lambda b: tile(28 + b)
        ix = lambda b: tile(67 + b)
        lq = lambda b: tile(71 + b)
        lru_act = steps("lru_act", [("abs",), ("exp",)] + [(n, b) for b in range(4) for n in ("r", "i", "zs")]
                        + [("q", b) for b in range(4)] + [("a", b) for b in range(4)] + [("sq", b) for b in range(4)])
        lru_pe = steps("lru_pe", [(n, b) for b in range(4) for n in ("r", "i")])
        lru_dve = steps("lru_dve", [(n, b) for b in range(4) for n in ("c3", "c2", "c1", "c0")]
                        + [(n,) for n in l1p_names()] + [("spm",), ("sp",)]
                        + [(n, b) for b in range(4) for n in ("la", "ixc", "zsz")]
                        + [(n, b) for b in range(4) for n in ("q1", "q1r", "q2")]
                        + [(n, b) for b in range(4) for n in ("u", "scan", "y")])

        def dve_conv(dve, st, src, dst, w, b, taps, key):
            st.inc(nc.vector.tensor_scalar(dst, src, w(3), b, ALU.mult, ALU.add), "c3", key)
            for j in (2, 1, 0):
                s = 3 - j
                st.wait(dve, f"c{j + 1}", key)
                st.inc(nc.vector.scalar_tensor_tensor(dst[:, s:T], src[:, 0:T - s], w(j), dst[:, s:T], ALU.mult, ALU.add),
                       f"c{j}", key)

        def dve_lru(dve):
            v = nc.vector
            for b in range(4):
                dve_conv(dve, lru_dve, tile(LX + b), xc(b), lambda j: V["lru_conv_w"][:, 4 * j + b:4 * j + b + 1],
                         V["lru_conv_b"][:, b:b + 1], 4, b)
            lru_act.wait(dve, "exp")
            dve_log1p(dve, lru_dve, sp4, spt, spz, spz2, spz)
            lru_dve.inc(v.tensor_scalar(spt, V["lru_lambda"], -1.0, 0.0, ALU.mult, ALU.max), "spm")
            lru_dve.wait(dve, "spm")
            lru_dve.inc(v.scalar_tensor_tensor(sp4, spz, 2.0, spt, ALU.mult, ALU.add), "sp")
            lru_dve.wait(dve, "sp")
            for b in range(4):
                lru_act.wait(dve, "r", b)
                lru_dve.inc(v.tensor_scalar(ra(b), ra(b), sp4[:, b:b + 1], 8.0, ALU.mult, ALU.mult), "la", b)
                lru_act.wait(dve, "i", b)
                lru_dve.inc(v.tensor_tensor(ix(b), ix(b), xc(b), ALU.mult), "ixc", b)
                lru_act.wait(dve, "zs", b)
                lru_dve.inc(v.tensor_tensor(tile(LZ + b), tile(LZ + b), xc2(b), ALU.mult), "zsz", b)
            for b in range(4):
                lru_act.wait(dve, "q", b)
                lru_dve.inc(v.tensor_scalar(xc(b), lq(b), 1.0, None, ALU.add), "q1", b)
                lru_dve.wait(dve, "q1", b)
                lru_dve.inc(v.reciprocal(xc(b), xc(b)), "q1r", b)
                lru_dve.wait(dve, "q1r", b)
                lru_dve.inc(v.scalar_tensor_tensor(lq(b), lq(b), 2.0, xc(b), ALU.mult, ALU.mult), "q2", b)
            for b in range(4):
                lru_act.wait(dve, "sq", b)
                lru_dve.inc(v.tensor_tensor(ix(b), ix(b), lq(b), ALU.mult), "u", b)
                lru_dve.wait(dve, "u", b)
                lru_act.wait(dve, "a", b)
                lru_dve.inc(v.tensor_tensor_scan(xc(b), ra(b), ix(b), 0.0, ALU.mult, ALU.add), "scan", b)
                lru_dve.wait(dve, "scan", b)
                lru_dve.inc(v.tensor_tensor(tile(LX + b), xc(b), tile(LZ + b), ALU.mult), "y", b)

        xc2 = lambda b: tile(16 + b)

        def pe_lru(pe):
            for b in range(4):
                lru_dve.wait(pe, "c0", b)
                if b >= 1:
                    lru_act.wait(pe, "i", b - 1)
                lru_pe.inc(pe.matmul(PB[5][:, 0:T], LW[:, b], xc(b), start=True, stop=True), "r", b)
                lru_pe.inc(pe.matmul(PB[6][:, 0:T], LW[:, 4 + b], xc(b), start=True, stop=True), "i", b)

        def act_lru(act):
            s = nc.scalar.activation
            lru_act.inc(s(sp4, V["lru_lambda"], ACT.Abs), "abs")
            lru_act.wait(act, "abs")
            lru_act.inc(s(sp4, sp4, ACT.Exp, scale=-1.0), "exp")
            for b in range(4):
                lru_pe.wait(act, "r", b)
                lru_act.inc(s(ra(b), PB[5][:, 0:T], ACT.Sigmoid, bias=V["lru_ba"][:, b:b + 1]), "r", b)
                lru_pe.wait(act, "i", b)
                lru_act.inc(s(ix(b), PB[6][:, 0:T], ACT.Sigmoid, bias=V["lru_bx"][:, b:b + 1]), "i", b)
                lru_act.inc(s(xc2(b), tile(LZ + b), ACT.Sigmoid), "zs", b)
            for b in range(4):
                lru_dve.wait(act, "la", b)
                lru_act.inc(s(lq(b), ra(b), ACT.Tanh), "q", b)
            for b in range(4):
                lru_act.wait(act, "q", b)
                lru_act.inc(s(ra(b), ra(b), ACT.Exp, scale=-1.0), "a", b)
            for b in range(4):
                lru_dve.wait(act, "q2", b)
                lru_act.inc(s(lq(b), lq(b), ACT.Sqrt), "sq", b)

        split_hi, split_lo = sem("split_high"), sem("split_low")
        splits = {}
        order = [("lru", 4), ("ml", 6), ("mo", 6), ("xo", 4), ("pp3", 4), ("pp2", 4), ("pp1", 4), ("pp0", 4), ("py", 16)]
        n0 = 0
        for name, n in order:
            splits[name] = n0
            n0 += n

        def act_split(act, name, k, src, dst):
            nc.scalar.activation(dst, src, ACT.Copy).then_inc(split_hi, 1)

        def dve_split(dve, name, k, src, dst, hi):
            dve.wait_ge(split_hi, splits[name] + k + 1)
            nc.vector.tensor_sub(dst, src, hi.bitcast(F32)).then_inc(split_lo, 1)

        def rows(t):
            return BIG[0:4, t, :]
        rF, rY, rT, rZ, rZ2, rB, rE, rM, rI = (rows(t) for t in (76, 77, 28, 29, 30, 31, 46, 47, G))
        QR = BIG[0:4, 73:76, :].rearrange("p a (b l) -> p (a b) l", l=P)
        QC = small[:, 20:44].rearrange("p (q h) -> p q h", h=4)
        m1, nm0 = small[0:4, 44:45], small[0:4, 45:46]
        fg_in, sel_in, lw_in = sem("forget_rows_in"), sem("sel_in"), sem("lru_w_in")
        mg_dve = steps("mg_dve", [("f",), ("i",)] + [(n,) for n in l1p_names()] + [("fm",), ("lf",), ("b0",), ("b1",),
                       ("e",), ("M0",), ("nm0",), ("m1",), ("M1",), ("bm",), ("qe",), ("qc",)] + [("t", h) for h in range(4)])
        mg_act = steps("mg_act", [("abs",), ("exp",), ("em",), ("w0",), ("s1",)]
                       + [("E", h, c) for h in range(4) for c in range(2)])
        mg_pe = steps("mg_pe", [("cols",), ("M", 0), ("M", 1), ("M", 2), ("M", 3)])

        def act_mgates(act):
            s = nc.scalar.activation
            act.dma_start(rF, BIG[4:8, G, :]).then_inc(fg_in, 16)
            act.dma_start(SEL, a["sel"]).then_inc(sel_in, 16)
            mg_dve.wait(act, "f")
            mg_act.inc(s(rY, rF, ACT.Abs), "abs")
            mg_act.wait(act, "abs")
            mg_act.inc(s(rY, rY, ACT.Exp, scale=-1.0), "exp")
            mg_dve.wait(act, "bm")
            mg_act.inc(s(QR[:, 2:4, :], rB.rearrange("p (c l) -> p c l", c=2), ACT.Exp, scale=-1.0), "em")
            mg_act.inc(s(QR[:, 4, :], rE[:, 0:P], ACT.Exp, bias=nm0), "w0")
            mg_act.inc(s(QR[:, 5, :], rM[:, P:T], ACT.Exp, bias=m1, scale=-1.0), "s1")
            for h in range(4):
                mg_dve.wait(act, "t", h)
                for c in range(2):
                    e = BIG[:, EX + h, c * P:(c + 1) * P]
                    mg_act.inc(s(e, e, ACT.Exp, bias=QC[:, c, h:h + 1]), "E", h, c)

        def dve_mgates(dve):
            v, st = nc.vector, mg_dve
            dve.wait_ge(fg_in, 16)
            st.inc(v.tensor_scalar(rF, rF, gb[0:4, 1:2], None, ALU.add), "f")
            st.inc(v.tensor_scalar(rI, rI, gb[0:4, 0:1], None, ALU.add), "i")
            mg_act.wait(dve, "exp")
            dve_log1p(dve, st, rY, rT, rZ, rZ2, rZ)
            st.inc(v.tensor_scalar(rF, rF, 0.0, None, ALU.min), "fm")
            st.wait(dve, "fm")
            st.inc(v.scalar_tensor_tensor(rF, rZ, -2.0, rF, ALU.mult, ALU.add), "lf")
            st.wait(dve, "lf")
            for c in range(2):
                st.inc(v.tensor_tensor_scan(rB[:, c * P:(c + 1) * P], ones[0:4, :], rF[:, c * P:(c + 1) * P], 0.0,
                                            ALU.mult, ALU.add), f"b{c}")
            st.wait(dve, "b1")
            st.inc(v.tensor_tensor(rE, rI, rB, ALU.subtract), "e")
            st.wait(dve, "e")
            st.inc(v.tensor_tensor_scan(rM[:, 0:P], ones[0:4, :], rE[:, 0:P], 0.0, ALU.mult, ALU.max), "M0")
            st.wait(dve, "M0")
            st.inc(v.tensor_scalar(nm0, rM[:, P - 1:P], -1.0, None, ALU.mult), "nm0")
            st.inc(v.tensor_tensor(m1, rM[:, P - 1:P], rB[:, P - 1:P], ALU.add), "m1")
            st.wait(dve, "m1")
            st.inc(v.tensor_tensor_scan(rM[:, P:T], ones[0:4, :], rE[:, P:T], m1, ALU.mult, ALU.max), "M1")
            st.wait(dve, "M1")
            st.inc(v.tensor_tensor(rB, rB, rM, ALU.add), "bm")
            st.inc(v.tensor_copy(QR[:, 0:2, :], rE.rearrange("p (c l) -> p c l", c=2)), "qe")
            mg_pe.wait(dve, "cols")
            st.inc(v.tensor_copy(small[:, 20:44], PB[5][:, 0:24]), "qc")
            for h in range(4):
                mg_pe.wait(dve, "M", 1 if h < 2 else 3)
                st.inc(v.scalar_tensor_tensor(BIG[:, EX + h, :].rearrange("p (c l) -> p c l", c=2),
                                              PB[6 + h // 2][:, (h % 2) * T:(h % 2 + 1) * T].rearrange("p (c l) -> p c l", c=2),
                                              -1.0, mlmask[:, :].unsqueeze(1).to_broadcast([P, 2, P]),
                                              ALU.mult, ALU.add), "t", h)

        def pe_mgates(pe):
            mg_act.wait(pe, "s1")
            mg_dve.wait(pe, "qe")
            for q in range(6):
                ins = pe.transpose(PB[5][:, 4 * q:4 * q + 4], QR[:, q, :], ident[0:4, 0:4])
            mg_pe.inc(ins, "cols")
            mg_dve.wait(pe, "bm")
            pe.wait_ge(sel_in, 16)
            for h in range(4):
                mg_pe.inc(pe.matmul(PB[6 + h // 2][:, (h % 2) * T:(h % 2 + 1) * T], SEL[:, h * P:(h + 1) * P], rM,
                                    start=True, stop=True, skip_group_check=True), "M", h)

        DH = 192
        BD = lambda n: BIG[:, 76 + (n % 4) // 2, (n % 2) * P:(n % 2 + 1) * P]
        VTV = BIG[:, VT:VT + 6, :].rearrange("p a t -> p (a t)").rearrange("p (c f) -> p c f", c=2)
        KTV = BIG[:, KTOK:KTOK + 3, :].rearrange("p a t -> p (a t)")
        SOV = BIG[:, SOT:SOT + 6, :].rearrange("p a t -> p (a t)").rearrange("p (c f) -> p c f", c=2)
        HNV = BIG[:, O:O + 6, :].rearrange("p a t -> p (a t)").rearrange("p (c f) -> p c f", c=2)
        mp_dve = steps("mp_dve", [(n, i) for i in range(6) for n in ("c3", "c2", "c1", "c0")] + [("uc", i) for i in range(6)]
                       + [("bd", n) for n in range(18)] + [("so", i) for i in range(6)])
        mp_act = steps("mp_act", [("sg", i) for i in range(6)]
                       + [(n, i) for i in range(6) for n in ("q", "k", "kt", "v")] + [("o", i) for i in range(6)])
        mp_pe = steps("mp_pe", [(n, i) for i in range(6) for n in ("q", "k", "v")] + [("o", i) for i in range(6)])

        def act_mproj(act):
            s = nc.scalar.activation
            for n, w in enumerate(("ml_wq", "ml_wk", "ml_wv")):
                act.dma_start(MW[:, n], a[w][0].rearrange("(t g) i o -> (g i) t o", g=32)).then_inc(mw_in, 16)
            for i in range(6):
                mp_dve.wait(act, "c0", i)
                mp_act.inc(s(tile(KT + i), tile(UC + i), ACT.Sigmoid), "sg", i)
            for i in range(6):
                mp_pe.wait(act, "q", i)
                mp_act.inc(s(tile(QT + i), PB[5][:, 0:T], ACT.Copy), "q", i)
                mp_pe.wait(act, "k", i)
                mp_act.inc(s(tile(KT + i), PB[6][:, 0:T], ACT.Copy, scale=DH ** -0.5), "k", i)
                mp_act.inc(s(KTV[:, i * P:(i + 1) * P], PB[6][:, T:T + P], ACT.Copy, scale=DH ** -0.5), "kt", i)
                mp_pe.wait(act, "v", i)
                mp_act.inc(s(VTV[:, :, i * P:(i + 1) * P], PB[7][:, 0:T].rearrange("p (c f) -> p c f", c=2), ACT.Copy), "v", i)
            for i in range(6):
                mp_act.inc(s(tile(O + i), tile(O + i), ACT.Sigmoid), "o", i)

        def dve_mproj(dve):
            v, st = nc.vector, mp_dve
            for i in range(6):
                dve_conv(dve, st, tile(U + i), tile(UC + i), lambda j: V["ml_conv_w"][:, 6 * j + i:6 * j + i + 1],
                         V["ml_conv_b"][:, i:i + 1], 4, i)
            for i in range(6):
                mp_act.wait(dve, "sg", i)
                st.inc(v.tensor_tensor(tile(UC + i), tile(UC + i), tile(KT + i), ALU.mult), "uc", i)
            dve.wait_ge(mw_in, 48)
            for n in range(18):
                i, m = n // 3, n % 3
                if n >= 4:
                    mp_pe.wait(dve, "qkv"[(n - 4) % 3], (n - 4) // 3)
                st.inc(v.tensor_tensor(BD(n).rearrange("p (g o) -> p g o", o=4),
                                       blockmask[:, :].rearrange("p (g o) -> p g o", o=4),
                                       MW[:, m, i, :].unsqueeze(1).to_broadcast([P, 32, 4]), ALU.mult), "bd", n)
            for i in range(6):
                mp_pe.wait(dve, "o", i)
                st.inc(v.tensor_copy(SOV[:, :, i * P:(i + 1) * P],
                                     PB[5 + i % 2][:, 0:T].rearrange("p (c f) -> p c f", c=2)), "so", i)

        def pe_mproj(pe):
            st = mp_pe
            for i in range(6):
                mp_dve.wait(pe, "bd", 3 * i)
                if i:
                    mp_act.wait(pe, "q", i - 1)
                st.inc(pe.matmul(PB[5][:, 0:T], BD(3 * i), tile(UC + i), start=True, stop=True), "q", i)
                mp_dve.wait(pe, "bd", 3 * i + 1)
                if i:
                    mp_act.wait(pe, "kt", i - 1)
                pe.matmul(PB[6][:, 0:T], BD(3 * i + 1), tile(UC + i), start=True, stop=True, skip_group_check=True)
                st.inc(pe.matmul(PB[6][:, T:T + P], tile(UC + i)[:, 0:P], BD(3 * i + 1), start=True, stop=True,
                                 skip_group_check=True), "k", i)
                mp_dve.wait(pe, "bd", 3 * i + 2)
                if i:
                    mp_act.wait(pe, "v", i - 1)
                for c in range(2):
                    ins = pe.matmul(PB[7][:, c * P:(c + 1) * P], tile(U + i)[:, c * P:(c + 1) * P], BD(3 * i + 2),
                                    start=True, stop=True, skip_group_check=True)
                st.inc(ins, "v", i)
            for i in range(6):
                mp_act.wait(pe, "o", i)
                if i >= 2:
                    mp_dve.wait(pe, "so", i - 2)
                for c in range(2):
                    ins = pe.transpose(PB[5 + i % 2][:, c * P:(c + 1) * P], tile(O + i)[:, c * P:(c + 1) * P], ident[:, :])
                st.inc(ins, "o", i)

        def segs(h):
            t = 3 * (h // 2)
            return [(t, 0, P, 0), (t + 1, 0, 64, P)] if h % 2 == 0 else [(t + 1, 64, P, 0), (t + 2, 0, P, 64)]

        CS = BIG[:, 16:21, :].rearrange("p a t -> p (a t)")[:, 0:6 * 193].rearrange("p (i e) -> p i e", e=193)
        WK = lambda h: BIG[:, 46 + h % 2, 0:DH]
        PT_ = lambda u: BIG[:, 76, (u % 2) * P:(u % 2 + 1) * P]
        NUM = BIG[:, 77, 0:193]
        INT = BIG[:, 75, 0:193]
        ST = small[:, 46:52]
        MV_ = small[:, 52:54]
        DEN = small[:, 54:55]
        units = [(h, c) for h in range(4) for c in range(2)]
        mh_dve = steps("mh_dve", [("wk", h) for h in range(4)] +
                       [k for u, (h, c) in enumerate(units) for k in
                        ([("p", u)] + ([("int", u)] if c else []) + [("num", u), ("abs", u), ("den", u), ("rden", u), ("h", u),
                         ("st", u), ("ag", u), ("rs", u), ("hn", u)])])
        mh_act = steps("mh_act", [("cs", h) for h in range(4)] + [("std", u) for u in range(8)])
        mh_pe = steps("mh_pe", [("cs", h) for h in range(4)] +
                      [k for u, (h, c) in enumerate(units) for k in ([("s", u)] + ([("int", u)] if c else []) + [("num", u)])])

        def pe_mheads(pe):
            for h in range(4):
                mh_dve.wait(pe, "wk", h)
                if h:
                    mh_act.wait(pe, "cs", h - 1)
                for n, (t, r0, r1, off) in enumerate(segs(h)):
                    w = WK(h)[:, off:off + r1 - r0]
                    pe.matmul(PB[7][r0:r1, 256 * n:256 * n + DH], w, VTV[:, 0, DH * h:DH * (h + 1)], start=True, stop=True,
                              skip_group_check=True)
                    ins = pe.matmul(PB[7][r0:r1, 256 * n + DH:256 * n + 193], w, ones[:, 0:1], start=True, stop=True,
                                    skip_group_check=True)
                mh_pe.inc(ins, "cs", h)
            mh_act.wait(pe, "cs", 3)
            for u, (h, c) in enumerate(units):
                if u:
                    mh_dve.wait(pe, "p", u - 1)
                sg = segs(h)
                for n, (t, r0, r1, off) in enumerate(sg):
                    ins = pe.matmul(PB[5][:, 0:P], BIG[r0:r1, KT + t, c * P:(c + 1) * P], BIG[r0:r1, QT + t, c * P:(c + 1) * P],
                                    start=n == 0, stop=n == 1)
                mh_pe.inc(ins, "s", u)
                if c:
                    if u >= 2:
                        mh_dve.wait(pe, "int", u - 2)
                    for n, (t, r0, r1, off) in enumerate(sg):
                        ins = pe.matmul(PB[7][:, 0:193], BIG[r0:r1, QT + t, P:T], CS[r0:r1, t, :], start=n == 0, stop=n == 1)
                    mh_pe.inc(ins, "int", u)
                mh_dve.wait(pe, "p", u)
                if u:
                    mh_dve.wait(pe, "num", u - 1)
                pe.matmul(PB[6][:, 0:DH], PT_(u), VTV[:, c, DH * h:DH * (h + 1)], start=True, stop=True, skip_group_check=True)
                mh_pe.inc(pe.matmul(PB[6][:, DH:193], PT_(u), ones[:, 0:1], start=True, stop=True, skip_group_check=True),
                          "num", u)

        def act_mheads(act):
            for h in range(4):
                mh_pe.wait(act, "cs", h)
                for n, (t, r0, r1, off) in enumerate(segs(h)):
                    ins = nc.scalar.activation(CS[r0:r1, t, :], PB[7][r0:r1, 256 * n:256 * n + 193], ACT.Copy)
                mh_act.inc(ins, "cs", h)
            for u in range(8):
                mh_dve.wait(act, "ag", u)
                mh_act.inc(nc.scalar.activation(MV_[:, 1:2], MV_[:, 1:2], ACT.Sqrt, bias=EPSLN), "std", u)

        def dve_mheads(dve):
            v, st = nc.vector, mh_dve
            for h in range(4):
                if h >= 2:
                    mh_pe.wait(dve, "cs", h - 2)
                st.inc(v.tensor_scalar(WK(h), KTV[:, DH * h:DH * (h + 1)], QC[:, 4, h:h + 1], None, ALU.mult), "wk", h)
            for u, (h, c) in enumerate(units):
                mh_pe.wait(dve, "s", u)
                if u >= 2:
                    mh_pe.wait(dve, "num", u - 2)
                st.inc(v.tensor_tensor(PT_(u), BIG[:, EX + h, c * P:(c + 1) * P], PB[5][:, 0:P], ALU.mult), "p", u)
                if c:
                    mh_pe.wait(dve, "int", u)
                    st.inc(v.tensor_scalar(INT, PB[7][:, 0:193], QC[:, 5, h:h + 1], None, ALU.mult), "int", u)
                    st.wait(dve, "int", u)
                    mh_pe.wait(dve, "num", u)
                    st.inc(v.tensor_tensor(NUM, PB[6][:, 0:193], INT, ALU.add), "num", u)
                else:
                    mh_pe.wait(dve, "num", u)
                    st.inc(v.tensor_copy(NUM, PB[6][:, 0:193]), "num", u)
                st.wait(dve, "num", u)
                st.inc(v.scalar_tensor_tensor(DEN, NUM[:, 192:193], -1.0, NUM[:, 192:193], ALU.mult, ALU.max), "abs", u)
                st.wait(dve, "abs", u)
                st.inc(v.tensor_scalar(DEN, DEN, QC[:, 2 + c, h:h + 1], None, ALU.max), "den", u)
                st.wait(dve, "den", u)
                st.inc(v.reciprocal(DEN, DEN), "rden", u)
                st.wait(dve, "rden", u)
                hn = HNV[:, c, DH * h:DH * (h + 1)]
                st.inc(v.scalar_tensor_tensor(hn, NUM[:, 0:DH], DEN, SOV[:, c, DH * h:DH * (h + 1)], ALU.mult, ALU.mult), "h", u)
                st.wait(dve, "h", u)
                st.inc(v.bn_stats(ST, hn), "st", u)
                st.wait(dve, "st", u)
                st.inc(v.bn_aggr(MV_, ST), "ag", u)
                mh_act.wait(dve, "std", u)
                st.inc(v.reciprocal(MV_[:, 1:2], MV_[:, 1:2]), "rs", u)
                st.wait(dve, "rs", u)
                st.inc(v.tensor_scalar(hn, hn, MV_[:, 0:1], MV_[:, 1:2], ALU.subtract, ALU.mult), "hn", u)

        mf_act = steps("mf_act", [("z", i) for i in range(6)])
        mf_dve = steps("mf_dve", [("z", i) for i in range(6)] + [("y", i) for i in range(6)])
        mf_pe = steps("mf_pe", [("t", i) for i in range(6)])

        def act_mfinish(act):
            for i in range(6):
                mf_act.inc(nc.scalar.activation(tile(QT + i), tile(Z + i), ACT.Sigmoid), "z", i)
            for i in range(6):
                mf_dve.wait(act, "y", i)
                act_split(act, "ml", i, tile(Z + i), XS[:, 4 + i, 0, T:2 * T])

        def dve_mfinish(dve):
            for i in range(6):
                mf_act.wait(dve, "z", i)
                mf_dve.inc(nc.vector.tensor_tensor(tile(Z + i), tile(Z + i), tile(QT + i), ALU.mult), "z", i)
            for i in range(6):
                mf_pe.wait(dve, "t", i)
                mf_dve.wait(dve, "z", i)
                mf_dve.inc(nc.vector.scalar_tensor_tensor(tile(Z + i), PB[5 + i % 2][:, 0:T], V["ml_g"][:, i:i + 1],
                                                          tile(Z + i), ALU.mult, ALU.mult), "y", i)
            for i in range(6):
                dve_split(dve, "ml", i, tile(Z + i), XS[:, 4 + i, 1, T:2 * T], XS[:, 4 + i, 0, T:2 * T])

        def pe_mfinish(pe):
            for i in range(6):
                if i >= 2:
                    mf_dve.wait(pe, "y", i - 2)
                for c in range(2):
                    ins = pe.transpose(PB[5 + i % 2][:, c * P:(c + 1) * P], HNV[:, c, i * P:(i + 1) * P], ident[:, :])
                mf_pe.inc(ins, "t", i)

        def slopes(n):
            pow2 = lambda m: [2.0 ** (-8.0 / m * (i + 1)) for i in range(m)]
            c = 2 ** int(np.floor(np.log2(n)))
            return pow2(c) + pow2(2 * c)[0::2][:n - c]

        DIST = BIG[:, 64:66, :]
        dist_in = sem("distances_in")

        class Attn:
            def __init__(self, name, heads, q, k, v, biased, outs, gates):
                self.heads, self.q, self.k, self.v, self.biased, self.outs, self.gates = heads, q, k, v, biased, outs, gates
                self.name = name
                self.pe = steps(name + "_pe", [("v", h) for h in range(heads)] + [("s", 0)] +
                                [x for h in range(heads) for x in ([("s", h + 1)] if h + 1 < heads else []) + [("t", h), ("o", h)]])
                self.act = steps(name + "_act", ([("z", h) for h in range(heads)] if gates else []) +
                                 [("v", h) for h in range(heads)] +
                                 [x for h in range(heads) for x in [("e", h, 0), ("e", h, 1), ("pt", h)]])
                self.dve = steps(name + "_dve", ([("z", h) for h in range(heads)] if gates else []) +
                                 ([("l", 0)] if biased else []) + [("mx", 0), ("nm", 0)] +
                                 [x for h in range(heads) for x in [("rs", h), ("nr", h, 0), ("nr", h, 1)] +
                                  ((([("l", h + 1)] if biased else []) + [("mx", h + 1), ("nm", h + 1)]) if h + 1 < heads else [])
                                  + [("o", h)]])

            def L(self, h):
                return BIG[:, 66 + 2 * (h % 2):68 + 2 * (h % 2), :]

            def PT(self, h):
                return BIG[:, 70 + 2 * (h % 2):72 + 2 * (h % 2), :]

        scale_o = float(P) ** -0.5
        mo_att = Attn("moba", 6, MQ, MK, MV, True, MZ, True)
        xa_att = Attn("cross", 4, 40, XAK, XAV, False, 44, False)
        AST = small[:, 46:56]

        def pe_attn(pe, A):
            for h in range(A.heads):
                if h >= 2:
                    A.act.wait(pe, "v", h - 2)
                for kt in range(2):
                    ins = pe.transpose(PB[6 + h % 2][:, kt * P:(kt + 1) * P], tile(A.v + h)[:, kt * P:(kt + 1) * P], ident[:, :])
                A.pe.inc(ins, "v", h)

            def scores(h):
                if h:
                    A.act.wait(pe, "e", h - 1, 1)
                for qt in range(2):
                    ins = pe.matmul(PB[5][:, qt * T:(qt + 1) * T], tile(A.q + h)[:, qt * P:(qt + 1) * P], tile(A.k + h),
                                    start=True, stop=True, skip_group_check=True)
                A.pe.inc(ins, "s", h)
            scores(0)
            A.act.wait(pe, "v", A.heads - 1)
            for h in range(A.heads):
                if h + 1 < A.heads:
                    scores(h + 1)
                A.dve.wait(pe, "nr", h, 1)
                if h:
                    A.act.wait(pe, "pt", h - 1)
                for kt in range(2):
                    for qt in range(2):
                        ins = pe.transpose(PB[6][:, kt * T + qt * P:kt * T + (qt + 1) * P],
                                           A.L(h)[:, qt, kt * P:(kt + 1) * P], ident[:, :])
                A.pe.inc(ins, "t", h)
                A.act.wait(pe, "pt", h)
                if h:
                    A.dve.wait(pe, "o", h - 1)
                for kt in range(2):
                    ins = pe.matmul(PB[7][:, 0:T], tile(A.v + h)[:, kt * P:(kt + 1) * P], A.PT(h)[:, kt, :],
                                    start=kt == 0, stop=kt == 1)
                A.pe.inc(ins, "o", h)

        def act_attn(act, A):
            s = nc.scalar.activation
            if A.gates:
                for h in range(A.heads):
                    A.act.inc(s(tile(16 + h), tile(A.outs + h), ACT.Sigmoid), "z", h)
            for h in range(A.heads):
                A.pe.wait(act, "v", h)
                A.act.inc(s(tile(A.v + h), PB[6 + h % 2][:, 0:T], ACT.Copy), "v", h)
            for h in range(A.heads):
                if h == 1:
                    prime(act, "moba" if A.gates else "cross", act_high)
                m = AST[:, 4 * (h % 2):4 * (h % 2) + 4]
                A.dve.wait(act, "nm", h)
                for qt in range(2):
                    src = A.L(h)[:, qt, :] if A.biased else PB[5][:, qt * T:(qt + 1) * T]
                    A.act.inc(s(A.L(h)[:, qt, :], src, ACT.Exp, bias=m[:, qt:qt + 1], scale=scale_o,
                                accum_out=m[:, 2 + qt:3 + qt]), "e", h, qt)
                A.pe.wait(act, "t", h)
                if h >= 2:
                    A.pe.wait(act, "o", h - 2)
                A.act.inc(s(A.PT(h).rearrange("p a t -> p (a t)"), PB[6][:, :], ACT.Copy), "pt", h)
            off = 10 if A.gates else 0
            for h in range(A.heads):
                A.dve.wait(act, "o", h)
                act_split(act, None, h, tile(A.outs + h), XS[:, off + h, 0, T:2 * T])

        def dve_attn(dve, A):
            v, st = nc.vector, A.dve
            sl = slopes(A.heads)
            if A.gates:
                for h in range(A.heads):
                    A.act.wait(dve, "z", h)
                    st.inc(v.tensor_tensor(tile(A.outs + h), tile(A.outs + h), tile(16 + h), ALU.mult), "z", h)
            if A.biased:
                dve.wait_ge(dist_in, 16)

            def maxima(h):
                m = AST[:, 4 * (h % 2):4 * (h % 2) + 4]
                A.pe.wait(dve, "s", h)
                if h >= 2:
                    A.pe.wait(dve, "t", h - 2)
                src = PB[5][:, :].rearrange("p (q t) -> p q t", q=2)
                if A.biased:
                    st.inc(v.scalar_tensor_tensor(A.L(h), DIST, sl[h] / scale_o, src, ALU.mult, ALU.add), "l", h)
                    src = A.L(h)
                st.inc(v.tensor_reduce(m[:, 0:2], src, AX.X, ALU.max), "mx", h)
                st.inc(v.tensor_scalar(m[:, 0:2], m[:, 0:2], -scale_o, None, ALU.mult), "nm", h)

            maxima(0)
            for h in range(A.heads):
                if h == 1:
                    prime(dve, "moba" if A.gates else "cross", dve_low)
                m = AST[:, 4 * (h % 2):4 * (h % 2) + 4]
                A.act.wait(dve, "e", h, 1)
                st.inc(v.reciprocal(m[:, 2:4], m[:, 2:4]), "rs", h)
                for qt in range(2):
                    st.inc(v.tensor_scalar(A.L(h)[:, qt, :], A.L(h)[:, qt, :], m[:, 2 + qt:3 + qt], None, ALU.mult), "nr", h, qt)
                if h + 1 < A.heads:
                    maxima(h + 1)
                A.pe.wait(dve, "o", h)
                if A.gates:
                    st.inc(v.tensor_tensor(tile(A.outs + h), PB[7][:, 0:T], tile(A.outs + h), ALU.mult), "o", h)
                else:
                    st.inc(v.tensor_copy(tile(A.outs + h), PB[7][:, 0:T]), "o", h)
            off = 10 if A.gates else 0
            for h in range(A.heads):
                dve_split(dve, "mo" if A.gates else "xo", h, tile(A.outs + h), XS[:, off + h, 1, T:2 * T],
                          XS[:, off + h, 0, T:2 * T])

        ADV = AD[:, :].rearrange("p (f v) -> p f v", v=2)
        md = sem("modulation_step")
        mdc = [0]

        def dve_mods(dve, l):
            v = nc.vector
            for w in range(2):
                v.tensor_tensor(MODS[:, 2 + w, :], ADV[:, 48 * l:48 * l + 16, w], V[f"ada_b{l}"][:, 0:16], ALU.add).then_inc(md, 1)
                v.tensor_tensor(MODS[:, w, :], ADV[:, 48 * l + 16:48 * l + 32, w], V[f"ada_b{l}"][:, 16:32], ALU.add).then_inc(md, 1)
                mdc[0] += 2
                dve.wait_ge(md, mdc[0])
                v.scalar_tensor_tensor(MODS[:, w, :], MODS[:, w, :], 1.0, V[f"pre{l}"], ALU.add, ALU.mult).then_inc(md, 1)
                mdc[0] += 1

        def dve_gates(dve, l):
            v = nc.vector
            for w in range(2):
                v.tensor_tensor(MODS[:, 4 + w, :], ADV[:, 48 * l + 32:48 * l + 48, w], V[f"ada_b{l}"][:, 32:48], ALU.add).then_inc(md, 1)
                mdc[0] += 1
                dve.wait_ge(md, mdc[0])
                v.tensor_tensor(MODS[:, 4 + w, :], MODS[:, 4 + w, :], V[f"post{l}"], ALU.mult).then_inc(md, 1)
                mdc[0] += 1

        flat = BIG[:, :, :].rearrange("p a t -> p (a t)")
        PADW = T + 16
        UPAD = flat[:, 64 * T:64 * T + 4 * 2 * PADW].rearrange("p (n s t) -> p n s t", n=4, s=2)
        p0 = 64 * T + 8 * PADW
        INV = flat[:, p0:p0 + T]
        TA = [flat[:, p0 + T + m * 2 * PADW:p0 + T + (m + 1) * 2 * PADW].rearrange("p (s t) -> p s t", s=2) for m in range(2)]
        GT = BIG[:, 64:72, :].rearrange("p (n a) t -> p n (a t)", a=2)
        inv_in, pooled, pool_link, pads = sem("inverse_counts_in"), sem("pooled"), sem("pool_link"), sem("pads_clear")
        plc = [0]

        def gp_pool(gp, g):
            w = 2 ** (g + 1)
            left = w // 2
            turn = POOLS.index(g)
            if turn == 0:
                gp.wait_ge(ends["dve"], POOL_STAGE)
                gp.wait_ge(ends["act"], POOL_STAGE)
                gp.wait_ge(ends["pe"], POOL_STAGE)
                nc.gpsimd.memset(UPAD[:, :, :, 0:8], 0.0).then_inc(pads, 1)
                nc.gpsimd.memset(UPAD[:, :, :, 8 + T:PADW], 0.0).then_inc(pads, 1)
                gp.wait_ge(pads, 2)
            else:
                gp.wait_ge(pooled, 4 * turn)
            gp.dma_start(INV, a["inv_counts"][g:g + 1, :].to_broadcast([P, T])).then_inc(inv_in, 16)
            gp.wait_ge(inv_in, 16 * (turn + 1))

            def link(ins):
                plc[0] += 1
                ins.then_inc(pool_link, 1)
                gp.wait_ge(pool_link, plc[0])
            for n in range(4):
                gp.wait_ge(act_freed, pu[g].free0 + n + 1)
                src, width, span = UPAD[:, n], PADW, 1
                m = 0
                while span < w:
                    width -= span
                    link(nc.gpsimd.tensor_tensor(TA[m][:, :, 0:width], src[:, :, 0:width], src[:, :, span:span + width], ALU.add))
                    src, m, span = TA[m], 1 - m, 2 * span
                link(nc.gpsimd.tensor_tensor(TA[m][:, :, 0:T], src[:, :, 8 - left:8 - left + T],
                                             INV.unsqueeze(1).to_broadcast([P, 2, T]), ALU.mult))
                u = UPAD[:, n, :, 8:8 + T]
                nc.gpsimd.tensor_tensor(u, TA[m][:, :, 0:T], u, ALU.subtract).then_inc(pooled, 1)
                gp.wait_ge(pooled, 4 * turn + n + 1)

        gate_steps = pgate.steps0

        def pooled_split(eng, me, g, former):
            if former is not None:
                eng.wait_ge(chunk_done, pg[former].chunk0 + 1)
            for n in range(4):
                u = UPAD[:, n, :, 8:8 + T]
                s2 = lambda part: PS[:, n, part, :].rearrange("p (s t) -> p s t", s=2)
                eng.wait_ge(pooled, 4 * POOLS.index(g) + n + 1)
                if me == "act":
                    act_split(eng, f"pp{g}", n, u, s2(0))
                else:
                    dve_split(eng, f"pp{g}", n, u, s2(1), s2(0))
            if me == "act":
                eng.wait_ge(split_lo, splits[f"pp{g}"] + 4)

        def gated_split(eng, me, j):
            if j == 0:
                eng.wait_ge(chunk_done, pgate.chunk0 + 16)
            for k in range(4 * j, 4 * j + 4):
                y = BIG[:, YT0 + 2 * k:YT0 + 2 * k + 2, :].rearrange("p a t -> p (a t)")
                if me == "act":
                    eng.wait_ge(resid, gate_steps + k + 1)
                    act_split(eng, "py", k, y, XS[:, k, 0, :])
                else:
                    dve_split(eng, "py", k, y, XS[:, k, 1, :], XS[:, k, 0, :])

        def run_pool_chain(eng, me, product):
            for n, p in enumerate(pool_chain):
                extra = None
                if p in pg:
                    g = pg.index(p)
                    turn = POOLS.index(g)
                    extra = lambda e, j, g=g, turn=turn: pooled_split(e, me, g, POOLS[turn - 1] if turn else None)
                if p is po:
                    extra = lambda e, j: gated_split(e, me, j)
                product(eng, p, former=pool_chain[n - 1] if n else None, last=p is po, extra=extra)

        def pe_pool_chain(pe):
            for p in pool_chain:
                ready = None
                if p in pg:
                    ready = lambda e, j, g=pg.index(p): e.wait_ge(split_lo, splits[f"pp{g}"] + 4)
                if p is po:
                    ready = lambda e, j: e.wait_ge(split_lo, splits["py"] + 4 * j + 4)
                pe_product(pe, p, ready)

        COS, SIN = tile(60), tile(61)
        ROT = BIG[:, 64, 0:P]
        RTMP = tile(62)
        KRT = BIG[:, 76:78, :].rearrange("p a t -> p (a t)")
        rope_in = sem("rope_in")
        OT = BIG[:, 65:67, :]
        VA = [BIG[:, 48 + 2 * h:50 + 2 * h, :].rearrange("p a (b d) -> p (a b) d", b=2) for h in range(2)]
        PP = [BIG[:, 52 + 2 * h:54 + 2 * h, :].rearrange("p a t -> p (a t)") for h in range(2)]
        PPT = [BIG[:, 56 + 2 * h:58 + 2 * h, :].rearrange("p a t -> p (a t)") for h in range(2)]
        mla_scale = float(192) ** -0.5
        def order(first, early, late):
            names = list(first)
            for j in range(1, 10):
                names += [(n[0], j - 2) + n[1:] for n in early if j >= 2]
                names += [(n[0], j - 1) + n[1:] for n in late if j <= 8]
            return names
        la_pe = steps("latent_pe", order([("kr",)], [("o", 3)], [("rot",), ("v", 0), ("v", 1), ("s", 0), ("s", 1), ("t", 0),
                      ("o", 0), ("s", 2), ("t", 1), ("o", 1), ("s", 3), ("t", 2), ("o", 2), ("t", 3)]))
        la_act = steps("latent_act", order([("g", k) for k in range(4)], [("hi",)], [("v", 0), ("v", 1), ("e", 0), ("e", 1),
                       ("pt", 0), ("e", 2), ("pt", 1), ("e", 3), ("pt", 2), ("pt", 3)]))
        la_dve = steps("latent_dve", order([("kr1",), ("kr2",), ("kr3",)] + [("g", k) for k in range(4)], [("o", 3), ("lo",)],
                       [("r1",), ("r2",), ("r3",), ("mx", 0), ("nm", 0), ("rs", 0), ("nr", 0), ("mx", 1), ("nm", 1), ("rs", 1),
                        ("nr", 1), ("o", 0), ("mx", 2), ("nm", 2), ("rs", 2), ("nr", 2), ("o", 1), ("mx", 3), ("nm", 3),
                        ("rs", 3), ("nr", 3), ("o", 2)]))

        def dve_rope(dve, x, names, key):
            v, st = nc.vector, la_dve
            st.inc(v.tensor_tensor(RTMP, PB[5][:, 0:T], SIN, ALU.mult), names[0], *key)
            st.inc(v.tensor_tensor(x, x, COS, ALU.mult), names[1], *key)
            st.wait(dve, names[1], *key)
            st.inc(v.tensor_tensor(x, x, RTMP, ALU.add), names[2], *key)

        def act_latent0(act):
            for k in range(4):
                la_act.inc(nc.scalar.activation(BIG[:, 32 + 4 * k:36 + 4 * k, :], BIG[:, 16 + 4 * k:20 + 4 * k, :], ACT.Sigmoid), "g", k)

        def pe_latent0(pe):
            pe.wait_ge(rope_in, 48)
            la_pe.inc(pe.matmul(PB[5][:, 0:T], ROT, KRT[:, 0:T], start=True, stop=True), "kr")

        def dve_latent0(dve):
            dve.wait_ge(rope_in, 48)
            la_pe.wait(dve, "kr")
            dve_rope(dve, KRT[:, 0:T], ("kr1", "kr2", "kr3"), ())
            for k in range(4):
                la_act.wait(dve, "g", k)
                la_dve.inc(nc.vector.tensor_tensor(BIG[:, 16 + 4 * k:20 + 4 * k, :], BIG[:, 16 + 4 * k:20 + 4 * k, :],
                                                   BIG[:, 32 + 4 * k:36 + 4 * k, :], ALU.mult), "g", k)

        q_of = lambda j: Q_SETS[j % 2]
        wide = lambda t: BIG[:, t:t + 2, :].rearrange("p a t -> p (a t)")
        k_of = lambda j, h: wide(KV_SETS[j % 2][2 * h])
        v_of = lambda j, h: wide(KV_SETS[j % 2][2 * h + 1])
        before = lambda j, u, n: divmod(4 * j + u - n, 4)

        def pe_pairs(pe):
            def scores(a, u):
                h, qt = u // 2, u % 2
                bank, r = PB[5 + u % 2], slice(64 * h, 64 * h + 64)
                if u >= 2:
                    la_act.wait(pe, "e", a, u - 2)
                elif u == 0:
                    la_dve.wait(pe, "r3", a)
                else:
                    la_act.wait(pe, "v", a, 0)
                pe.matmul(bank[:, :], tile(q_of(a)[h])[:, qt * P:(qt + 1) * P], k_of(a, h), start=True, stop=False)
                la_pe.inc(pe.matmul(bank[:, :], BIG[r, q_of(a)[2], qt * P:(qt + 1) * P], KRT[r, :], start=False, stop=True),
                          "s", a, u)

            def probs(a, u):
                la_dve.wait(pe, "nr", a, u)
                if u:
                    la_act.wait(pe, "pt", a, u - 1)
                else:
                    la_act.wait(pe, "v", a, 1)
                for kt in range(4):
                    ins = pe.transpose(PB[7][:, kt * P:(kt + 1) * P], PP[u % 2][:, kt * P:(kt + 1) * P], ident[:, :])
                la_pe.inc(ins, "t", a, u)

            def output(a, u):
                la_act.wait(pe, "pt", a, u)
                b, w = before(a, u, 1)
                if b >= 0:
                    la_dve.wait(pe, "o", b, w)
                for kt in range(4):
                    ins = pe.matmul(PB[4][:, 0:P], VA[u // 2][:, kt, :], PPT[u % 2][:, kt * P:(kt + 1) * P],
                                    start=kt == 0, stop=kt == 3)
                la_pe.inc(ins, "o", a, u)

            for j in range(10):
                products_on, a = j < 8, j - 1
                att = 0 <= a < 8

                def product(p, n):
                    if products_on:
                        if p is ukv and n == 3 and j:
                            pe.wait_ge(ada_moved, 40 + j)
                        pe_chunk(pe, p[j], 0, 0, only=n)
                product(uq, 0)
                if j >= 2:
                    output(j - 2, 3)
                if att:
                    pe.wait_ge(dve_freed, uq[a].free0 + 3)
                    pe.wait_ge(act_freed, ukv[a].free0 + 4)
                    if a:
                        la_act.wait(pe, "e", a - 1, 2)
                    la_pe.inc(pe.matmul(PB[5][:, 0:T], ROT, tile(q_of(a)[2]), start=True, stop=True), "rot", a)
                    for h in range(2):
                        if a:
                            la_act.wait(pe, *(("e", a - 1, 3), ("pt", a - 1, 3))[h])
                        for kt in range(4):
                            ins = pe.transpose(PB[6 + h][:, kt * P:(kt + 1) * P], v_of(a, h)[:, kt * P:(kt + 1) * P], ident[:, :])
                        la_pe.inc(ins, "v", a, h)
                    pe_ada(pe, 40 + a, bank=3)
                product(uq, 1)
                if att:
                    scores(a, 0)
                product(uq, 2)
                if att:
                    scores(a, 1)
                product(ukv, 0)
                if att:
                    probs(a, 0)
                product(ukv, 1)
                if att:
                    output(a, 0)
                    scores(a, 2)
                    probs(a, 1)
                product(ukv, 2)
                if att:
                    output(a, 1)
                    scores(a, 3)
                    probs(a, 2)
                product(ukv, 3)
                if att:
                    output(a, 2)
                    probs(a, 3)

        def act_pairs(act):
            s = nc.scalar.activation

            def exponentials(a, u):
                m = AST[:, 2 * (u % 2):2 * (u % 2) + 2]
                la_dve.wait(act, "nm", a, u)
                b, w = before(a, u, 2)
                if b >= 0:
                    la_pe.wait(act, "t", b, w)
                la_act.inc(s(PP[u % 2], PB[5 + u % 2][:, :], ACT.Exp, bias=m[:, 0:1], scale=mla_scale, accum_out=m[:, 1:2]),
                           "e", a, u)

            def transposed(a, u):
                la_pe.wait(act, "t", a, u)
                b, w = before(a, u, 2)
                if b >= 0:
                    la_pe.wait(act, "o", b, w)
                la_act.inc(s(PPT[u % 2], PB[7][:, :], ACT.Copy), "pt", a, u)

            act_high(act, ukv[0], 0, 0)
            for j in range(10):
                a = j - 1
                att = 0 <= a < 8
                if j >= 2:
                    la_dve.wait(act, "o", j - 2, 3)
                    la_act.inc(s(XS[:, 2 * j - 4:2 * j - 2, 0, 0:T], OT, ACT.Copy), "hi", j - 2)
                if att:
                    for h in range(2):
                        la_pe.wait(act, "v", a, h)
                        if a:
                            la_pe.wait(act, "o", a - 1, 2 * h + 1)
                        la_act.inc(s(VA[h].rearrange("p k d -> p (k d)"), PB[6 + h][:, :], ACT.Copy), "v", a, h)
                    act_ada(act, 40 + a, bank=3)
                if j < 8:
                    act_evac(act, uq[j], 0, 0)
                    act_evac(act, uq[j], 0, 1)
                if att:
                    exponentials(a, 0)
                if j < 8:
                    act_evac(act, uq[j], 0, 2)
                    if j < 7:
                        act_high(act, uq[j + 1], 0, 0)
                if att:
                    exponentials(a, 1)
                    transposed(a, 0)
                if j < 8:
                    act_evac(act, ukv[j], 0, 0)
                    act_evac(act, ukv[j], 0, 1)
                if att:
                    exponentials(a, 2)
                    transposed(a, 1)
                if j < 8:
                    act_evac(act, ukv[j], 0, 2)
                if att:
                    exponentials(a, 3)
                    transposed(a, 2)
                if j < 8:
                    act_evac(act, ukv[j], 0, 3)
                if att:
                    transposed(a, 3)
                if j < 7:
                    act_high(act, ukv[j + 1], 0, 0)

        def dve_pairs(dve):
            v, st = nc.vector, la_dve

            def maxima(a, u):
                m = AST[:, 2 * (u % 2):2 * (u % 2) + 2]
                la_pe.wait(dve, "s", a, u)
                st.inc(v.tensor_reduce(m[:, 0:1], PB[5 + u % 2][:, :], AX.X, ALU.max), "mx", a, u)
                st.inc(v.tensor_scalar(m[:, 0:1], m[:, 0:1], -mla_scale, None, ALU.mult), "nm", a, u)

            def probs(a, u):
                m = AST[:, 2 * (u % 2):2 * (u % 2) + 2]
                la_act.wait(dve, "e", a, u)
                st.inc(v.reciprocal(m[:, 1:2], m[:, 1:2]), "rs", a, u)
                st.inc(v.tensor_scalar(PP[u % 2], PP[u % 2], m[:, 1:2], None, ALU.mult), "nr", a, u)

            def output(a, u):
                h, qt = u // 2, u % 2
                la_pe.wait(dve, "o", a, u)
                st.inc(v.tensor_tensor(OT[:, h, qt * P:(qt + 1) * P], PB[4][:, 0:P],
                                       BIG[:, 16 + 2 * a + h, qt * P:(qt + 1) * P], ALU.mult), "o", a, u)

            dve_low(dve, ukv[0], 0, 0)
            for j in range(10):
                a = j - 1
                att, on = 0 <= a < 8, j < 8
                if j >= 2:
                    output(j - 2, 3)
                    la_act.wait(dve, "hi", j - 2)
                    st.inc(v.tensor_sub(XS[:, 2 * j - 4:2 * j - 2, 1, 0:T], OT, XS[:, 2 * j - 4:2 * j - 2, 0, 0:T].bitcast(F32)),
                           "lo", j - 2)
                if att:
                    la_pe.wait(dve, "rot", a)
                    dve_rope(dve, tile(q_of(a)[2]), ("r1", "r2", "r3"), (a,))
                if on:
                    dve_evac(dve, uq[j], 0, 0)
                    dve_evac(dve, uq[j], 0, 1)
                if att:
                    maxima(a, 0)
                if 0 < j < 8:
                    dve_low(dve, ukv[j], 0, 0)
                if on:
                    dve_evac(dve, uq[j], 0, 2)
                if att:
                    probs(a, 0)
                if j < 7:
                    dve_low(dve, uq[j + 1], 0, 0)
                if att:
                    maxima(a, 1)
                if on:
                    dve_ada(dve, uq[j], 0, 0, only=0)
                if att:
                    probs(a, 1)
                    output(a, 0)
                    maxima(a, 2)
                if on:
                    dve_ada(dve, uq[j], 0, 0, only=1)
                if att:
                    probs(a, 2)
                    output(a, 1)
                    maxima(a, 3)
                if on:
                    dve_ada(dve, ukv[j], 0, 0, only=0)
                if att:
                    probs(a, 3)
                    output(a, 2)
                if on:
                    dve_ada(dve, ukv[j], 0, 0, only=1)

        def sp_pairs(sp):
            sp_chunk(sp, uq[0], 0, 0)
            sp_chunk(sp, ukv[0], 0, 0)
            for j in range(8):
                if j < 7:
                    sp_chunk(sp, uq[j + 1], 0, 0)
                sp_unit(sp, uq[j], 0, 0, 0)
                if j < 7:
                    sp_chunk(sp, ukv[j + 1], 0, 0)
                sp_unit(sp, uq[j], 0, 0, 1)
                sp_unit(sp, ukv[j], 0, 0, 0)
                sp_unit(sp, ukv[j], 0, 0, 1)

        out_t, out_c = sem("out_turned"), sem("out_copied")
        OUTT = BIG[:, 16:32, :].rearrange("p (a k) t -> p a (k t)", a=2)

        def pe_out(pe):
            last = norms["post1"]
            pe_norm(pe, last)
            pe.wait_ge(std_ready, last["index"] + 1)
            for n in range(8):
                k4, h = n // 2, n % 2
                if h == 0:
                    pe.wait_ge(norm_done, last["nd0"] + 4 * k4 + 4)
                if n >= 2:
                    pe.wait_ge(out_c, n - 1)
                for m in range(4):
                    ins = pe.transpose(PB[5 + n % 2][:, m * P:(m + 1) * P], BIG[:, 4 * k4 + m, h * P:(h + 1) * P], ident[:, :])
                ins.then_inc(out_t, 1)

        def act_out(act):
            act_norm(act, norms["post1"])
            for n in range(8):
                k4, h = n // 2, n % 2
                act.wait_ge(out_t, n + 1)
                nc.scalar.activation(OUTT[:, h, 512 * k4:512 * (k4 + 1)], PB[5 + n % 2][:, :], ACT.Copy).then_inc(out_c, 1)

        def sp_out(sp):
            for n in range(8):
                k4, h = n // 2, n % 2
                sp.wait_ge(out_c, n + 1)
                sp.dma_start(out[0, h * P:(h + 1) * P, 512 * k4:512 * (k4 + 1)],
                             OUTT[:, h, 512 * k4:512 * (k4 + 1)]).then_inc(out_done, 16)
            sp.wait_ge(out_done, 16 * 8)

        STAGES = ["in_mem", "kv", "in_x", "win_ab", "lru", "mgates", "mproj", "mheads", "mfinish", "win_c", "moba", "mixo",
                  "norm_xa", "xq", "cross", "xo", "final", "pre0", "pools",
                  "post0", "pre1", "latents", "latnorm",
                  "latent0", "pairs"] + [] + ["mo", "out"]
        CHAINS = {"win_ab": [win_a, win_b], "latents": [ckv, kr, cq, mg]}
        stage_of = {p.name: name for name, chain in CHAINS.items() for p in chain}
        POOL_STAGE = STAGES.index("pre0") + 1
        by_name = {p.name: p for p in products}

        def run(eng, me, stage_fn, product_fn, split=None, loads=None):
            for name in STAGES:
                if DEBUG_STOP == name:
                    name = "dump"
                if loads:
                    loads(name)
                if split and name not in ("pairs", "in_mem", "in_x", "pre0", "moba", "cross"):
                    prime(eng, name, split)
                if name in CHAINS:
                    chain = CHAINS[name]
                    for n, p in enumerate(chain):
                        if me == "pe":
                            product_fn(eng, p)
                        else:
                            product_fn(eng, p, former=chain[n - 1] if n else None, last=p is chain[-1])
                elif name in by_name:
                    product_fn(eng, by_name[name])
                elif name in stage_fn:
                    stage_fn[name](eng)
                if name == "dump":
                    return
                if split and name == "pairs":
                    prime(eng, name, split)
                if name != "out":
                    stage_end(eng, me)

        @block.sync
        def _(sp):
            sp_turn(sp, 0, a["mem"][0])
            sp_product(sp, kv)
            for p in products[1:3]:
                sp_product(sp, p)
            if DEBUG_STOP:
                lim = STAGES.index(DEBUG_STOP)
            else:
                lim = len(STAGES)
            for p in products[3:]:
                if p in uq[1:] + ukv:
                    continue
                stage = "pools" if p in pool_chain else "pairs" if p is uq[0] else stage_of.get(p.name, p.name)
                if STAGES.index(stage) >= lim:
                    break
                if p is uq[0]:
                    sp_pairs(sp)
                    continue
                sp_product(sp, p)
            if not DEBUG_STOP:
                sp_out(sp)

        @block.gpsimd
        def _(gp):
            if not DEBUG_STOP or STAGES.index(DEBUG_STOP) > STAGES.index("pools"):
                for g in POOLS:
                    gp_pool(gp, g)

        @block.scalar
        def _(act):
            for name, st in all_steps:
                if name.endswith("_act"):
                    st.chain = act
            def in_mem(act):
                act_setup(act)
                setup.wait(act, "epsln")
                prime(act, "in_mem", act_high)
                act_turn(act, 0)
                act_norm(act, norms["mem"])

            def in_x(act):
                act_turn(act, 1)
                prime(act, "in_x", act_high)
                act_norm(act, norms["mix"])

            def final(act):
                act_norm(act, norms["final"])
                act_turn(act, 2)

            def pre0(act):
                prime(act, "pre0", act_high)
                act_norm(act, norms["pre0"], norms["pre0c"])

            def lru(act):
                act_lru(act)
                for b in range(4):
                    lru_dve.wait(act, "y", b)
                    act_split(act, "lru", b, tile(LX + b), XS[:, b, 0, T:2 * T])
            def loads(name):
                if name == "kv":
                    sp_turn(act, 1, a["x"][0])
                if name == "win_ab":
                    act.dma_start(LW[:, 0:4], a["lru_wa"][0].rearrange("g i o -> i g o")).then_inc(lw_in, 16)
                    act.dma_start(LW[:, 4:8], a["lru_wx"][0].rearrange("g i o -> i g o")).then_inc(lw_in, 16)
                if name == "win_c":
                    act.dma_start(DIST, a["dist"].rearrange("(q p) k -> p q k", p=P)).then_inc(dist_in, 16)
                if name == "xo":
                    sp_turn(act, 2, a["ctx_2"][0])
                if name == "latent0":
                    act.dma_start(COS, a["cos"]).then_inc(rope_in, 16)
                    act.dma_start(SIN, a["sin"]).then_inc(rope_in, 16)
                    act.dma_start(ROT, a["rot"]).then_inc(rope_in, 16)
            both = lambda *names: (lambda act: act_norm(act, *[norms[n] for n in names]))
            stages_ = dict(in_mem=in_mem, in_x=in_x, lru=lru, mgates=act_mgates, mproj=act_mproj, mheads=act_mheads,
                           mfinish=act_mfinish, moba=lambda e: act_attn(e, mo_att), norm_xa=both("xa"),
                           cross=lambda e: act_attn(e, xa_att), final=final, pre0=pre0, pools=lambda e: run_pool_chain(e, "act", act_product),
                           post0=both("post0", "post0c"), pre1=both("pre1", "pre1c"), latnorm=both("ckv", "ckvc", "cq"),
                           latent0=act_latent0, pairs=act_pairs, out=act_out)
            run(act, "act", stages_, act_product, act_high, loads)

        @block.vector
        def _(dve):
            for name, st in all_steps:
                if name.endswith("_dve"):
                    st.chain = dve
            def in_mem(dve):
                dve_setup(dve)
                prime(dve, "in_mem", dve_low)
                dve_norm(dve, norms["mem"])

            def in_x(dve):
                prime(dve, "in_x", dve_low)
                dve_norm(dve, norms["mix"])

            def pre0(dve):
                dve_mods(dve, 0)
                prime(dve, "pre0", dve_low)
                dve_norm(dve, norms["pre0"])
                dve_norm(dve, norms["pre0c"])

            def post0(dve):
                dve_gates(dve, 0)
                dve_norm(dve, norms["post0"])
                dve_norm(dve, norms["post0c"])

            def pre1(dve):
                dve_mods(dve, 1)
                dve_norm(dve, norms["pre1"])
                dve_norm(dve, norms["pre1c"])

            def post1(dve):
                dve_gates(dve, 1)
                dve_norm(dve, norms["post1"])

            def lru(dve):
                dve_lru(dve)
                for b in range(4):
                    dve_split(dve, "lru", b, tile(LX + b), XS[:, b, 1, T:2 * T], XS[:, b, 0, T:2 * T])
            both = lambda *names: (lambda dve: [dve_norm(dve, norms[n]) for n in names])
            stages_ = dict(in_mem=in_mem, in_x=in_x, lru=lru, mgates=dve_mgates, mproj=dve_mproj, mheads=dve_mheads,
                           mfinish=dve_mfinish, moba=lambda e: dve_attn(e, mo_att), norm_xa=both("xa"),
                           cross=lambda e: dve_attn(e, xa_att), final=both("final"), pre0=pre0, pools=lambda e: run_pool_chain(e, "dve", dve_product),
                           post0=post0, pre1=pre1, latnorm=lambda e: [dve_norm(e, norms[n]) for n in ("ckv", "ckvc", "cq")], latent0=dve_latent0, pairs=dve_pairs, out=post1)
            run(dve, "dve", stages_, dve_product, dve_low)

        @block.tensor
        def _(pe):
            def turn_norm(q, *names):
                def go(pe):
                    if q is not None:
                        pe_turn(pe, q)
                    for n in names:
                        pe_norm(pe, norms[n])
                return go

            def in_mem(pe):
                setup.wait(pe, "ones")
                pe_setup(pe)
                pe.wait_ge(pv_ready, 1)
                turn_norm(0, "mem")(pe)

            def final(pe):
                pe_norm(pe, norms["final"])
                pe.wait_ge(std_ready, norms["final"]["index"] + 1)
                pe_turn(pe, 2)

            def lru(pe):
                pe.wait_ge(lw_in, 32)
                pe_lru(pe)
            stages_ = dict(in_mem=in_mem, in_x=turn_norm(1, "mix"), lru=lru, mgates=pe_mgates, mproj=pe_mproj, mheads=pe_mheads,
                           mfinish=pe_mfinish, moba=lambda e: pe_attn(e, mo_att), norm_xa=turn_norm(None, "xa"),
                           cross=lambda e: pe_attn(e, xa_att), final=final, pre0=turn_norm(None, "pre0", "pre0c"),
                           pools=pe_pool_chain, post0=turn_norm(None, "post0", "post0c"), pre1=turn_norm(None, "pre1", "pre1c"),
                           latnorm=turn_norm(None, "ckv", "ckvc", "cq"), latent0=pe_latent0, pairs=pe_pairs, 
                           out=pe_out)
            run(pe, "pe", stages_, pe_product)


def constants():
    p = np.arange(P)
    t = np.arange(T)
    dist = t[None, :] - t[:, None]
    freqs = 10000.0 ** (-np.arange(16, dtype=np.float32) / np.float32(16))
    pos = np.stack([t // 64, t % 64]).astype(np.float32)
    axis, part, f = (p % 64) // 32, (p % 32) // 16, p % 16
    ang = pos[axis, :] * freqs[f].astype(np.float32)[:, None]
    rot = np.zeros((P, P), np.float32)
    partner = np.where(part == 0, p + 16, p - 16)
    rot[partner, p] = np.where(part == 0, -1.0, 1.0)
    counts = []
    for w in (2, 4, 8, 16):
        left = w // 2
        counts.append(np.minimum(t + w - left, T) - np.maximum(t - left, 0))
    return {
        "ident": np.eye(P, dtype=np.float32),
        "blockmask": (p[:, None] // 4 == p[None, :] // 4).astype(np.float32),
        "mlmask": np.where(p[:, None] <= p[None, :], 0.0, NEG).astype(np.float32),
        "sel": np.kron(np.eye(4, dtype=np.float32), np.ones((1, P), np.float32)),
        "dist": np.where(dist <= 0, dist, -1e33).astype(np.float32),
        "cos": np.cos(ang).astype(np.float32), "sin": np.sin(ang).astype(np.float32), "rot": rot,
        "inv_counts": (1.0 / np.stack(counts)).astype(np.float32),
    }


def kernel(**inputs):
    import concourse.bacc as bacc
    from concourse.bass_utils import run_bass_kernel_spmd

    nc = bacc.Bacc("TRN2", target_bir_lowering=False, num_devices=1, dynamic_dma_scratch_size=1024)
    arrays, args = {}, {}
    for name, value in list(inputs.items()) + list(constants().items()):
        x = np.ascontiguousarray(value)
        arrays["in_" + name] = x
        args[name] = nc.dram_tensor("in_" + name, x.shape, F32, kind="ExternalInput").ap()
    out = nc.dram_tensor("out_0", (1, T, D), F32, kind="ExternalOutput").ap()
    build(nc, args, out)
    result = run_bass_kernel_spmd(nc, [arrays], core_ids=[0])
    return result.results[0]["out_0"]
```
